# Optimizing a Trainium2 kernel written in Bass

```python
import jax
import jax.numpy as jnp
from jax import lax
import numpy as np
import jax, jax.numpy as jnp

D_MODEL = 1024
BATCH = 1
SEQ = 512
DEPTH = 1

GRID_W = 64
CTX_LEN = 256
EPS = 1e-6
N_MOD = 6

HG_HEADS = 8
HG_DK = 128
HG_DV = 128
HG_WIDTH = HG_HEADS * HG_DK
HG_CHUNK = 32

CONV_WIDTH = D_MODEL
CONV_K = 3

N_HEADS = 16
N_KV_HEADS = 4
HEAD_DIM = 64
GQA_GROUP = N_HEADS // N_KV_HEADS
ATTN_WIDTH = N_HEADS * HEAD_DIM
KV_WIDTH = N_KV_HEADS * HEAD_DIM
Q_BLOCK = 128
ROPE_THETA = 10000.0
ATTN_SCALE = HEAD_DIM ** -0.5

N_BRANCHES = 3
IN_SPLITS = (HG_WIDTH,) * 5 + (CONV_WIDTH,) * 3 + (ATTN_WIDTH, KV_WIDTH, KV_WIDTH) + (D_MODEL,) * N_BRANCHES
IN_WIDTH = 5 * HG_WIDTH + 3 * CONV_WIDTH + ATTN_WIDTH + 2 * KV_WIDTH + N_BRANCHES * D_MODEL

N_EXPERTS = 16
EXPERT_FF = 1024
CAPACITY_FACTOR = 2


def rmsnorm(x, g):
    xf = x.astype(jnp.float32)
    y = xf * lax.rsqrt(jnp.mean(xf * xf, axis=-1, keepdims=True) + EPS)
    return (y * g).astype(x.dtype)

def modulation(cvec, w, b):
    mod = jax.nn.silu(cvec) @ w + b
    return jnp.split(mod[:, None, :], N_MOD, axis=-1)

def modulate(h, g, shift, scale):
    return rmsnorm(h, g) * (1 + scale) + shift

def project(h, w_in):
    p = h @ w_in
    return jnp.split(p, np.cumsum(IN_SPLITS)[:-1].tolist(), axis=-1)

def to_heads(t, d):
    return t.reshape(t.shape[0], t.shape[1], -1, d)

def axial_rope_tables(n):
    rows = n // GRID_W
    row = jnp.repeat(jnp.arange(rows), GRID_W).astype(jnp.float32)
    col = jnp.tile(jnp.arange(GRID_W), rows).astype(jnp.float32)
    inv = ROPE_THETA ** (-jnp.arange(0, HEAD_DIM // 2, 2, dtype=jnp.float32) / (HEAD_DIM // 2))
    ang = jnp.concatenate([row[:, None] * inv, col[:, None] * inv], axis=-1)
    return jnp.cos(ang), jnp.sin(ang)

def apply_rope(x, cos, sin):
    x1, x2 = x[..., 0::2], x[..., 1::2]
    c, s = cos[None, :, None, :], sin[None, :, None, :]
    return jnp.stack([x1 * c - x2 * s, x1 * s + x2 * c], axis=-1).reshape(x.shape).astype(x.dtype)

def hgrn_chunk_scan(q, log_f, k, v, s0):
    bsz, n, h, _ = q.shape
    dv = v.shape[-1]
    nc = n // HG_CHUNK

    def chunks(t):
        return t.astype(jnp.float32).reshape(bsz, nc, HG_CHUNK, h, t.shape[-1]).transpose(1, 0, 3, 2, 4)

    lower = jnp.tril(jnp.ones((HG_CHUNK, HG_CHUNK), dtype=bool))[:, :, None]

    def step(s, blk):
        qc, lfc, kc, vc = blk
        b = jnp.cumsum(lfc, axis=2)
        decay = jnp.exp(jnp.where(lower, b[:, :, :, None, :] - b[:, :, None, :, :], -jnp.inf))
        a = jnp.einsum('bhtd,bhsd,bhtsd->bhts', qc, kc, decay)
        o = jnp.einsum('bhts,bhse->bhte', a, vc) + jnp.einsum('bhtd,bhde->bhte', qc * jnp.exp(b), s)
        b_last = b[:, :, -1:, :]
        s_new = jnp.exp(b_last)[:, :, 0, :, None] * s + jnp.einsum('bhsd,bhse->bhde', kc * jnp.exp(b_last - b), vc)
        return s_new, o

    s_fin, o = lax.scan(step, s0, (chunks(q), chunks(log_f), chunks(k), chunks(v)))
    return o.transpose(1, 0, 3, 2, 4).reshape(bsz, n, h, dv), s_fin

def hgrn_direction(q, z, v, lb, s0, reverse):
    z = z.astype(jnp.float32)
    lb = lb.reshape(HG_HEADS, HG_DK)
    log_f = jnp.logaddexp(jnp.log(lb), jnp.log1p(-lb) + jax.nn.log_sigmoid(z))
    k = (1.0 - lb) * jax.nn.sigmoid(-z)
    if reverse:
        q, log_f, k, v = (jnp.flip(t, axis=1) for t in (q, log_f, k, v))
    o, s = hgrn_chunk_scan(q, log_f, k, v, s0)
    if reverse:
        o = jnp.flip(o, axis=1)
    return o, s

def hgrn_readout(o, g, norm_g):
    o = rmsnorm(o, norm_g.reshape(HG_HEADS, HG_DV))
    return o.reshape(o.shape[0], o.shape[1], HG_WIDTH).astype(g.dtype) * jax.nn.silu(g)

def depthwise_conv3(u, w):
    return lax.conv_general_dilated(u, w[:, None, :].astype(u.dtype), window_strides=(1,), padding='SAME',
                                    dimension_numbers=('NWC', 'WIO', 'NWC'), feature_group_count=CONV_WIDTH)

def gqa_softmax(qg, k, v):
    s = jnp.einsum('bqkgd,bskd->bkgqs', qg, k).astype(jnp.float32) * ATTN_SCALE
    p = jax.nn.softmax(s, axis=-1)
    return jnp.einsum('bkgqs,bskd->bqkgd', p.astype(v.dtype), v)

def attend_latent(q, k_lat, v_lat, k_ctx, v_ctx):
    bsz, n = q.shape[:2]
    k_all = jnp.concatenate([k_ctx, k_lat], axis=1)
    v_all = jnp.concatenate([v_ctx, v_lat], axis=1)
    qb = q.reshape(bsz, n // Q_BLOCK, Q_BLOCK, N_KV_HEADS, GQA_GROUP, HEAD_DIM).transpose(1, 0, 2, 3, 4, 5)
    o = lax.map(lambda qi: gqa_softmax(qi, k_all, v_all), qb)
    return o.transpose(1, 0, 2, 3, 4, 5).reshape(bsz, n, ATTN_WIDTH)

def attend_ctx(q, k, v):
    bsz, n = q.shape[:2]
    o = gqa_softmax(q.reshape(bsz, n, N_KV_HEADS, GQA_GROUP, HEAD_DIM), k, v)
    return o.reshape(bsz, n, ATTN_WIDTH)

def merge(pr, o_a, o_b, o_c, w_proj_a, w_proj_b, w_proj_c, w_out):
    ga, gb, gc = (jax.nn.sigmoid(t) for t in pr[11:14])
    y = ga * (o_a @ w_proj_a) + gb * (o_b @ w_proj_b) + gc * (o_c @ w_proj_c)
    return y @ w_out

def token_mixer(h_lat, h_ctx, w_in, lb_fwd, lb_bwd, hg_norm_g, conv_w, q_norm_g, k_norm_g,
                w_proj_a, w_proj_b, w_proj_c, w_out, cos, sin, ctx_out):
    pl = project(h_lat, w_in)
    pc = project(h_ctx, w_in)
    bsz = h_lat.shape[0]
    zero_state = jnp.zeros((bsz, HG_HEADS, HG_DK, HG_DV), jnp.float32)
    qc_h, ic_h = to_heads(pc[0], HG_DK), to_heads(pc[3], HG_DV)
    ql_h, il_h = to_heads(pl[0], HG_DK), to_heads(pl[3], HG_DV)
    oc_f, sc_f = hgrn_direction(qc_h, to_heads(pc[1], HG_DK), ic_h, lb_fwd, zero_state, False)
    oc_b, sc_b = hgrn_direction(qc_h, to_heads(pc[2], HG_DK), ic_h, lb_bwd, zero_state, True)
    ol_f, _ = hgrn_direction(ql_h, to_heads(pl[1], HG_DK), il_h, lb_fwd, sc_f, False)
    ol_b, _ = hgrn_direction(ql_h, to_heads(pl[2], HG_DK), il_h, lb_bwd, sc_b, True)
    a_lat = hgrn_readout(ol_f + ol_b, pl[4], hg_norm_g)
    b_lat = pl[5] * depthwise_conv3(pl[6] * pl[7], conv_w)
    q_l = apply_rope(rmsnorm(to_heads(pl[8], HEAD_DIM), q_norm_g), cos, sin)
    k_l = apply_rope(rmsnorm(to_heads(pl[9], HEAD_DIM), k_norm_g), cos, sin)
    v_l = to_heads(pl[10], HEAD_DIM)
    k_c = rmsnorm(to_heads(pc[9], HEAD_DIM), k_norm_g)
    v_c = to_heads(pc[10], HEAD_DIM)
    c_lat = attend_latent(q_l, k_l, v_l, k_c, v_c)
    y_lat = merge(pl, a_lat, b_lat, c_lat, w_proj_a, w_proj_b, w_proj_c, w_out)
    if not ctx_out:
        return y_lat, None
    a_ctx = hgrn_readout(oc_f + oc_b, pc[4], hg_norm_g)
    b_ctx = pc[5] * depthwise_conv3(pc[6] * pc[7], conv_w)
    q_c = rmsnorm(to_heads(pc[8], HEAD_DIM), q_norm_g)
    att_c = attend_ctx(q_c, k_c, v_c)
    y_ctx = merge(pc, a_ctx, b_ctx, att_c, w_proj_a, w_proj_b, w_proj_c, w_out)
    return y_lat, y_ctx

def expert_choice_ffn(h, router_w, w_gate, w_up, w_down):
    bsz, n, d = h.shape
    cap = CAPACITY_FACTOR * n // N_EXPERTS
    aff = jax.nn.softmax((h @ router_w).astype(jnp.float32), axis=-1)
    w_sel, idx = lax.top_k(aff.transpose(0, 2, 1), cap)
    xs = jax.vmap(lambda hb, ib: hb[ib])(h, idx)
    hid = jax.nn.silu(jnp.einsum('becd,edf->becf', xs, w_gate)) * jnp.einsum('becd,edf->becf', xs, w_up)
    ys = jnp.einsum('becf,efd->becd', hid, w_down) * w_sel[..., None].astype(h.dtype)
    return jax.vmap(lambda yb, ib: jnp.zeros((n, d), h.dtype).at[ib.reshape(-1)].add(yb.reshape(-1, d)))(ys, idx)

def first_inputs(seed: int = 0) -> dict:
    key = jax.random.key(seed)
    ks = jax.random.split(key, 23)

    def nrm(k, shape, scale):
        return jax.random.normal(k, shape, jnp.float32) * scale

    return {
        'x': nrm(ks[0], (BATCH, SEQ, D_MODEL), 1.0),
        'c': nrm(ks[1], (BATCH, D_MODEL), 1.0),
        'ctx': nrm(ks[2], (BATCH, CTX_LEN, D_MODEL), 1.0),
        'c_ctx': nrm(ks[3], (D_MODEL,), 1.0),
        'ada_w': nrm(ks[4], (DEPTH, D_MODEL, N_MOD * D_MODEL), 0.5 * D_MODEL ** -0.5),
        'ada_b': nrm(ks[5], (DEPTH, N_MOD * D_MODEL), 0.02),
        'norm1_g': 1.0 + nrm(ks[6], (DEPTH, D_MODEL), 0.1),
        'norm2_g': 1.0 + nrm(ks[7], (DEPTH, D_MODEL), 0.1),
        'w_in': nrm(ks[8], (DEPTH, D_MODEL, IN_WIDTH), D_MODEL ** -0.5),
        'hg_lb_logits': nrm(ks[9], (DEPTH, 2, HG_WIDTH), 1.0),
        'hg_norm_g': 1.0 + nrm(ks[10], (DEPTH, HG_WIDTH), 0.1),
        'conv_w': nrm(ks[11], (DEPTH, CONV_K, CONV_WIDTH), CONV_K ** -0.5),
        'q_norm_g': 1.0 + nrm(ks[12], (DEPTH, HEAD_DIM), 0.1),
        'k_norm_g': 1.0 + nrm(ks[13], (DEPTH, HEAD_DIM), 0.1),
        'w_proj_a': nrm(ks[14], (DEPTH, HG_WIDTH, D_MODEL), HG_WIDTH ** -0.5),
        'w_proj_b': nrm(ks[15], (DEPTH, CONV_WIDTH, D_MODEL), CONV_WIDTH ** -0.5),
        'w_proj_c': nrm(ks[16], (DEPTH, ATTN_WIDTH, D_MODEL), ATTN_WIDTH ** -0.5),
        'w_out': nrm(ks[17], (DEPTH, D_MODEL, D_MODEL), D_MODEL ** -0.5),
        'router_w': nrm(ks[18], (DEPTH, D_MODEL, N_EXPERTS), D_MODEL ** -0.5),
        'w_gate': nrm(ks[19], (DEPTH, N_EXPERTS, D_MODEL, EXPERT_FF), D_MODEL ** -0.5),
        'w_up': nrm(ks[20], (DEPTH, N_EXPERTS, D_MODEL, EXPERT_FF), D_MODEL ** -0.5),
        'w_down': nrm(ks[21], (DEPTH, N_EXPERTS, EXPERT_FF, D_MODEL), EXPERT_FF ** -0.5),
        'final_norm_g': 1.0 + nrm(ks[22], (D_MODEL,), 0.1),
    }

def first_block(x, c, ctx, c_ctx, ada_w, ada_b, norm1_g, norm2_g, w_in, hg_lb_logits, hg_norm_g, conv_w,
              q_norm_g, k_norm_g, w_proj_a, w_proj_b, w_proj_c, w_out, router_w, w_gate, w_up, w_down,
              final_norm_g):
    cos, sin = axial_rope_tables(x.shape[1])
    lb = jnp.cumsum(jax.nn.softmax(hg_lb_logits.astype(jnp.float32), axis=0), axis=0)
    lb = lb - lb[:1]
    h_ctx = ctx
    for l in range(DEPTH):
        ctx_out = l < DEPTH - 1
        sh_a, sc_a, g_a, sh_f, sc_f, g_f = modulation(c, ada_w[l], ada_b[l])
        csh_a, csc_a, cg_a, csh_f, csc_f, cg_f = modulation(c_ctx[None, :], ada_w[l], ada_b[l])
        y_lat, y_ctx = token_mixer(modulate(x, norm1_g[l], sh_a, sc_a), modulate(h_ctx, norm1_g[l], csh_a, csc_a),
                                   w_in[l], lb[l, 0], lb[l, 1], hg_norm_g[l], conv_w[l], q_norm_g[l], k_norm_g[l],
                                   w_proj_a[l], w_proj_b[l], w_proj_c[l], w_out[l], cos, sin, ctx_out)
        x = x + g_a * y_lat
        x = x + g_f * expert_choice_ffn(modulate(x, norm2_g[l], sh_f, sc_f), router_w[l], w_gate[l], w_up[l], w_down[l])
        if ctx_out:
            h_ctx = h_ctx + cg_a * y_ctx
            h_ctx = h_ctx + cg_f * expert_choice_ffn(modulate(h_ctx, norm2_g[l], csh_f, csc_f),
                                                     router_w[l], w_gate[l], w_up[l], w_down[l])
    return rmsnorm(x, final_norm_g)


DEPTH_2 = 2

N_MIXERS = 2
N_LAYERS_A = (DEPTH_2 + 1) // 2
N_LAYERS_B = DEPTH_2 // 2
MLA_HEADS = 8
QK_NOPE = 128
QK_ROPE = 64
V_DIM = 128
Q_LORA = 384
KV_LORA = 256
SWA_HEADS = 16
SWA_KV_HEADS = 4
SWA_HEAD_DIM = 64
WINDOW = 128
D_FF = 4 * D_MODEL
BLOCK_Q = 128


def rmsnorm_2(x, g):
    xf = x.astype(jnp.float32)
    y = xf * lax.rsqrt(jnp.mean(xf * xf, axis=-1, keepdims=True) + EPS)
    return (y * g.astype(jnp.float32)).astype(x.dtype)

def modulate_2(x, g, shift, scale):
    return rmsnorm_2(x, g) * (1.0 + scale[:, None, :]) + shift[:, None, :]

def rope(x, positions):
    half = QK_ROPE // 2
    inv_freq = ROPE_THETA ** (-jnp.arange(half, dtype=jnp.float32) / half)
    ang = positions.astype(jnp.float32)[..., None] * inv_freq
    shape = ang.shape[:2] + (1,) * (x.ndim - 3) + (half,)
    cos = jnp.cos(ang).reshape(shape)
    sin = jnp.sin(ang).reshape(shape)
    xf = x.astype(jnp.float32)
    x1, x2 = xf[..., :half], xf[..., half:]
    out = jnp.concatenate([x1 * cos - x2 * sin, x1 * sin + x2 * cos], axis=-1)
    return out.astype(x.dtype)

def alibi_slopes(n_heads):
    return jnp.asarray(2.0 ** (-8.0 * np.arange(1, n_heads + 1) / n_heads), dtype=jnp.float32)

def mla(h, positions, w_dq, g_q, w_uq, w_dkv, g_kv, w_ukv, w_o):
    B, S, _ = h.shape
    H = MLA_HEADS
    cq = rmsnorm_2(h @ w_dq, g_q)
    q = (cq @ w_uq).reshape(B, S, H, QK_NOPE + QK_ROPE)
    q_nope = q[..., :QK_NOPE]
    q_rope = rope(q[..., QK_NOPE:], positions)
    ckv_kr = h @ w_dkv
    ckv = rmsnorm_2(ckv_kr[..., :KV_LORA], g_kv)
    k_rope = rope(ckv_kr[..., KV_LORA:], positions)
    kv = (ckv @ w_ukv).reshape(B, S, H, QK_NOPE + V_DIM)
    k_nope, v = kv[..., :QK_NOPE], kv[..., QK_NOPE:]
    scale = (QK_NOPE + QK_ROPE) ** -0.5
    n_blk = S // BLOCK_Q
    qn_blk = q_nope.reshape(B, n_blk, BLOCK_Q, H, QK_NOPE).transpose(1, 0, 2, 3, 4)
    qr_blk = q_rope.reshape(B, n_blk, BLOCK_Q, H, QK_ROPE).transpose(1, 0, 2, 3, 4)
    key_idx = jnp.arange(S)

    def one_block(args):
        i, qn, qr = args
        s = (jnp.einsum('bqhd,bkhd->bhqk', qn, k_nope)
             + jnp.einsum('bqhr,bkr->bhqk', qr, k_rope)).astype(jnp.float32) * scale
        q_idx = i * BLOCK_Q + jnp.arange(BLOCK_Q)
        causal = key_idx[None, :] <= q_idx[:, None]
        s = jnp.where(causal[None, None], s, -jnp.inf)
        p = jax.nn.softmax(s, axis=-1).astype(v.dtype)
        return jnp.einsum('bhqk,bkhd->bqhd', p, v)

    o = lax.map(one_block, (jnp.arange(n_blk), qn_blk, qr_blk))
    o = o.transpose(1, 0, 2, 3, 4).reshape(B, S, H * V_DIM)
    return o @ w_o

def swa(h, w_qkv, b_qkv, sinks, w_o, b_o):
    B, S, _ = h.shape
    Hq, Hk, Dh, W = SWA_HEADS, SWA_KV_HEADS, SWA_HEAD_DIM, WINDOW
    G = Hq // Hk
    qkv = h @ w_qkv + b_qkv
    q = qkv[..., :Hq * Dh]
    k = qkv[..., Hq * Dh:(Hq + Hk) * Dh].reshape(B, S, Hk, Dh)
    v = qkv[..., (Hq + Hk) * Dh:].reshape(B, S, Hk, Dh)
    n_blk = S // W
    qb = q.reshape(B, n_blk, W, Hk, G, Dh)

    def band(t):
        tb = t.reshape(B, n_blk, W, Hk, Dh)
        prev = jnp.pad(tb[:, :-1], ((0, 0), (1, 0), (0, 0), (0, 0), (0, 0)))
        return jnp.concatenate([prev, tb], axis=2)

    kb, vb = band(k), band(v)
    s = jnp.einsum('bnqkgd,bnjkd->bnkgqj', qb, kb).astype(jnp.float32) * (Dh ** -0.5)
    dist = W + jnp.arange(W)[:, None] - jnp.arange(2 * W)[None, :]
    in_window = (dist >= 0) & (dist < W)
    real_key = (jnp.arange(n_blk)[:, None] > 0) | (jnp.arange(2 * W)[None, :] >= W)
    mask = in_window[None] & real_key[:, None, :]
    slopes = alibi_slopes(Hq).reshape(Hk, G)
    s = s - slopes[:, :, None, None] * dist.astype(jnp.float32)
    s = jnp.where(mask[None, :, None, None], s, -jnp.inf)
    sink = sinks.astype(jnp.float32).reshape(Hk, G)[:, :, None]
    m = jnp.maximum(s.max(axis=-1), sink)
    p = jnp.exp(s - m[..., None])
    denom = p.sum(axis=-1) + jnp.exp(sink - m)
    p = (p / denom[..., None]).astype(vb.dtype)
    o = jnp.einsum('bnkgqj,bnjkd->bnqkgd', p, vb).reshape(B, S, Hq * Dh)
    return o @ w_o + b_o

def second_inputs(seed: int = 0) -> dict:
    key = jax.random.key(seed)
    ks = jax.random.split(key, 24)
    f32 = jnp.float32

    def w(k, shape, fan_in, gain=1.0):
        return jax.random.normal(k, shape, f32) * (gain * fan_in ** -0.5)

    def g(k, shape):
        return 1.0 + 0.05 * jax.random.normal(k, shape, f32)

    A, Bn = N_LAYERS_A, N_LAYERS_B
    x = jax.random.normal(ks[0], (BATCH, SEQ, D_MODEL), f32)
    c = jax.random.normal(ks[1], (BATCH, D_MODEL), f32)
    positions = (jnp.arange(SEQ, dtype=jnp.int32)[None, :]
                 + jax.random.randint(ks[2], (BATCH, 1), 0, 1024, dtype=jnp.int32))
    return {
        'x': x,
        'c': c,
        'positions': positions,
        'w_ada': w(ks[3], (DEPTH_2, D_MODEL, 6 * D_MODEL), D_MODEL, 0.5),
        'b_ada': 0.02 * jax.random.normal(ks[4], (DEPTH_2, 6 * D_MODEL), f32),
        'g_mix': g(ks[5], (DEPTH_2, D_MODEL)),
        'g_mlp': g(ks[6], (DEPTH_2, D_MODEL)),
        'mla_w_dq': w(ks[7], (A, D_MODEL, Q_LORA), D_MODEL),
        'mla_g_q': g(ks[8], (A, Q_LORA)),
        'mla_w_uq': w(ks[9], (A, Q_LORA, MLA_HEADS * (QK_NOPE + QK_ROPE)), Q_LORA),
        'mla_w_dkv': w(ks[10], (A, D_MODEL, KV_LORA + QK_ROPE), D_MODEL),
        'mla_g_kv': g(ks[11], (A, KV_LORA)),
        'mla_w_ukv': w(ks[12], (A, KV_LORA, MLA_HEADS * (QK_NOPE + V_DIM)), KV_LORA),
        'mla_w_o': w(ks[13], (A, MLA_HEADS * V_DIM, D_MODEL), MLA_HEADS * V_DIM),
        'swa_w_qkv': w(ks[14], (Bn, D_MODEL, (SWA_HEADS + 2 * SWA_KV_HEADS) * SWA_HEAD_DIM), D_MODEL),
        'swa_b_qkv': 0.02 * jax.random.normal(ks[15], (Bn, (SWA_HEADS + 2 * SWA_KV_HEADS) * SWA_HEAD_DIM), f32),
        'swa_sinks': 0.5 * jax.random.normal(ks[16], (Bn, SWA_HEADS), f32),
        'swa_w_o': w(ks[17], (Bn, SWA_HEADS * SWA_HEAD_DIM, D_MODEL), SWA_HEADS * SWA_HEAD_DIM),
        'swa_b_o': 0.02 * jax.random.normal(ks[18], (Bn, D_MODEL), f32),
        'w_ff1': w(ks[19], (DEPTH_2, D_MODEL, D_FF), D_MODEL),
        'w_ff2': w(ks[20], (DEPTH_2, D_FF, D_MODEL), D_FF),
        'g_final': g(ks[21], (D_MODEL,)),
    }

def second_block(x, c, positions, w_ada, b_ada, g_mix, g_mlp,
              mla_w_dq, mla_g_q, mla_w_uq, mla_w_dkv, mla_g_kv, mla_w_ukv, mla_w_o,
              swa_w_qkv, swa_b_qkv, swa_sinks, swa_w_o, swa_b_o,
              w_ff1, w_ff2, g_final):
    cond = jax.nn.silu(c)
    for i in range(DEPTH_2):
        mod = cond @ w_ada[i] + b_ada[i]
        sh1, sc1, gt1, sh2, sc2, gt2 = jnp.split(mod, 6, axis=-1)
        h = modulate_2(x, g_mix[i], sh1, sc1)
        j = i // N_MIXERS
        if i % N_MIXERS == 0:
            y = mla(h, positions, mla_w_dq[j], mla_g_q[j], mla_w_uq[j], mla_w_dkv[j],
                    mla_g_kv[j], mla_w_ukv[j], mla_w_o[j])
        else:
            y = swa(h, swa_w_qkv[j], swa_b_qkv[j], swa_sinks[j], swa_w_o[j], swa_b_o[j])
        x = x + gt1[:, None, :] * y
        h = modulate_2(x, g_mlp[i], sh2, sc2)
        y = jnp.square(jax.nn.relu(h @ w_ff1[i])) @ w_ff2[i]
        x = x + gt2[:, None, :] * y
    return rmsnorm_2(x, g_final)


def setup_inputs(seed=0):
    out = dict(first_inputs(seed))
    for name, value in second_inputs(seed + 1).items():
        if name != "x":
            out[name + "_2"] = value
    return out


def reference(
    x, c, ctx, c_ctx, ada_w, ada_b, norm1_g, norm2_g, w_in, hg_lb_logits, hg_norm_g, conv_w,
    q_norm_g, k_norm_g, w_proj_a, w_proj_b, w_proj_c, w_out, router_w, w_gate, w_up, w_down,
    final_norm_g, c_2, positions_2, w_ada_2, b_ada_2, g_mix_2, g_mlp_2, mla_w_dq_2, mla_g_q_2,
    mla_w_uq_2, mla_w_dkv_2, mla_g_kv_2, mla_w_ukv_2, mla_w_o_2, swa_w_qkv_2, swa_b_qkv_2,
    swa_sinks_2, swa_w_o_2, swa_b_o_2, w_ff1_2, w_ff2_2, g_final_2,
):
    x = first_block(
        x, c, ctx, c_ctx, ada_w, ada_b, norm1_g, norm2_g, w_in, hg_lb_logits, hg_norm_g, conv_w,
        q_norm_g, k_norm_g, w_proj_a, w_proj_b, w_proj_c, w_out, router_w, w_gate, w_up, w_down,
        final_norm_g,
    )
    return second_block(
        x, c_2, positions_2, w_ada_2, b_ada_2, g_mix_2, g_mlp_2, mla_w_dq_2, mla_g_q_2,
        mla_w_uq_2, mla_w_dkv_2, mla_g_kv_2, mla_w_ukv_2, mla_w_o_2, swa_w_qkv_2, swa_b_qkv_2,
        swa_sinks_2, swa_w_o_2, swa_b_o_2, w_ff1_2, w_ff2_2, g_final_2,
    )


_drawn_inputs = setup_inputs


def setup_inputs(seed=0):
    import zlib

    import numpy as np

    out = dict(_drawn_inputs(seed))
    spreads = {}
    factors = {'ctx': 6.885,
     'c_ctx': 2.835,
     'norm2_g': 2.966,
     'hg_norm_g': 4.711,
     'q_norm_g': 8.0,
     'k_norm_g': 8.0,
     'g_mix_2': 6.463,
     'mla_g_q_2': 8.0,
     'mla_g_kv_2': 8.0,
     'swa_b_qkv_2': 8.0,
     'swa_sinks_2': 145.909,
     'swa_b_o_2': 31.294}
    for name, (base, spread) in spreads.items():
        noise = np.random.default_rng([zlib.crc32(name.encode()), seed]).standard_normal(out[name].shape)
        drawn = base * np.exp(spread * noise) if base else spread * noise
        out[name] = jnp.asarray(drawn.astype(out[name].dtype))
    for name, factor in factors.items():
        out[name] = (out[name] * factor).astype(out[name].dtype)
    return out
```

```python
import numpy as np
import concourse.bass as bass
from concourse import mybir
from contextlib import ExitStack

P = 128
D = 1024
KT = D // P
T = 512
TC = 256
TA = T + TC
NT, NC_, NA = T // P, TC // P, TA // P
HG = 8
GRID_W = 64
EPS = 1e-6
NE, CAP, FF = 16, 64, 1024
NPAIR = NE // 2
LEVELS = (64, 32, 16, 8, 4, 2, 1)
NL = len(LEVELS)
SLOTS, WIDE = 4, 8
UNIT = 2048
NEG = -1e30
MLA_H, NOPE, ROPE_D, QL, KVL = 8, 128, 64, 384, 256
QT, KVT = QL // P, KVL // P
DFF = 4 * D
FT = DFF // P

C_ID, C_ONE, C_BLK, C_ROT1, C_ROT2 = 0, 128, 256, 384, 512
C_CAUS = 640
C_DIST = 768
C_SLOPE = C_DIST + 256
C_PART = C_SLOPE + 16
C_SEL = C_PART + 4
C_INV = C_SEL + 4
N_CST = C_INV + 4
H_MASK, H_SCAN = 0, 2 * (NL + 1) * P
N_HCST = H_SCAN + TA
A_COS, A_SIN, N_ACST = 0, T, 2 * T

V_C, V_CC, V_C2, V_ADAB, V_N1, V_N2, V_FN, V_HG, V_CONV = 0, 8, 16, 24, 72, 80, 88, 96, 104
V_ADAB2, V_GMIX, V_GMLP = 128, 224, 240
V_GF, V_GQ, V_GKV, V_BQKV, V_BO, V_QN, V_KN = 256, 264, 267, 269, 281, 289, 290
N_VEC = 384

U_ADA = 0
U_HG = U_ADA + 3 * 24
U_QKV = U_HG + 4 * HG
U_MERGE = U_QKV + 6
U_OUT = U_MERGE + 24
U_EXP = U_OUT + 4
U_MD = U_EXP + 24 * NPAIR
U_MUQ = U_MD + 4
U_MUKV = U_MUQ + 3
U_MWO = U_MUKV + 2
U_FF = (U_MWO + 4, U_MWO + 4 + 32 + 10)
U_SQKV = U_MWO + 4 + 32
U_SWO = U_SQKV + 6
N_UNITS = U_FF[1] + 32
N_STREAM = U_MD + (N_UNITS - U_MD + SLOTS - 1) // SLOTS * SLOTS
assert (U_MD - U_EXP) % WIDE == 0 and (U_MD - U_EXP) % SLOTS == 0

G_X = 0
G_ADA = G_X + 2 * KT
G_HG = G_ADA + 36
HGG = 10
G_QKV = G_HG + HGG * HG
G_MERGE = G_QKV + 14
G_OUT = G_MERGE + 48
G_H2T = G_OUT + KT
G_MD = G_H2T + 8
G_MUQ = G_MD + 6
G_MUKV = G_MUQ + 12
G_MWO = G_MUKV + 16
G_FF0 = G_MWO + KT
G_SQKV = G_FF0 + FT
G_SWO = G_SQKV + 12
G_FF1 = G_SWO + KT
G_FIN = G_FF1 + FT


def build(nc, stream, vecs, cst, hcst, acst, iota, x, ctxt, router, pos, sinks, bv, out):
    fp32, i32, u32 = mybir.dt.float32, mybir.dt.int32, mybir.dt.uint32
    ALU, ACT, AX = mybir.AluOpType, mybir.ActivationFunctionType, mybir.AxisListType
    ctx = ExitStack()
    with ctx:
        def sb(name, shape, dt=fp32):
            return ctx.enter_context(nc.sbuf_tensor(name, shape, dt))

        def sem(name):
            return ctx.enter_context(nc.semaphore(name))

        ring = [sb(f"ring{s}", [P, UNIT]) for s in range(SLOTS)]
        xT = sb("xT", [P, KT, T])
        hT = sb("hT", [P, KT, T])
        C = sb("C", [P, N_CST])
        V = sb("V", [P, N_VEC])
        cs = sb("cs", [P, KT, 32])
        mod = sb("mod", [P, 48])
        modc = sb("modc", [P, 16])
        mod2 = sb("mod2", [P, 96])
        gsc = sb("gsc", [P, 7, KT])
        rstd = sb("rstd", [P, T])
        pt = sb("pt", [P, 2, T])
        st8 = sb("st8", [P, 32])
        arena_n = 33100
        arena = sb("arena", [P, arena_n])
        PS = ctx.enter_context(nc.psum_tensor("PS", [P, 8, 512], fp32))

        def area(at, *shape):
            n = int(np.prod(shape))
            assert at + n <= arena_n, (at + n, arena_n)
            v = arena[:, at:at + n]
            names = "abcd"[:len(shape)]
            if len(shape) == 1:
                return v
            return v.rearrange(f"p ({' '.join(names)}) -> p {' '.join(names)}",
                               **{k: s for k, s in zip(names[1:], shape[1:])})

        def slot(u):
            j = u - U_EXP
            if 0 <= j < U_MD - U_EXP and j % WIDE >= SLOTS:
                return j % WIDE
            return u % SLOTS

        def arrival(u):
            j = u - U_EXP
            if j < 0:
                return u // SLOTS + 1
            before = sum(1 for s in range(slot(u), U_EXP, SLOTS))
            if j < U_MD - U_EXP:
                return j // WIDE + 1 + (before if slot(u) < SLOTS else 0)
            return before + (U_MD - U_EXP) // WIDE + (u - U_MD) // SLOTS + 1

        ring += [area(arena_n - (WIDE - s) * UNIT, UNIT) for s in range(SLOTS, WIDE)]

        ident = C[:, C_ID:C_ID + P]
        ones = C[:, C_ONE:C_ONE + P]

        w_loaded = [sem(f"w_loaded{s}") for s in range(WIDE)]
        w_used = sem("w_used")
        mm_done = sem("mm_done")
        evac_done = sem("evac_done")
        pt_used = sem("pt_used")
        in_const, in_vec, in_x, in_cst2, in_acst, in_iota = (sem(n) for n in
            ("in_const", "in_vec", "in_x", "in_cst2", "in_acst", "in_iota"))
        vec_t, vec_ok, cs_ok, ada_sel, mods_ok = (sem(n) for n in
            ("vec_t", "vec_ok", "cs_ok", "ada_sel", "mods_ok"))
        n_sq, n_ss, n_r, n_h = (sem(n) for n in ("n_sq", "n_ss", "n_r", "n_h"))
        x_ok = sem("x_ok")

        def unit_wait(pe, su, per=0):
            pe.wait_ge(w_loaded[slot(su)], 16 * arrival(su) + 16 * per)

        def apart(act):
            nc.scalar.activation(st8[0:1, 30:31], st8[0:1, 31:32], ACT.Copy)
            act.drain()

        def first(eng, s):
            eng.drain().then_inc(s, 1)

        pend = [0]

        def mm(out_, lhsT, rhs, start, stop_, done=None, **kw):
            ins = nc.tensor.matmul(out_, lhsT, rhs, start=start, stop=stop_, **kw)
            if done is not None:
                ins.then_inc(done, 1)
            elif pend[0]:
                ins.then_inc(w_used, pend[0])
                pend[0] = 0

        def flush(pe):
            if pend[0]:
                pe.drain().then_inc(w_used, pend[0])
                pend[0] = 0

        def bank_wait(pe, g, first_free=2):
            if isinstance(g, int) and g < 2:
                return
            pe.wait_ge(evac_done, g - 1)

        def gemm(pe, g, gp, su, per, tiles, rhs, kt=KT, ncol=T, units=None, cols=512, waits=True):
            kpu = UNIT // cols
            for n, c0 in enumerate(tiles):
                bank = (gp + n) % 2
                bank_wait(pe, g + n)
                for k in range(kt):
                    if n == 0 and k % kpu == 0 and waits:
                        unit_wait(pe, su + k // kpu, per)
                    w = ring[slot(su + k // kpu)][:, :].rearrange("p (k n) -> p k n", n=cols)
                    mm(PS[:, bank, 0:ncol], w[:, k % kpu, c0:c0 + P], rhs[:, k, 0:ncol],
                       k == 0, k == kt - 1, mm_done if k == kt - 1 else None)

        def gemm_tok(pe, g, gp, su, tok, toks, c0, ncol, kt=KT, cols=512):
            kpu = UNIT // cols
            bank = gp % 2
            bank_wait(pe, g)
            for m, t0 in enumerate(toks):
                for k in range(kt):
                    w = ring[slot(su + k // kpu)][:, :].rearrange("p (k n) -> p k n", n=cols)
                    last = k == kt - 1 and m == len(toks) - 1
                    mm(PS[:, bank, m * ncol:(m + 1) * ncol], tok[:, k, t0:t0 + P],
                       w[:, k % kpu, c0:c0 + ncol], k == 0, k == kt - 1, mm_done if last else None)

        def evac(act, g, gp, dst, n=T, func=ACT.Copy, w=None, **kw):
            act.wait_ge(mm_done, g + 1)
            src = PS[:, gp % 2, 0:n]
            if w is not None:
                src = src.rearrange("p (a b) -> p a b", b=w)
            nc.scalar.activation(dst, src, func, **kw).then_inc(evac_done, 1)

        def norm_pe(pe, use, sq, kt=KT, n=T):
            for k in range(kt):
                pe.wait_ge(n_sq, NSQ[use] + k + 1)
                mm(PS[:, 7, 0:n], ones, sq[:, k, 0:n], k == 0, k == kt - 1, n_ss if k == kt - 1 else None)

        def norm_act(act, use, src, sq, kt=KT, n=T, ready=None):
            if ready is not None:
                act.wait_ge(*ready)
            for k in range(kt):
                nc.scalar.activation(sq[:, k, 0:n], src[:, k, 0:n], ACT.Square).then_inc(n_sq, 1)
            act.wait_ge(n_ss, use + 1)
            if use > 0:
                act.wait_ge(n_h, NH[use])
            act.drain()
            nc.scalar.activation(rstd[:, 0:n], PS[:, 7, 0:n], ACT.Ln, bias=epsb, scale=1.0 / (kt * P))
            act.drain()
            nc.scalar.activation(rstd[:, 0:n], rstd[:, 0:n], ACT.Exp, scale=-0.5).then_inc(n_r, 1)

        def norm_dve(v, use, src, dst, g, sh=None, kt=KT, n=T):
            v.wait_ge(n_r, use + 1)
            for k in range(kt):
                v.drain()
                if sh is None:
                    nc.vector.scalar_tensor_tensor(dst[:, k, 0:n], src[:, k, 0:n], g(k), rstd[:, 0:n],
                                                   ALU.mult, ALU.mult).then_inc(n_h, 1)
                else:
                    nc.vector.tensor_tensor(dst[:, k, 0:n], src[:, k, 0:n], rstd[:, 0:n], ALU.mult)
                    v.drain()
                    nc.vector.tensor_scalar(dst[:, k, 0:n], dst[:, k, 0:n], g(k), sh(k),
                                            ALU.mult, ALU.add).then_inc(n_h, 1)

        KTS = [KT, KT, KT, KT, KT, QT, KVT, KT, KT, KT, KT]
        NSQ = [sum(KTS[:i]) for i in range(len(KTS) + 1)]
        NH = NSQ
        epsb = st8[:, 31:32]
        HC = area(0, KT, TC)
        OA = area(2048, KT, T)
        OB = area(6144, KT, T)
        x_tok = area(10240, NT, D)
        c_tok = area(14336, NC_, D)
        cT = area(16384, KT, TC)
        arow = area(18432, 2, 512)
        v_rows = area(19456, 3, P)
        at = 10240
        H_CST = area(at, N_HCST); at += N_HCST
        hq = area(at, 2, T); at += 2 * T
        hg = area(at, 2, T); at += 2 * T
        hv = area(at, 2, NA, P); at += 2 * TA
        hz = area(at, 2, TA); at += 2 * TA
        hp = area(at, 3, T); at += 3 * T
        hW = area(at, NL, T); at += NL * T
        hk = area(at, 2, TA); at += 2 * TA
        hX = area(at, TA); at += TA
        htmp = area(at, TA); at += TA
        hQ = area(at, 2, T); at += 2 * T
        hKo = area(at, 2, TA); at += 2 * TA
        hKT = area(at, TA); at += TA
        hS = area(at, 2, 5, P); at += 10 * P
        hAT = area(at, 2, T); at += 2 * T
        ho = area(at, T); at += T
        hsq = area(at, T); at += T
        hT_ = area(at, 2, NA); at += 2 * NA
        hr = rstd[:, :]
        hM = pt[:, :, :].rearrange("p a b -> p (a b)")
        hmask = H_CST[:, H_MASK:H_MASK + 2 * (NL + 1) * P].rearrange("p (d n) -> p d n", d=2)
        hscan = H_CST[:, H_SCAN:H_SCAN + TA]

        h_l, h_km, h_x, h_e, h_kout, h_w, h_d, h_wl = (sem(n) for n in
            ("h_l", "h_km", "h_x", "h_e", "h_kout", "h_w", "h_d", "h_wl"))
        h_T, h_kT, h_A, h_afree, h_at, h_st, h_S, h_conv = (sem(n) for n in
            ("h_T", "h_kT", "h_A", "h_afree", "h_at", "h_st", "h_S", "h_conv"))
        h_o, h_sq, h_ss, h_r, h_out = (sem(n) for n in ("h_o", "h_sq", "h_ss", "h_r", "h_out"))
        h_sl, h_sm, h_sg = (sem(n) for n in ("h_sl", "h_sm", "h_sg"))

        WALK = [[NT + i for i in range(NC_)] + list(range(NT - 1)),
                [NA - 1 - i for i in range(NC_)] + list(range(NT - 1, 0, -1))]
        BEFORE = [[NC_ - 1 + i for i in range(NT)], [NC_ - 1 + NT - 1 - i for i in range(NT)]]

        def start_pe(pe):
            pe.wait_ge(in_const, 16)
            pe.wait_ge(in_vec, 16)
            for j in range(3):
                nc.tensor.transpose(PS[:, 6, j * P:(j + 1) * P], v_rows[:, j, :], ident)\
                    .then_inc(vec_t, 1)
            pe.wait_ge(in_x, 32)
            for k in range(KT):
                g = G_X + k
                bank_wait(pe, g)
                for m in range(NT):
                    ins = nc.tensor.transpose(PS[:, g % 2, m * P:(m + 1) * P],
                                              x_tok[:, m, k * P:(k + 1) * P], ident)
                ins.then_inc(mm_done, 1)
            for k in range(KT):
                g = G_X + KT + k
                bank_wait(pe, g)
                for m in range(NC_):
                    ins = nc.tensor.transpose(PS[:, g % 2, m * P:(m + 1) * P],
                                              c_tok[:, m, k * P:(k + 1) * P], ident)
                ins.then_inc(mm_done, 1)
            pe.wait_ge(cs_ok, 2)
            first(pe, ada_sel)
            sel = C[:, C_SEL:C_SEL + 3]

            def select(i, c):
                pe.wait_ge(evac_done, G_ADA + 2 * i + c + 1)
                for j in range(4):
                    ins = nc.tensor.matmul(PS[:, 4, bass.ds(24 * i + 12 * c + 3 * j, 3)],
                                           arow[:, c, j * P:(j + 1) * P], sel, start=True, stop=True)
                ins.then_inc(ada_sel, 1)

            with pe.Fori(0, 18) as i:
                for c in range(2):
                    g = G_ADA + 2 * i + c
                    pe.wait_ge(evac_done, g - 1)
                    for k in range(KT):
                        q = k % 4
                        if k % 4 == 0:
                            unit_wait(pe, U_ADA + 2 * c + k // 4, i)
                        w = ring[2 * c + k // 4][:, (k % 4) * 512:(k % 4 + 1) * 512]
                        ins = nc.tensor.matmul(PS[32 * q:32 * q + 32, (G_ADA + c) % 2, :], cs[:, k, :], w,
                                               start=k < 4, stop=k >= 4, tile_position=(0, 32 * q))
                        if k == KT - 1:
                            ins.then_inc(mm_done, 1)
                        elif k % 4 == 3:
                            ins.then_inc(w_used, 1)
                select(i, 0)
                select(i, 1)
                pe.drain().then_inc(w_used, 2)

        def start_act(act):
            act.wait_ge(vec_t, 3)
            nc.scalar.activation(V[:, :], PS[:, 6, 0:N_VEC], ACT.Copy).then_inc(vec_ok, 1)
            act.wait_ge(cs_ok, 1)
            act.drain()
            for j, v0 in enumerate((V_C, V_CC, V_C2)):
                ins = nc.scalar.activation(cs[:, :, j], V[:, v0:v0 + KT], ACT.Silu)
            ins.then_inc(cs_ok, 1)
            for k in range(KT):
                evac(act, G_X + k, G_X + k, xT[:, k, :])
            for k in range(KT):
                evac(act, G_X + KT + k, G_X + KT + k, cT[:, k, :], n=TC)
            with act.Fori(0, 18) as i:
                for c in range(2):
                    g = G_ADA + 2 * i + c
                    act.wait_ge(mm_done, g + 1)
                    act.wait_ge(ada_sel, 2 * i + 1)
                    nc.scalar.activation(arow[:, c, :], PS[:, (G_ADA + c) % 2, :], ACT.Copy)\
                        .then_inc(evac_done, 1)
            nc.scalar.preload_act_table_set("natural_log_exp_and_others")

        def start_dve(v):
            nc.vector.memset(st8[:, 31:32], EPS)
            nc.vector.memset(cs[:, :, :], 0.0).then_inc(cs_ok, 1)
            v.wait_ge(ada_sel, 37)
            v.wait_ge(vec_ok, 1)
            m3 = PS[:, 4, 0:432].rearrange("p (c m) -> p c m", m=3)
            nc.vector.tensor_tensor(mod[:, :], m3[:, 0:48, 0], V[:, V_ADAB:V_ADAB + 48], ALU.add)
            nc.vector.tensor_tensor(modc[:, :], m3[:, 0:16, 1], V[:, V_ADAB:V_ADAB + 16], ALU.add)
            nc.vector.tensor_tensor(mod2[:, :], m3[:, 48:144, 2], V[:, V_ADAB2:V_ADAB2 + 96], ALU.add)
            v.drain()
            for r, (m, s, n) in enumerate(((modc, 8, V_N1), (mod, 8, V_N1), (mod, 32, V_N2),
                                           (mod2, 8, V_GMIX), (mod2, 56, V_GMIX + 8), (mod2, 32, V_GMLP))):
                nc.vector.scalar_tensor_tensor(gsc[:, r, :], m[:, s:s + KT], 1.0, V[:, n:n + KT],
                                               ALU.add, ALU.mult)
            nc.vector.scalar_tensor_tensor(gsc[:, 6, :], mod2[:, 80:88], 1.0, V[:, V_GMLP + 8:V_GMLP + 16],
                                           ALU.add, ALU.mult).then_inc(mods_ok, 1)
            v.drain()
            norm_dve(v, 0, cT, HC, lambda k: gsc[:, 0, k:k + 1], lambda k: modc[:, k:k + 1], n=TC)
            norm_dve(v, 1, xT, hT, lambda k: gsc[:, 1, k:k + 1], lambda k: mod[:, k:k + 1])

        def start_norm_act(act):
            norm_act(act, 0, cT, HC, n=TC, ready=(evac_done, G_X + 2 * KT))
            norm_act(act, 1, xT, hT)

        def start_norm_pe(pe):
            norm_pe(pe, 0, HC, n=TC)
            norm_pe(pe, 1, hT)
            pe.wait_ge(n_h, NH[2])

        def first_products(pe, h, par, hh):
            g = G_HG + HGG * h
            gemm(pe, g, G_HG, U_HG, hh, (0, 128, 256, 384), hT)
            pend[0] += 2
            gemm(pe, g + 4, G_HG + 4, U_HG + 2, hh, (0,), hT)

        def second_products(pe, h, par, hh):
            g = G_HG + HGG * h
            gemm(pe, g + 5, G_HG + 5, U_HG + 2, hh, (128, 256), hT, waits=False)
            bank = (G_HG + 7) % 2
            bank_wait(pe, g + 7)
            for d in range(2):
                for k in range(KT):
                    w = ring[slot(U_HG + 2 + k // 4)]
                    c0 = (k % 4) * 512 + 128 + 128 * d
                    mm(PS[:, bank, d * TC:(d + 1) * TC], w[:, c0:c0 + P], HC[:, k, :], k == 0, k == KT - 1,
                       mm_done if d == 1 and k == KT - 1 else None)
            gemm_tok(pe, g + 8, G_HG + 8, U_HG + 2, hT, range(0, T, P), 384, P)
            gemm_tok(pe, g + 9, G_HG + 9, U_HG + 2, HC, range(0, TC, P), 384, P)
            pend[0] += 2
            flush(pe)

        def rec_pe(pe, h, par, d):
            Ko, W = hKo[:, d, :], hW
            pe.wait_ge(h_kout, 2 * h + d + 2)
            if d == 0:
                pe.wait_ge(h_r, h + 1)
            else:
                pe.wait_ge(h_S, 2 * h + 1)
            for m in range(NA):
                ins = nc.tensor.transpose(PS[:, 6 + m // 4, (m % 4) * P:(m % 4 + 1) * P],
                                          Ko[:, m * P:(m + 1) * P], ident)
            ins.then_inc(h_T, 1)
            pe.wait_ge(h_wl, 2 * h + d + 1)
            for i in range(NT):
                b0 = 2 + 2 * (i % 2)
                n = 8 * h + 4 * d + i
                pe.wait_ge(h_afree, n + 1)
                tile = slice(i * P, (i + 1) * P)
                for lv in range(NL):
                    nc.tensor.matmul(PS[:, b0 + lv // 4, (lv % 4) * P:(lv % 4 + 1) * P],
                                     W[:, lv, tile], W[:, lv, tile], start=True, stop=True)
                nc.tensor.matmul(PS[:, b0 + NL // 4, (NL % 4) * P:(NL % 4 + 1) * P],
                                 hk[:, d, tile], hq[:, par, tile], start=True, stop=True).then_inc(h_A, 1)
            pe.wait_ge(h_kT, 2 * h + d + 1)
            for n, m in enumerate(WALK[d]):
                ins = nc.tensor.matmul(PS[:, 6 + n // 4, (n % 4) * P:(n % 4 + 1) * P],
                                       hKT[:, m * P:(m + 1) * P], hv[:, par, m, :], start=True, stop=True)
            ins.then_inc(h_st, 1)

        def out_pe(pe, h, par):
            pe.wait_ge(h_S, 2 * h + 2)
            pe.wait_ge(h_at, 2 * h + 2)
            for i in range(NT):
                tile = slice(i * P, (i + 1) * P)
                o = PS[:, 6, tile]
                nc.tensor.matmul(o, hv[:, par, i, :], hAT[:, 0, tile], start=True, stop=False)
                nc.tensor.matmul(o, hv[:, par, i, :], hAT[:, 1, tile], start=False, stop=False)
                nc.tensor.matmul(o, hS[:, 0, BEFORE[0][i], :], hQ[:, 0, tile], start=False, stop=False)
                ins = nc.tensor.matmul(o, hS[:, 1, BEFORE[1][i], :], hQ[:, 1, tile], start=False, stop=True)
            ins.then_inc(h_o, 1)
            pe.wait_ge(h_sq, h + 1)
            nc.tensor.matmul(PS[:, 7, :], ones, hsq, start=True, stop=True).then_inc(h_ss, 1)

        def head_pe(pe, h, par, more):
            if more:
                first_products(pe, h + 1, 1 - par, h + 1)
                flush(pe)
            rec_pe(pe, h, par, 0)
            if more:
                second_products(pe, h + 1, 1 - par, h + 1)
            rec_pe(pe, h, par, 1)
            out_pe(pe, h, par)

        def hgrn_pe(pe):
            pe.wait_ge(in_cst2, 16)
            first(pe, h_ss)
            first_products(pe, 0, 0, 0)
            flush(pe)
            second_products(pe, 0, 0, 0)
            with pe.Fori(0, 3) as i:
                head_pe(pe, 2 * i, 0, True)
                head_pe(pe, 2 * i + 1, 1, True)
            head_pe(pe, 6, 0, True)
            head_pe(pe, 7, 1, False)

        def evac_first(act, h, par, n):
            g = G_HG + HGG * h
            if n == 2 and not (isinstance(h, int) and h == 0):
                act.wait_ge(h_conv, h)
            dst = (hq[:, par, :], hg[:, par, :], hp[:, 0, :], hp[:, 1, :], hp[:, 2, :])[n]
            act.wait_ge(mm_done, g + n + 1)
            nc.scalar.activation(dst, PS[:, (G_HG + n) % 2, :], ACT.Copy).then_inc(evac_done, 1)

        def evac_second(act, h, par, n):
            g = G_HG + HGG * h + 5
            act.wait_ge(mm_done, g + n + 1)
            src = PS[:, (G_HG + 5 + n) % 2, :]
            if n < 2:
                dst = hz[:, n, 0:T]
            elif n == 2:
                dst, src = hz[:, :, T:TA], src.rearrange("p (a b) -> p a b", a=2)
            elif n == 3:
                dst, src = hv[:, par, 0:NT, :], src.rearrange("p (a b) -> p a b", b=P)
            else:
                dst, src = hv[:, par, NT:NA, :], src[:, 0:TC].rearrange("p (a b) -> p a b", b=P)
            nc.scalar.activation(dst, src, ACT.Copy).then_inc(evac_done, 1)

        def gate_act(act, h, par):
            if not (isinstance(h, int) and h == 0):
                act.drain()
                act.wait_ge(h_ss, h + 1)
            else:
                act.drain()
            nc.scalar.activation(hsq, hg[:, par, :], ACT.Abs)
            act.drain()
            nc.scalar.activation(hsq, hsq, ACT.Exp, scale=-1.0)
            act.drain()
            nc.scalar.activation(hsq, hsq, ACT.Ln, bias=1.0).then_inc(h_sl, 1)
            act.wait_ge(h_sm, h + 1)
            nc.scalar.activation(hsq, hsq, ACT.Exp).then_inc(h_sg, 1)

        def prep_act(act, h, par, d):
            z = hz[:, d, :]
            n = 2 * h + d
            if not (isinstance(n, int) and n == 0):
                act.drain()
                act.wait_ge(h_kout, n + 1)
            else:
                act.drain()
            nc.scalar.activation(htmp, z, ACT.Abs)
            act.drain()
            nc.scalar.activation(htmp, htmp, ACT.Exp, scale=-1.0)
            act.drain()
            nc.scalar.activation(htmp, htmp, ACT.Ln, bias=1.0).then_inc(h_l, 1)
            act.wait_ge(h_km, n + 1)
            nc.scalar.activation(hk[:, d, :], hk[:, d, :], ACT.Exp)
            act.wait_ge(h_x, n + 1)
            nc.scalar.activation(hT_[:, d, :], hT_[:, d, :], ACT.Exp)
            if d == 0:
                nc.scalar.activation(hKo[:, 0, :], htmp, ACT.Exp)
                nc.scalar.activation(hQ[:, 0, :], hX[:, 0:T], ACT.Exp).then_inc(h_e, 1)
            else:
                nc.scalar.activation(hKo[:, 1, :], hX, ACT.Exp)
                nc.scalar.activation(hQ[:, 1, :], htmp[:, 0:T], ACT.Exp).then_inc(h_e, 1)

        def level_act(act, h, d, lv):
            act.wait_ge(h_d, 2 * NL * h + NL * d + lv + 1)
            nc.scalar.activation(hW[:, lv, :], hW[:, lv, :], ACT.Exp).then_inc(h_w, 1)

        def keys_act(act, h, d):
            act.wait_ge(h_T, 2 * h + d + 1)
            nc.scalar.activation(hKT, PS[:, 6:8, :].rearrange("p a b -> p (a b)")[:, 0:TA], ACT.Copy)\
                .then_inc(h_kT, 1)

        def head_act(act, h, par, more):
            gate_act(act, h, par)
            prep_act(act, h, par, 0)
            after = {0: 0, 1: 1, 3: 2, 5: 3}
            for lv in range(NL):
                level_act(act, h, 0, lv)
                if more and lv in after:
                    evac_first(act, h + 1, 1 - par, after[lv])
            prep_act(act, h, par, 1)
            if more:
                evac_first(act, h + 1, 1 - par, 4)
            keys_act(act, h, 0)
            after = {0: 0, 1: 1, 3: 2, 5: 3, 6: 4}
            for lv in range(NL):
                level_act(act, h, 1, lv)
                if more and lv in after:
                    evac_second(act, h + 1, 1 - par, after[lv])
            keys_act(act, h, 1)
            act.wait_ge(h_o, h + 1)
            if not (isinstance(h, int) and h == 0):
                act.wait_ge(h_out, h + 1)
            nc.scalar.activation(ho, PS[:, 6, :], ACT.Copy)
            act.wait_ge(h_gm, h + 1)
            nc.scalar.activation(hsq, PS[:, 6, :], ACT.Square).then_inc(h_sq, 1)
            act.wait_ge(h_ss, h + 2)
            nc.scalar.activation(hr, PS[:, 7, :], ACT.Ln, bias=epsb, scale=1.0 / P)
            act.drain()
            nc.scalar.activation(hr, hr, ACT.Exp, scale=-0.5).then_inc(h_r, 1)

        h_gm = sem("h_gm")

        def hgrn_act(act):
            first(act, h_r)
            for n in range(5):
                evac_first(act, 0, 0, n)
            for n in range(5):
                evac_second(act, 0, 0, n)
            with act.Fori(0, 3) as i:
                head_act(act, 2 * i, 0, True)
                head_act(act, 2 * i + 1, 1, True)
            head_act(act, 6, 0, True)
            head_act(act, 7, 1, False)

        def conv_dve(v, h):
            v.wait_ge(evac_done, G_HG + HGG * h + 5)
            w = [V[:, bass.ds(V_CONV + 8 * t + h, 1)] for t in range(3)]
            p5, p6, p7 = hp[:, 0, :], hp[:, 1, :], hp[:, 2, :]
            nc.vector.tensor_tensor(p6, p6, p7, ALU.mult)
            v.drain()
            nc.vector.tensor_scalar(p7, p6, w[1], None, ALU.mult)
            v.drain()
            nc.vector.scalar_tensor_tensor(p7[:, 1:T], p6[:, 0:T - 1], w[0], p7[:, 1:T], ALU.mult, ALU.add)
            v.drain()
            nc.vector.scalar_tensor_tensor(p7[:, 0:T - 1], p6[:, 1:T], w[2], p7[:, 0:T - 1],
                                           ALU.mult, ALU.add)
            v.drain()
            dst = OB[:, h, :] if isinstance(h, int) else OB[:, bass.ds(h, 1), :].rearrange("p a b -> p (a b)")
            nc.vector.tensor_tensor(dst, p7, p5, ALU.mult).then_inc(h_conv, 1)

        def prep_dve(v, h, par, d):
            z = hz[:, d, :]
            n = 2 * h + d
            v.wait_ge(h_l, n + 1)
            nc.vector.scalar_tensor_tensor(htmp, z, 0.0, htmp, ALU.min, ALU.subtract)
            v.drain()
            nc.vector.tensor_tensor(hk[:, d, :], htmp, z, ALU.subtract).then_inc(h_km, 1)
            nc.vector.tensor_tensor_scan(hX, hscan, htmp, 0.0, ALU.mult, ALU.add)
            v.drain()
            x3 = hX.rearrange("p (m t) -> p m t", t=P)
            t3 = htmp.rearrange("p (m t) -> p m t", t=P)
            nc.vector.tensor_copy(hT_[:, d, :], x3[:, :, P - 1])
            if d == 1:
                v.drain()
                nc.vector.tensor_tensor(hX, hX, htmp, ALU.subtract)
            v.drain()
            nc.vector.tensor_tensor(t3, hT_[:, d, :].unsqueeze(2).broadcast_to([P, NA, P]), x3,
                                    ALU.subtract).then_inc(h_x, 1)
            v.wait_ge(h_e, n + 1)
            nc.vector.tensor_tensor(hKo[:, d, :], hKo[:, d, :], hk[:, d, :], ALU.mult)
            nc.vector.tensor_tensor(hQ[:, d, :], hQ[:, d, :], hq[:, par, :], ALU.mult).then_inc(h_kout, 1)

        def level_views(lv):
            L = LEVELS[lv]
            X = hX[:, 0:T].rearrange("p (n a l) -> p n a l", a=2, l=L)
            W = hW[:, lv, :].rearrange("p (n a l) -> p n a l", a=2, l=L)
            return L, X, W

        def levels_dve(v, h, par, d):
            def factors(lv):
                L, X, W = level_views(lv)
                mid = X[:, :, 1, 0:1].broadcast_to([P, T // (2 * L), L])
                nc.vector.tensor_tensor(W[:, :, 0, :], mid, X[:, :, 0, :], ALU.subtract)
                nc.vector.tensor_tensor(W[:, :, 1, :], X[:, :, 1, :], mid, ALU.subtract).then_inc(h_d, 1)

            def roles(lv):
                L, X, W = level_views(lv)
                v.wait_ge(h_w, 2 * NL * h + NL * d + lv + 1)
                a, b = (hk[:, d, 0:T], hq[:, par, :]) if d == 0 else (hq[:, par, :], hk[:, d, 0:T])
                a = a.rearrange("p (n a l) -> p n a l", a=2, l=L)
                b = b.rearrange("p (n a l) -> p n a l", a=2, l=L)
                nc.vector.tensor_tensor(W[:, :, 0, :], W[:, :, 0, :], a[:, :, 0, :], ALU.mult)
                ins = nc.vector.tensor_tensor(W[:, :, 1, :], W[:, :, 1, :], b[:, :, 1, :], ALU.mult)
                if lv == NL - 1:
                    ins.then_inc(h_wl, 1)

            factors(0)
            for lv in range(NL):
                if lv + 1 < NL:
                    factors(lv + 1)
                roles(lv)

        def scores_dve(v, h, d):
            for i in range(NT):
                b0 = 2 + 2 * (i % 2)
                v.drain()
                v.wait_ge(h_A, 8 * h + 4 * d + i + 1)
                nc.vector.tensor_tensor(hM, PS[:, b0:b0 + 2, :].rearrange("p a b -> p (a b)"),
                                        hmask[:, d, :], ALU.mult).then_inc(h_afree, 1)
                v.drain()
                ins = nc.vector.tensor_reduce(hAT[:, d, i * P:(i + 1) * P],
                                              hM.rearrange("p (l t) -> p t l", t=P), AX.X, ALU.add)
            ins.then_inc(h_at, 1)

        def states_dve(v, h, d):
            for n, m in enumerate(WALK[d]):
                src = PS[:, 6 + n // 4, (n % 4) * P:(n % 4 + 1) * P]
                v.drain()
                if n == 0:
                    v.wait_ge(h_st, 2 * h + d + 1)
                    nc.vector.tensor_copy(hS[:, d, 0, :], src)
                else:
                    ins = nc.vector.scalar_tensor_tensor(hS[:, d, n, :], hS[:, d, n - 1, :],
                                                         hT_[:, d, m:m + 1], src, ALU.mult, ALU.add)
            ins.then_inc(h_S, 1)

        def head_dve(v, h, par, more):
            v.wait_ge(h_sl, h + 1)
            nc.vector.scalar_tensor_tensor(hsq, hg[:, par, :], 0.0, hsq, ALU.min, ALU.subtract).then_inc(h_sm, 1)
            v.wait_ge(h_sg, h + 1)
            nc.vector.tensor_tensor(hg[:, par, :], hg[:, par, :], hsq, ALU.mult).then_inc(h_gm, 1)
            prep_dve(v, h, par, 0)
            levels_dve(v, h, par, 0)
            prep_dve(v, h, par, 1)
            if more:
                conv_dve(v, h + 1)
            scores_dve(v, h, 0)
            states_dve(v, h, 0)
            levels_dve(v, h, par, 1)
            scores_dve(v, h, 1)
            states_dve(v, h, 1)
            v.wait_ge(h_r, h + 2)
            gn = V[:, bass.ds(V_HG + h, 1)]
            nc.vector.scalar_tensor_tensor(ho, ho, gn, hr, ALU.mult, ALU.mult)
            v.drain()
            dst = OA[:, h, :] if isinstance(h, int) else OA[:, bass.ds(h, 1), :].rearrange("p a b -> p (a b)")
            nc.vector.tensor_tensor(dst, ho, hg[:, par, :], ALU.mult).then_inc(h_out, 1)

        def hgrn_dve(v):
            v.wait_ge(in_cst2, 16)
            first(v, h_kout)
            first(v, h_out)
            conv_dve(v, 0)
            v.wait_ge(evac_done, G_HG + HGG)
            v.drain().then_inc(h_afree, 2)
            with v.Fori(0, 3) as i:
                head_dve(v, 2 * i, 0, True)
                head_dve(v, 2 * i + 1, 1, True)
            head_dve(v, 6, 0, True)
            head_dve(v, 7, 1, False)

        A_CST = area(10240, 2, T)
        qT = area(11264, KT, T)
        KP = area(15360, 4, 2, TA)
        VKV = area(21504, NA, 256)
        Pb = area(23040, 2, TA)
        PT = area(24576, 2, 6, T)
        qs = area(30720, 1, T)
        vs = area(31232, NA, 64)
        qk_k = area(23040, 2, T)
        qk_c = area(24064, T)
        qk_sq = area(24576, 2, T)
        qk_r = area(25600, 2, T)
        qk_t = area(26624, T)
        items = [qT[:, j, :] for j in range(8)] + [qk_k[:, 0, :], qk_k[:, 1, :], qk_c]
        NI = len(items)
        q_sq, q_ss, q_r, q_n, q_rot, q_done, kp_ok = (sem(n) for n in
            ("q_sq", "q_ss", "q_r", "q_n", "q_rot", "q_done", "kp_ok"))

        def qkv_pe(pe):
            pe.wait_ge(h_out, HG + 1)
            for j in range(14):
                g, su = G_QKV + j, U_QKV + 2 * min(j // 4, 2)
                if j < 10:
                    gemm(pe, g, g, su, 0, ((j % 4) * P,), hT)
                elif j == 10:
                    bank_wait(pe, g)
                    for t in range(2):
                        for k in range(KT):
                            w = ring[slot(su + k // 4)]
                            c0 = (k % 4) * 512 + P * t
                            mm(PS[:, g % 2, t * TC:(t + 1) * TC], w[:, c0:c0 + P], HC[:, k, :],
                               k == 0, k == KT - 1, mm_done if t == 1 and k == KT - 1 else None)
                else:
                    tok, t0 = (hT, (j - 11) * 2 * P) if j < 13 else (HC, 0)
                    gemm_tok(pe, g, g, su, tok, (t0, t0 + P), 256, 256)
                if j in (3, 7, 13):
                    pend[0] += 2
                n = j - 1
                if 0 <= n < NI:
                    pe.wait_ge(q_sq, n + 1)
                    if n >= 2:
                        pe.wait_ge(q_r, n - 1)
                    mm(PS[:, 4 + n % 2, :], C[:, C_BLK:C_BLK + P], qk_sq[:, n % 2, :], True, True, q_ss)
                n = j - 2
                if 0 <= n < NI - 1:
                    pe.wait_ge(q_n, n + 1)
                    if n >= 2:
                        pe.wait_ge(q_done, n - 1)
                    mm(PS[:, 6 + n % 2, :], C[:, C_ROT1:C_ROT1 + P], items[n], True, True, q_rot)
            flush(pe)

        def qkv_act(act):
            act.wait_ge(h_out, HG + 1)
            for j in range(14):
                g = G_QKV + j
                if j < NI:
                    evac(act, g, g, items[j])
                    act.drain()
                    if j >= 2:
                        act.wait_ge(q_ss, j - 1)
                    nc.scalar.activation(qk_sq[:, j % 2, :], items[j], ACT.Square).then_inc(q_sq, 1)
                else:
                    m = 2 * (j - 11)
                    evac(act, g, g, VKV[:, m:m + 2, :], w=256)
                n = j - 1
                if 0 <= n < NI:
                    act.wait_ge(q_ss, n + 1)
                    if n >= 2:
                        act.wait_ge(q_n, n - 1)
                    r = qk_r[:, n % 2, :]
                    nc.scalar.activation(r, PS[:, 4 + n % 2, :], ACT.Ln, bias=epsb, scale=1.0 / 64)
                    act.drain()
                    nc.scalar.activation(r, r, ACT.Exp, scale=-0.5).then_inc(q_r, 1)

        def rotate_dve(v, x, rot, tmp, cos, sin, done):
            nc.vector.tensor_tensor(tmp, rot, sin, ALU.mult)
            nc.vector.tensor_tensor(x, x, cos, ALU.mult)
            v.drain()
            nc.vector.tensor_tensor(x, x, tmp, ALU.add).then_inc(done, 1)

        def qkv_dve(v):
            v.drain()
            v.wait_ge(in_acst, 16)
            nc.vector.memset(KP[:, :, :, :], 0.0)
            for n in range(NI):
                v.wait_ge(q_r, n + 1)
                gn = V_QN if n < 8 else V_KN
                nc.vector.scalar_tensor_tensor(items[n], items[n], V[:, gn:gn + 1], qk_r[:, n % 2, :],
                                               ALU.mult, ALU.mult).then_inc(q_n, 1)
                v.drain()
                if n < NI - 1:
                    v.wait_ge(q_rot, n + 1)
                    rotate_dve(v, items[n], PS[:, 6 + n % 2, :], qk_t, A_CST[:, 0, :], A_CST[:, 1, :], q_done)
                v.drain()
            for g in range(4):
                r0 = (g % 2) * 64
                for e in range(2):
                    dst = slice(64 * e, 64 * e + 64)
                    nc.vector.tensor_copy(KP[dst, g, e, 0:T], qk_k[r0:r0 + 64, g // 2, :])
                    ins = nc.vector.tensor_copy(KP[dst, g, e, T:TA],
                                                qk_c[r0:r0 + 64, (g // 2) * TC:(g // 2 + 1) * TC])
            ins.then_inc(kp_ok, 1)

        def attention(name, E, keys, loads, score, value, store, scale, Pb, PT, bias=None, sink=None):
            a_ld, a_s, a_m, a_e, a_p, a_t, a_te, a_pv, a_oe = (sem(f"{name}_{x}") for x in
                ("ld", "s", "m", "e", "p", "t", "te", "pv", "oe"))
            NB = E * NT
            S2 = [PS[:, 2 * i:2 * i + 2, :].rearrange("p a b -> p (a b)") for i in range(2)]
            TB = PS[:, 4:6, :].rearrange("p a b -> p (a b)")
            per_out = E // 2

            def pe_(pe):
                pe.drain().then_inc(a_t, 2)
                pe.drain().then_inc(a_pv, 2)
                with pe.Fori(0, 4) as it:
                    def scores(b):
                        n = NB * it + b
                        pe.wait_ge(a_e, n + 1)
                        score(pe, it, b // NT, b % NT, S2[b % 2]).then_inc(a_s, 1)
                    pe.wait_ge(a_ld, it + 1)
                    def values(e):
                        pe.wait_ge(a_te, NB * it + NT * e + NT + 1)
                        if e % per_out == 0:
                            pe.wait_ge(a_oe, 2 * it + e // per_out + 1)
                        value(pe, it, e).then_inc(a_pv, 1)

                    scores(0)
                    scores(1)
                    for b in range(NB):
                        e, qb = b // NT, b % NT
                        if b + 2 < NB:
                            scores(b + 2)
                        pe.wait_ge(a_te, NB * it + b + 1)
                        pe.wait_ge(a_p, NB * it + b + 1)
                        nk = keys(qb)[1]
                        for t in range(nk):
                            ins = nc.tensor.transpose(TB[:, t * P:(t + 1) * P],
                                                      Pb[:, b % 2, t * P:(t + 1) * P], ident)
                        ins.then_inc(a_t, 1)
                        if qb == 0 and e > 0:
                            values(e - 1)
                    values(E - 1)

            def act_(act):
                act.drain().then_inc(a_e, 2)
                act.drain().then_inc(a_oe, 2)
                first(act, a_te)
                with act.Fori(0, 4) as it:
                    def transposed(b):
                        e, qb = b // NT, b % NT
                        if qb == 0:
                            act.wait_ge(a_pv, E * it + e + 1)
                        act.wait_ge(a_t, NB * it + b + 3)
                        nk = keys(qb)[1]
                        nc.scalar.activation(PT[:, e % 2, 0:nk, qb * P:(qb + 1) * P],
                                             TB[:, 0:nk * P].rearrange("p (a b) -> p a b", b=P),
                                             ACT.Copy).then_inc(a_te, 1)

                    def output(e):
                        act.wait_ge(a_pv, E * it + e + 3)
                        apart(act)
                        nc.scalar.activation(store(it, e), PS[:, 6 + e // per_out, :], ACT.Copy)\
                            .then_inc(a_oe, 1)

                    act.wait_ge(a_pv, E * it + 2)
                    apart(act)
                    for i, (dst, src) in enumerate(loads(it)):
                        ins = nc.scalar.activation(dst, src, ACT.Copy)
                    ins.then_inc(a_ld, 1)
                    for b in range(NB):
                        n = NB * it + b
                        w = keys(b % NT)[1] * P
                        act.wait_ge(a_t, n + 1)
                        act.wait_ge(a_m, n + 1)
                        nm = st8[:, 2 + b % 2:3 + b % 2]
                        if sink is not None:
                            apart(act)
                            nc.scalar.activation(st8[:, 8 + b % 2:9 + b % 2], sink(it, b // NT), ACT.Exp, bias=nm)
                        nc.scalar.activation(Pb[:, b % 2, 0:w], S2[b % 2][:, 0:w], ACT.Exp, bias=nm,
                                             scale=scale, accum_out=st8[:, 4 + b % 2:5 + b % 2]).then_inc(a_e, 1)
                        if b >= 1:
                            transposed(b - 1)
                        if b >= 2 and (b - 2) % NT == NT - 1 and ((b - 2) // NT + 1) % per_out == 0:
                            output((b - 2) // NT)
                    transposed(NB - 1)
                    output(E - 1)

            def dve_(v):
                with v.Fori(0, 4) as it:
                    def maximum(b):
                        n = NB * it + b
                        w = keys(b % NT)[1] * P
                        v.drain()
                        v.wait_ge(a_s, n + 1)
                        if bias is not None:
                            bias(it, b // NT, b % NT, S2[b % 2])
                            v.drain()
                        nc.vector.tensor_reduce(st8[:, b % 2:b % 2 + 1], S2[b % 2][:, 0:w], AX.X, ALU.max)
                        v.drain()
                        mx, nm = st8[:, b % 2:b % 2 + 1], st8[:, 2 + b % 2:3 + b % 2]
                        if sink is None:
                            nc.vector.tensor_scalar(nm, mx, -scale, None, ALU.mult).then_inc(a_m, 1)
                        else:
                            nc.vector.tensor_scalar(nm, mx, -scale, nsink(it, b // NT), ALU.mult, ALU.min)\
                                .then_inc(a_m, 1)

                    def normalise(b):
                        w = keys(b % NT)[1] * P
                        v.wait_ge(a_e, NB * it + b + 3)
                        s, r = st8[:, 4 + b % 2:5 + b % 2], st8[:, 6 + b % 2:7 + b % 2]
                        if sink is not None:
                            nc.vector.tensor_tensor(s, s, st8[:, 8 + b % 2:9 + b % 2], ALU.add)
                            v.drain()
                        nc.vector.reciprocal(r, s)
                        v.drain()
                        nc.vector.tensor_scalar(Pb[:, b % 2, 0:w], Pb[:, b % 2, 0:w], r, None, ALU.mult)\
                            .then_inc(a_p, 1)

                    maximum(0)
                    maximum(1)
                    for b in range(NB):
                        normalise(b)
                        if b + 2 < NB:
                            maximum(b + 2)

            return pe_, act_, dve_, a_oe

        def tile_of(a, i):
            return a[:, bass.ds(i, 1), :].rearrange("p a b -> p (a b)")

        qs4 = [qs[:, 0, :], rstd[:, :]]

        def gqa_score(pe, it, e, qb, S):
            q = qs4[e // 2][:, qb * P:(qb + 1) * P]
            kp = KP[:, bass.ds(it, 1), e % 2, :].rearrange("p a b -> p (a b)")
            nc.tensor.matmul(S[:, 0:512], q, kp[:, 0:512], start=True, stop=True)
            return nc.tensor.matmul(S[:, 512:TA], q, kp[:, 512:TA], start=True, stop=True)

        def gqa_value(pe, it, e):
            o = PS[64 * (e % 2):64 * (e % 2) + 64, 6 + e // 2, :]
            for t in range(NA):
                ins = nc.tensor.matmul(o, vs[:, t, :], PT[:, e % 2, t, :], start=t == 0, stop=t == NA - 1)
            return ins

        gqa_pe, gqa_act, gqa_dve, gqa_oe = attention(
            "gqa", 4, lambda qb: (0, NA),
            lambda it: [(qs4[0], tile_of(qT, 2 * it)), (qs4[1], tile_of(qT, 2 * it + 1)),
                        (vs, VKV[:, :, bass.ds(64 * it, 64)])],
            gqa_score, gqa_value, lambda it, e: tile_of(qT, 2 * it + e // 2), 0.125, Pb, PT)

        gt = area(15360, 4, T)
        y = area(17408, KT, T)
        ytmp = area(21504, T)
        y_ok = sem("y_ok")
        OC = qT

        def merge_pe(pe):
            pe.wait_ge(gqa_oe, 2 + 8)
            with pe.Fori(0, 2) as n:
                for b, o in enumerate((OA, OB, OC)):
                    for w, rhs in enumerate((hT, o)):
                        g, u = 24 * n + 8 * b + 4 * w, 4 * b + 2 * w
                        gemm(pe, G_MERGE + g, G_MERGE, U_MERGE + u, 3 * n, (0, 128, 256, 384), rhs)
                        pend[0] += 2
                flush(pe)

        def merge_act(act):
            with act.Fori(0, 2) as n:
                for b in range(3):
                    for t in range(4):
                        act.wait_ge(pt_used, 12 * n + 4 * b + (t - 1 if b else max(t - 1, 1)))
                        evac(act, G_MERGE + 24 * n + 8 * b + t, t, gt[:, t, :], func=ACT.Sigmoid)
                    for t in range(4):
                        act.wait_ge(pt_used, 12 * n + 4 * b + t + 1)
                        evac(act, G_MERGE + 24 * n + 8 * b + 4 + t, t, pt[:, t % 2, :])

        def merge_dve(v):
            v.drain().then_inc(pt_used, 2)
            with v.Fori(0, 2) as n:
                for b in range(3):
                    for t in range(4):
                        v.drain()
                        v.wait_ge(evac_done, G_MERGE + 24 * n + 8 * b + 4 + t + 1)
                        dst = tile_of(y, 4 * n + t)
                        if b == 0:
                            nc.vector.tensor_tensor(dst, pt[:, t % 2, :], gt[:, t, :], ALU.mult)\
                                .then_inc(pt_used, 1)
                        else:
                            nc.vector.tensor_tensor(ytmp, pt[:, t % 2, :], gt[:, t, :], ALU.mult)\
                                .then_inc(pt_used, 1)
                            v.drain()
                            nc.vector.tensor_tensor(dst, dst, ytmp, ALU.add)
                v.drain().then_inc(y_ok, 1)

        def residual_pe(pe, g, su, rhs):
            for c in range(2):
                gemm(pe, g + 4 * c, g, su + 2 * c, 0, (0, 128, 256, 384), rhs)
                pend[0] += 2
            flush(pe)

        def residual_act(act, g, r, bias=None):
            for j in range(KT):
                act.wait_ge(pt_used, r + j + 1)
                if bias is None:
                    evac(act, g + j, g + j, pt[:, (r + j) % 2, :])
                else:
                    evac(act, g + j, g + j, pt[:, (r + j) % 2, :], func=ACT.Identity,
                         bias=V[:, bias + j:bias + j + 1])

        def residual_dve(v, g, r, gate):
            for j in range(KT):
                v.wait_ge(evac_done, g + j + 1)
                nc.vector.scalar_tensor_tensor(xT[:, j, :], pt[:, (r + j) % 2, :], gate(j), xT[:, j, :],
                                               ALU.mult, ALU.add).then_inc(pt_used, 1)
            v.drain().then_inc(x_ok, 1)

        h2 = area(0, NT, D)
        Pm = area(4096, NT, NE * CAP)
        PTm = area(8192, NPAIR, T)
        acc = area(12288, KT, T)
        xs = area(16384, KT, P)
        hid = area(17408, FF)
        hidT = area(18432, FF // P, P)
        ys = area(19456, D)
        sg = area(20480, 2, 512)
        iota_s = area(21504, T)
        aff = area(22016, NT, NE)
        affT = area(22080, 2, T)
        vals = area(23104, CAP)
        idxf = area(23232, CAP)
        blk = area(23296, NE, CAP)
        idxc = area(24320, NPAIR)
        wsel = area(24328, NPAIR)
        rw = area(24336, KT, NE)
        mx4 = area(24464, NT)
        sm4 = area(24468, NT)
        rs4 = area(24472, NT)
        idxu = sb("idxu", [NE, CAP], u32)
        in_router, r_lg, r_mx, r_ex, r_aff, r_affT, r_top, r_tt, r_blk, r_row, r_ok = (sem(n) for n in
            ("in_router", "r_lg", "r_mx", "r_ex", "r_aff", "r_affT", "r_top", "r_tt", "r_blk", "r_row", "r_ok"))
        e_g, e_xs, e_gu, e_sg, e_hid, e_T, e_hT, e_dn, e_ys, e_cb, e_acc = (sem(n) for n in
            ("e_g", "e_xs", "e_gu", "e_sg", "e_hid", "e_T", "e_hT", "e_dn", "e_ys", "e_cb", "e_acc"))

        def route_pe(pe):
            pe.wait_ge(n_h, NH[3])
            pe.wait_ge(in_router, 16)
            for m in range(NT):
                for k in range(KT):
                    ins = nc.tensor.matmul(PS[:, 6, m * NE:(m + 1) * NE], hT[:, k, m * P:(m + 1) * P],
                                           rw[:, k, :], start=k == 0, stop=k == KT - 1)
            ins.then_inc(r_lg, 1)
            for i in range(8):
                g = G_H2T + i
                bank_wait(pe, g)
                for k in range(4):
                    kk = 4 * (i % 2) + k
                    ins = nc.tensor.transpose(PS[:, g % 2, k * P:(k + 1) * P],
                                              hT[:, kk, (i // 2) * P:(i // 2 + 1) * P], ident)
                ins.then_inc(mm_done, 1)
            pe.wait_ge(r_aff, 1)
            for m in range(NT):
                ins = nc.tensor.transpose(PS[0:NE, 7, m * P:(m + 1) * P], aff[:, m, :], ident)
            ins.then_inc(r_affT, 1)
            pe.wait_ge(r_top, 1)
            nc.tensor.transpose(PS[0:CAP, 6, 0:NE], vals[0:NE, :], C[0:NE, C_ID:C_ID + NE])
            nc.tensor.transpose(PS[0:CAP, 6, NE:2 * NE], idxf[0:NE, :], C[0:NE, C_ID:C_ID + NE]).then_inc(r_tt, 1)
            pe.wait_ge(r_blk, 1)
            for c in range(2):
                ins = nc.tensor.matmul(PS[:, 4 + c, :], C[0:NE, C_ONE:C_ONE + P],
                                       blk[0:NE, 8 * c:8 * c + 8, :].rearrange("p a b -> p (a b)"),
                                       start=True, stop=True)
            ins.then_inc(r_row, 1)

        def route_act(act):
            act.wait_ge(r_mx, 1)
            for m in range(NT):
                ins = nc.scalar.activation(aff[:, m, :], PS[:, 6, m * NE:(m + 1) * NE], ACT.Exp,
                                           bias=mx4[:, m:m + 1], accum_out=sm4[:, m:m + 1])
            ins.then_inc(r_ex, 1)
            for i in range(8):
                g = G_H2T + i
                evac(act, g, g, h2[:, i // 2, (i % 2) * 512:(i % 2 + 1) * 512])

        def route_dve(v):
            v.wait_ge(r_lg, 1)
            nc.vector.tensor_reduce(mx4, PS[:, 6, 0:NT * NE].rearrange("p (m e) -> p m e", e=NE),
                                    AX.X, ALU.max, negate=True).then_inc(r_mx, 1)
            nc.vector.memset(acc[:, :, :], 0.0)
            v.wait_ge(r_ex, 1)
            nc.vector.reciprocal(rs4, sm4)
            v.drain()
            for m in range(NT):
                ins = nc.vector.tensor_scalar(aff[:, m, :], aff[:, m, :], rs4[:, m:m + 1], None, ALU.mult)
            ins.then_inc(r_aff, 1)
            v.wait_ge(r_affT, 1)
            nc.vector.tensor_copy(affT[0:NE, 0, :], PS[0:NE, 7, :])
            for r in range(CAP // 8):
                cur, nxt, top = affT[0:NE, r % 2, :], affT[0:NE, 1 - r % 2, :], vals[0:NE, 8 * r:8 * r + 8]
                v.drain()
                nc.vector.max(top, cur)
                v.drain()
                nc.vector.max_index(idxu[:, 8 * r:8 * r + 8], top, cur)
                if r < CAP // 8 - 1:
                    nc.vector.match_replace(nxt, top, cur, -1.0)
            v.drain()
            nc.vector.tensor_copy(idxf[0:NE, :], idxu[:, :])
            v.drain().then_inc(r_top, 1)
            nc.vector.tensor_tensor(blk[0:NE, :, :], idxf[0:NE, :].unsqueeze(1).broadcast_to([NE, NE, CAP]),
                                    C[0:NE, C_ID:C_ID + NE].unsqueeze(2).broadcast_to([NE, NE, CAP]),
                                    ALU.mult).then_inc(r_blk, 1)
            v.wait_ge(r_tt, 1)
            for e in range(2):
                dst = slice(CAP * e, CAP * e + CAP)
                nc.vector.tensor_copy(wsel[dst, :], PS[0:CAP, 6, e:NE:2])
                nc.vector.tensor_copy(idxc[dst, :], PS[0:CAP, 6, NE + e:2 * NE:2])
            v.drain()
            v.wait_ge(in_iota, 16)
            for p in range(NPAIR):
                nc.vector.tensor_scalar(PTm[:, p, :], iota_s, idxc[:, p:p + 1], None, ALU.is_equal)
            v.wait_ge(r_row, 1)
            for m in range(NT):
                nc.vector.tensor_scalar(Pm[:, m, :], PS[:, 4:6, :].rearrange("p a b -> p (a b)"),
                                        C[:, C_PART + m:C_PART + m + 1], None, ALU.is_equal)
            v.drain().then_inc(r_ok, 1)
            v.drain().then_inc(e_acc, 2)

        def pair_product(pe, p, j, x_, bank, done):
            for kg in range(2):
                for e in range(2):
                    unit_wait(pe, U_EXP + 4 * j + 2 * kg + e, 3 * p)
                for kk in range(4):
                    k = 4 * kg + kk
                    for e in range(2):
                        w = ring[slot(U_EXP + 4 * j + 2 * kg + e)][:, kk * 512:(kk + 1) * 512]
                        mm(PS[64 * e:64 * e + 64, bank, :], x_[:, k, 64 * e:64 * e + 64], w,
                           k == 0, k == KT - 1, done if k == KT - 1 and e == 1 else None)
                pend[0] += 2

        def experts_pe(pe):
            pe.wait_ge(r_ok, 1)
            pe.wait_ge(evac_done, G_H2T + 8)
            first(pe, e_cb)
            with pe.Fori(0, NPAIR) as p:
                pe.wait_ge(e_hT, p + 1)
                for k in range(KT):
                    for m in range(NT):
                        mm(PS[:, 4 + k // 4, (k % 4) * P:(k % 4 + 1) * P], h2[:, m, k * P:(k + 1) * P],
                           Pm[:, m, bass.ds(P * p, P)], m == 0, m == NT - 1,
                           e_g if k == KT - 1 and m == NT - 1 else None)
                pe.wait_ge(e_xs, p + 1)
                pe.wait_ge(e_ys, 2 * p + 1)
                for c in range(2):
                    pair_product(pe, p, 2 * c, xs, 2 * c, e_gu)
                    pair_product(pe, p, 2 * c + 1, xs, 2 * c + 1, e_gu)
                for j in range(KT):
                    if j % 4 == 0:
                        pe.wait_ge(e_hid, 2 * p + j // 4 + 1)
                    ins = nc.tensor.transpose(PS[:, 4 + j // 4, (j % 4) * P:(j % 4 + 1) * P],
                                              hid[:, j * P:(j + 1) * P], ident)
                ins.then_inc(e_T, 1)
                pe.wait_ge(e_hT, p + 2)
                for c in range(2):
                    pair_product(pe, p, 4 + c, hidT, c, e_dn)
                for k in range(KT):
                    if k % 4 == 0:
                        pe.wait_ge(e_ys, 2 * p + k // 4 + 2)
                    pe.wait_ge(e_acc, 8 * p + k + 1)
                    mm(PS[:, 6 + k % 2, :], ys[:, k * P:(k + 1) * P], tile_of(PTm, p), True, True, e_cb)
                flush(pe)

        def experts_act(act):
            first(act, e_hT)
            first(act, e_ys)
            with act.Fori(0, NPAIR) as p:
                two = PS[:, 4:6, :].rearrange("p a b -> p (a b)")
                act.wait_ge(e_g, p + 1)
                nc.scalar.activation(xs.rearrange("p a b -> p (a b)"), two, ACT.Copy).then_inc(e_xs, 1)
                for c in range(2):
                    act.wait_ge(e_gu, 4 * p + 2 * c + 1)
                    nc.scalar.activation(sg[:, c, :], PS[:, 2 * c, :], ACT.Silu).then_inc(e_sg, 1)
                act.wait_ge(e_T, p + 1)
                nc.scalar.activation(hidT.rearrange("p a b -> p (a b)"), two, ACT.Copy).then_inc(e_hT, 1)
                for c in range(2):
                    act.wait_ge(e_cb, 8 * p + 1)
                    act.wait_ge(e_dn, 2 * p + c + 1)
                    apart(act)
                    nc.scalar.activation(ys[:, c * 512:(c + 1) * 512], PS[:, c, :], ACT.Copy,
                                         scale=wsel[:, bass.ds(p, 1)]).then_inc(e_ys, 1)

        def experts_dve(v):
            with v.Fori(0, NPAIR) as p:
                for c in range(2):
                    v.wait_ge(e_gu, 4 * p + 2 * c + 2)
                    v.wait_ge(e_sg, 2 * p + c + 1)
                    nc.vector.tensor_tensor(hid[:, c * 512:(c + 1) * 512], sg[:, c, :], PS[:, 2 * c + 1, :],
                                            ALU.mult).then_inc(e_hid, 1)
                v.drain()
                for k in range(KT):
                    v.wait_ge(e_cb, 8 * p + k + 2)
                    nc.vector.tensor_tensor(acc[:, k, :], acc[:, k, :], PS[:, 6 + k % 2, :], ALU.add)\
                        .then_inc(e_acc, 1)
                v.drain()
            for k in range(KT):
                ins = nc.vector.scalar_tensor_tensor(xT[:, k, :], acc[:, k, :], mod[:, 40 + k:41 + k],
                                                     xT[:, k, :], ALU.mult, ALU.add)
            ins.then_inc(x_ok, 1)

        cq = area(0, QT, T)
        ckv = area(1536, KVT, T)
        kr = area(2560, T)
        down = area(0, 6, T)
        krp = area(3072, 2, T)
        qn = area(4096, KT, T)
        qr = area(8192, 4, T)
        up = area(4096, 12, T)
        kn = area(10240, KT, T)
        vt = area(14336, NT, D)
        sqb = area(18432, QT, T)
        cs2 = area(19968, 2, T)
        ang = area(20992, 2, T)
        Pb2 = area(22016, 2, TA)
        PT2 = area(23552, 2, 6, T)
        qs2 = area(29696, 3, T)
        vs2 = area(31232, 2, NT, P)
        rt2 = area(22016, T)
        posi = area(21504, T).bitcast(i32)
        in_pos, t_ang, t_cs, r2_rot, r2_done, krp_ok = (sem(n) for n in
            ("in_pos", "t_ang", "t_cs", "r2_rot", "r2_done", "krp_ok"))

        def angles_dve(v):
            two_pi = 2 * np.pi
            c1 = 6.28125
            c2 = float(np.round((two_pi - c1) * 2.0 ** 21) / 2.0 ** 21)
            c3 = float(np.float32(two_pi - c1 - c2))
            magic = 1.5 * 2.0 ** 23
            a, w = ang[:, 0, :], ang[:, 1, :]
            v.wait_ge(in_pos, 16)
            v.wait_ge(x_ok, 2)
            nc.vector.tensor_copy(a, posi)
            v.drain()
            nc.vector.tensor_scalar(a, a, C[:, C_INV:C_INV + 1], None, ALU.mult)
            for i, (shift, turn) in enumerate(((np.pi / 2, 0.25), (0.0, 0.0))):
                t = cs2[:, i, :]
                v.drain()
                nc.vector.tensor_scalar(w, a, 1.0 / two_pi, turn, ALU.mult, ALU.add)
                v.drain()
                nc.vector.tensor_scalar(w, w, magic, None, ALU.add)
                v.drain()
                nc.vector.tensor_scalar(w, w, magic, None, ALU.subtract)
                v.drain()
                nc.vector.scalar_tensor_tensor(t, w, -c1, a, ALU.mult, ALU.add)
                v.drain()
                nc.vector.scalar_tensor_tensor(t, w, -c2, t, ALU.mult, ALU.add)
                v.drain()
                nc.vector.scalar_tensor_tensor(t, w, -c3, t, ALU.mult, ALU.add)
                v.drain()
                nc.vector.tensor_scalar(t, t, float(shift), 3.1415925, ALU.add, ALU.min)
                v.drain()
                nc.vector.tensor_scalar(t, t, -3.1415925, None, ALU.max)
            v.drain().then_inc(t_ang, 1)

        def angles_act(act):
            act.wait_ge(t_ang, 1)
            nc.scalar.activation(cs2[:, :, :], cs2[:, :, :], ACT.Sin).then_inc(t_cs, 1)

        def mla_pe(pe):
            pe.wait_ge(n_h, NH[5])
            gemm(pe, G_MD, G_MD, U_MD, 0, (0, 128, 256, 384), hT)
            pend[0] += 2
            gemm(pe, G_MD + 4, G_MD + 4, U_MD + 2, 0, (0, 128), hT)
            pend[0] += 2
            flush(pe)
            norm_pe(pe, 5, sqb, kt=QT)
            norm_pe(pe, 6, sqb, kt=KVT)
            pe.wait_ge(n_h, NH[6])
            for c in range(3):
                gemm(pe, G_MUQ + 4 * c, G_MUQ, U_MUQ + c, 0, (0, 128, 256, 384), cq, kt=QT)
                pend[0] += 1
            pe.wait_ge(n_h, NH[7])
            gemm(pe, G_MUKV, G_MUKV, U_MUKV, 0, range(0, D, P), ckv, kt=KVT, cols=1024)
            pend[0] += 1
            unit_wait(pe, U_MUKV + 1)
            for m in range(NT):
                for c in range(2):
                    g = G_MUKV + 8 + 2 * m + c
                    gemm_tok(pe, g, g, U_MUKV + 1, ckv, (m * P,), c * 512, 512, kt=KVT, cols=1024)
            pend[0] += 1
            flush(pe)
            for n in range(5):
                x = qr[:, n, :] if n < 4 else kr
                if n >= 2:
                    pe.wait_ge(r2_done, n - 1)
                nc.tensor.matmul(PS[:, 4 + n % 2, :], C[:, C_ROT2:C_ROT2 + P], x, start=True, stop=True)\
                    .then_inc(r2_rot, 1)

        def mla_act(act):
            for j in range(6):
                evac(act, G_MD + j, G_MD + j, down[:, j, :])
            act.drain()
            norm_act(act, 5, cq, sqb, kt=QT)
            act.wait_ge(n_h, NH[6])
            norm_act(act, 6, ckv, sqb, kt=KVT)
            for j in range(12):
                evac(act, G_MUQ + j, G_MUQ + j, up[:, j, :])
            for j in range(8):
                evac(act, G_MUKV + j, G_MUKV + j, kn[:, j, :])
            for j in range(8):
                evac(act, G_MUKV + 8 + j, G_MUKV + 8 + j, vt[:, j // 2, (j % 2) * 512:(j % 2 + 1) * 512])

        def mla_dve(v):
            norm_dve(v, 5, cq, cq, lambda k: V[:, V_GQ + k:V_GQ + k + 1], kt=QT)
            norm_dve(v, 6, ckv, ckv, lambda k: V[:, V_GKV + k:V_GKV + k + 1], kt=KVT)
            nc.vector.memset(krp[:, :, :], 0.0)
            v.wait_ge(t_cs, 1)
            for n in range(5):
                x = qr[:, n, :] if n < 4 else kr
                v.drain()
                v.wait_ge(r2_rot, n + 1)
                rotate_dve(v, x, PS[:, 4 + n % 2, :], rt2, cs2[:, 0, :], cs2[:, 1, :], r2_done)
            v.drain()
            for e in range(2):
                half = slice(64 * e, 64 * e + 64)
                nc.vector.tensor_copy(krp[half, e, :], kr[half, :])
            v.drain().then_inc(krp_ok, 1)

        def mla_score(pe, it, e, qb, S):
            w = (qb + 1) * P
            q = slice(qb * P, (qb + 1) * P)
            nc.tensor.matmul(S[:, 0:w], qs2[:, e, q], tile_of(kn, 2 * it + e)[:, 0:w], start=True, stop=False)
            return nc.tensor.matmul(S[:, 0:w], qs2[:, 2, q], krp[:, e, 0:w], start=False, stop=True)

        def mla_bias(it, e, qb, S):
            d = S[:, qb * P:(qb + 1) * P]
            nc.vector.tensor_tensor(d, d, C[:, C_CAUS:C_CAUS + P], ALU.add)

        def mla_value(pe, it, e):
            for t in range(NT):
                ins = nc.tensor.matmul(PS[:, 6 + e, t * P:T], vs2[:, e, t, :], PT2[:, e, t, t * P:T],
                                       start=t == 0, stop=t == NT - 1)
            return ins

        mla_att_pe, mla_att_act, mla_att_dve, mla_oe = attention(
            "mla", 2, lambda qb: (0, qb + 1),
            lambda it: [(qs2[:, 0, :], tile_of(qn, 2 * it)), (qs2[:, 1, :], tile_of(qn, 2 * it + 1)),
                        (qs2[:, 2, :], tile_of(qr, it)),
                        (vs2[:, 0, :, :], vt[:, :, bass.ds(256 * it, P)]),
                        (vs2[:, 1, :, :], vt[:, :, bass.ds(256 * it + P, P)])],
            mla_score, mla_value, lambda it, e: tile_of(qn, 2 * it + e), float((NOPE + ROPE_D) ** -0.5),
            Pb2, PT2, bias=mla_bias)

        fh = area(0, FT, T)
        f_h, f_mm, f_x = (sem(n) for n in ("f_h", "f_mm", "f_x"))

        def ff_pe(pe, L, use):
            pe.wait_ge(n_h, NH[use + 1])
            g0 = (G_FF0, G_FF1)[L]
            with pe.Fori(0, 4) as i:
                for c in range(2):
                    gemm(pe, g0 + 8 * i + 4 * c, g0, U_FF[L] + 2 * c, i, (0, 128, 256, 384), hT)
                    pend[0] += 2
                flush(pe)
            pe.wait_ge(f_h, FT * (L + 1))
            with pe.Fori(0, 2) as n:
                pe.wait_ge(f_x, 8 * L + 4 * n + 1)
                for kc in range(4):
                    for j in range(4):
                        for k in range(KT):
                            su = U_FF[L] + 16 + 2 * kc + k // 4
                            if j == 0 and k % 4 == 0:
                                unit_wait(pe, su, 2 * n)
                            c0 = (k % 4) * 512 + j * P
                            last = kc == 3 and k == KT - 1
                            mm(PS[:, 4 + j, :], ring[slot(su)][:, c0:c0 + P], fh[:, 8 * kc + k, :],
                               kc == 0 and k == 0, last, f_mm if last else None, skip_group_check=True)
                    pend[0] += 2
                flush(pe)

        def ff_act(act, L):
            g0 = (G_FF0, G_FF1)[L]
            with act.Fori(0, 4) as i:
                for j in range(8):
                    act.wait_ge(mm_done, g0 + 8 * i + j + 1)
                    apart(act)
                    nc.scalar.activation(tile_of(fh, 8 * i + j), PS[:, (g0 + j) % 2, :], ACT.Relu)\
                        .then_inc(evac_done, 1)

        def ff_dve(v, L):
            if L == 0:
                first(v, f_x)
            g0 = (G_FF0, G_FF1)[L]
            with v.Fori(0, 4) as i:
                for j in range(8):
                    t = tile_of(fh, 8 * i + j)
                    v.wait_ge(evac_done, g0 + 8 * i + j + 1)
                    nc.vector.tensor_tensor(t, t, t, ALU.mult).then_inc(f_h, 1)
            with v.Fori(0, 2) as n:
                for j in range(4):
                    v.wait_ge(f_mm, 8 * L + 4 * n + j + 1)
                    gate = mod2[:, bass.ds(48 * L + 40 + j + 4 * n, 1)]
                    t = tile_of(xT, 4 * n + j)
                    nc.vector.scalar_tensor_tensor(t, PS[:, 4 + j, :], gate, t, ALU.mult, ALU.add)\
                        .then_inc(f_x, 1)
            v.drain().then_inc(x_ok, 1)

        KP2 = area(10240, 4, 2, T)
        VK2 = area(14336, NT, 256)
        bvs = area(15360, 256)
        snk = area(15616, 2, 16)
        kl2 = area(22016, 2, T)
        in_swa, v_ok = sem("in_swa"), sem("v_ok")

        def swa_qkv_pe(pe):
            pe.wait_ge(n_h, NH[9])
            for j in range(12):
                g, su = G_SQKV + j, U_SQKV + 2 * min(j // 4, 2)
                if j < 10:
                    gemm(pe, g, g, su, 0, ((j % 4) * P,), hT)
                else:
                    t0 = (j - 10) * 2 * P
                    gemm_tok(pe, g, g, su, hT, (t0, t0 + P), 256, 256)
                if j in (3, 7, 11):
                    pend[0] += 2
            flush(pe)

        def swa_qkv_act(act):
            for j in range(12):
                g = G_SQKV + j
                if j < 10:
                    dst = qn[:, j, :] if j < 8 else kl2[:, j - 8, :]
                    evac(act, g, g, dst, func=ACT.Identity, bias=V[:, V_BQKV + j:V_BQKV + j + 1])
                else:
                    evac(act, g, g, VK2[:, 2 * (j - 10):2 * (j - 10) + 2, :], w=256)

        def swa_qkv_dve(v):
            nc.vector.memset(KP2[:, :, :, :], 0.0)
            v.drain()
            v.wait_ge(evac_done, G_SQKV + 10)
            for g in range(4):
                r0 = (g % 2) * 64
                for e in range(2):
                    nc.vector.tensor_copy(KP2[64 * e:64 * e + 64, g, e, :], kl2[r0:r0 + 64, g // 2, :])
            v.wait_ge(in_swa, 32)
            nc.vector.tensor_scalar(snk[:, 1, :], snk[:, 0, :], -1.0, None, ALU.mult)
            v.wait_ge(evac_done, G_SQKV + 12)
            nc.vector.tensor_tensor(VK2[:, :, :], VK2[:, :, :], bvs.unsqueeze(1).broadcast_to([P, NT, 256]),
                                    ALU.add)
            v.drain().then_inc(v_ok, 1)

        def swa_keys(qb):
            return (max(qb - 1, 0), min(qb + 1, 2))

        qs3, vs3 = area(29696, 2, T), area(31232, NT, 64)

        def swa_score(pe, it, e, qb, S):
            k0, nk = swa_keys(qb)
            kp = KP2[:, bass.ds(it, 1), e % 2, :].rearrange("p a b -> p (a b)")
            return nc.tensor.matmul(S[:, 0:nk * P], qs3[:, e // 2, qb * P:(qb + 1) * P],
                                    kp[:, k0 * P:(k0 + nk) * P], start=True, stop=True)

        def swa_bias(it, e, qb, S):
            nk = swa_keys(qb)[1]
            s = S[:, 0:nk * P]
            nc.vector.scalar_tensor_tensor(s, C[:, C_DIST + (2 - nk) * P:C_DIST + 2 * P],
                                           C[:, bass.ds(C_SLOPE + 4 * it + e, 1)], s, ALU.mult, ALU.add)

        def swa_value(pe, it, e):
            for qb in range(NT):
                k0, nk = swa_keys(qb)
                o = PS[64 * (e % 2):64 * (e % 2) + 64, 6 + e // 2, qb * P:(qb + 1) * P]
                for t in range(nk):
                    ins = nc.tensor.matmul(o, vs3[:, k0 + t, :], PT2[:, e % 2, t, qb * P:(qb + 1) * P],
                                           start=t == 0, stop=t == nk - 1)
            return ins

        def nsink(it, e):
            return snk[:, 1, bass.ds(4 * it + e, 1)]

        swa_att_pe, swa_att_act, swa_att_dve, swa_oe = attention(
            "swa", 4, swa_keys,
            lambda it: [(qs3[:, 0, :], tile_of(qn, 2 * it)), (qs3[:, 1, :], tile_of(qn, 2 * it + 1)),
                        (vs3, VK2[:, :, bass.ds(64 * it, 64)])],
            swa_score, swa_value, lambda it, e: tile_of(qn, 2 * it + e // 2), 0.125, Pb2, PT2,
            bias=swa_bias, sink=lambda it, e: snk[:, 0, bass.ds(4 * it + e, 1)])

        xf = area(0, KT, T)
        otok = area(4096, NT, D)
        out_done = sem("out_done")

        def end_pe(pe):
            norm_pe(pe, 10, hT)
            pe.wait_ge(n_h, NH[11])
            for i in range(8):
                g = G_FIN + i
                bank_wait(pe, g)
                for k in range(4):
                    kk = 4 * (i % 2) + k
                    ins = nc.tensor.transpose(PS[:, g % 2, k * P:(k + 1) * P],
                                              xf[:, kk, (i // 2) * P:(i // 2 + 1) * P], ident)
                ins.then_inc(mm_done, 1)

        def end_act(act):
            norm_act(act, 10, xT, hT, ready=(x_ok, 6))
            for i in range(8):
                g = G_FIN + i
                evac(act, g, g, otok[:, i // 2, (i % 2) * 512:(i % 2 + 1) * 512])

        def end_dve(v):
            norm_dve(v, 10, xT, xf, lambda k: V[:, V_GF + k:V_GF + k + 1])
        block = ctx.enter_context(nc.Block())
        @block.sync
        def _(sp):
            def load(u, used, base=0):
                if used is not None:
                    sp.wait_ge(w_used, base + used)
                src = stream[bass.ds(base + u, 1), :, :].rearrange("a p n -> (a p) n")
                sp.dma_start(ring[slot(u)][:, :], src).then_inc(w_loaded[slot(u)], 16)

            def turns(first_, last, width):
                n = (last - first_) // width
                with sp.Fori(0, n) as turn:
                    for s in range(width):
                        load(first_ + s, first_ + s - width + 1, width * turn)
                for u in range(first_ + n * width, last):
                    load(u, u - width + 1)

            for u in range(SLOTS):
                load(u, None)
            turns(SLOTS, U_EXP, SLOTS)
            for j in range(WIDE):
                load(U_EXP + j, U_EXP + min(j, SLOTS - 1) - SLOTS + 1)
            turns(U_EXP + WIDE, U_MD, WIDE)
            for u in range(U_MD, U_MD + SLOTS):
                load(u, u - WIDE + 1)
            turns(U_MD + SLOTS, N_STREAM, SLOTS)
            for m in range(NT):
                sp.wait_ge(evac_done, G_FIN + 2 * m + 2)
                sp.dma_start(out[m * P:(m + 1) * P, :], otok[:, m, :]).then_inc(out_done, 16)
            sp.wait_ge(out_done, 16 * NT)

        @block.gpsimd
        def _(pool):
            pool.dma_start(C[:, :], cst).then_inc(in_const, 16)
            pool.dma_start(v_rows, vecs).then_inc(in_vec, 16)
            pool.dma_start(x_tok, x.rearrange("(m p) d -> p m d", p=P)).then_inc(in_x, 16)
            pool.dma_start(c_tok, ctxt.rearrange("(m p) d -> p m d", p=P)).then_inc(in_x, 16)
            pool.wait_ge(evac_done, G_X + 2 * KT)
            pool.dma_start(H_CST, hcst).then_inc(in_cst2, 16)
            pool.wait_ge(h_out, HG + 1)
            pool.dma_start(A_CST, acst.rearrange("p (a b) -> p a b", a=2)).then_inc(in_acst, 16)
            pool.wait_ge(y_ok, 2)
            pool.dma_start(iota_s, iota).then_inc(in_iota, 16)
            pool.dma_start(rw, router).then_inc(in_router, 16)
            pool.wait_ge(x_ok, 2)
            pool.dma_start(posi, pos).then_inc(in_pos, 16)
            pool.wait_ge(x_ok, 4)
            pool.dma_start(bvs, bv).then_inc(in_swa, 16)
            pool.dma_start(snk[:, 0, :], sinks).then_inc(in_swa, 16)

        @block.tensor
        def _(pe):
            start_pe(pe)
            start_norm_pe(pe)
            hgrn_pe(pe)
            qkv_pe(pe)
            pe.wait_ge(kp_ok, 1)
            gqa_pe(pe)
            merge_pe(pe)
            pe.wait_ge(y_ok, 2)
            residual_pe(pe, G_OUT, U_OUT, y)
            norm_pe(pe, 2, hT)
            route_pe(pe)
            experts_pe(pe)
            norm_pe(pe, 3, hT)
            norm_pe(pe, 4, hT)
            mla_pe(pe)
            pe.wait_ge(krp_ok, 1)
            mla_att_pe(pe)
            pe.wait_ge(mla_oe, 2 + 8)
            residual_pe(pe, G_MWO, U_MWO, qn)
            norm_pe(pe, 7, hT)
            ff_pe(pe, 0, 7)
            norm_pe(pe, 8, hT)
            swa_qkv_pe(pe)
            pe.wait_ge(v_ok, 1)
            swa_att_pe(pe)
            pe.wait_ge(swa_oe, 2 + 8)
            residual_pe(pe, G_SWO, U_SWO, qn)
            norm_pe(pe, 9, hT)
            ff_pe(pe, 1, 9)
            end_pe(pe)

        @block.scalar
        def _(act):
            tables = lambda: nc.scalar.preload_act_table_set("natural_log_exp_and_others")
            start_act(act)
            start_norm_act(act)
            hgrn_act(act)
            qkv_act(act)
            gqa_act(act)
            merge_act(act)
            residual_act(act, G_OUT, 24)
            tables()
            norm_act(act, 2, xT, hT, ready=(x_ok, 1))
            route_act(act)
            experts_act(act)
            angles_act(act)
            tables()
            norm_act(act, 3, xT, hT, ready=(x_ok, 2))
            norm_act(act, 4, xT, hT, ready=(n_h, NH[4]))
            mla_act(act)
            mla_att_act(act)
            residual_act(act, G_MWO, 32)
            norm_act(act, 7, xT, hT, ready=(x_ok, 3))
            ff_act(act, 0)
            norm_act(act, 8, xT, hT, ready=(x_ok, 4))
            swa_qkv_act(act)
            act.wait_ge(v_ok, 1)
            swa_att_act(act)
            residual_act(act, G_SWO, 40, bias=V_BO)
            norm_act(act, 9, xT, hT, ready=(x_ok, 5))
            ff_act(act, 1)
            end_act(act)

        @block.vector
        def _(v):
            start_dve(v)
            hgrn_dve(v)
            qkv_dve(v)
            gqa_dve(v)
            merge_dve(v)
            residual_dve(v, G_OUT, 24, lambda j: mod[:, 16 + j:17 + j])
            norm_dve(v, 2, xT, hT, lambda k: gsc[:, 2, k:k + 1], lambda k: mod[:, 24 + k:25 + k])
            route_dve(v)
            experts_dve(v)
            angles_dve(v)
            norm_dve(v, 3, xT, xT, lambda k: V[:, V_FN + k:V_FN + k + 1])
            norm_dve(v, 4, xT, hT, lambda k: gsc[:, 3, k:k + 1], lambda k: mod2[:, k:k + 1])
            mla_dve(v)
            mla_att_dve(v)
            residual_dve(v, G_MWO, 32, lambda j: mod2[:, 16 + j:17 + j])
            norm_dve(v, 7, xT, hT, lambda k: gsc[:, 5, k:k + 1], lambda k: mod2[:, 24 + k:25 + k])
            ff_dve(v, 0)
            norm_dve(v, 8, xT, hT, lambda k: gsc[:, 4, k:k + 1], lambda k: mod2[:, 48 + k:49 + k])
            swa_qkv_dve(v)
            swa_att_dve(v)
            residual_dve(v, G_SWO, 40, lambda j: mod2[:, 64 + j:65 + j])
            norm_dve(v, 9, xT, hT, lambda k: gsc[:, 6, k:k + 1], lambda k: mod2[:, 72 + k:73 + k])
            ff_dve(v, 1)
            end_dve(v)


def _units(w, cols, row0=0, kt=KT, width=512):
    w = w[row0:row0 + kt * P][:, cols]
    w = np.concatenate([w, np.zeros((w.shape[0], width - w.shape[1]), w.dtype)], 1) if w.shape[1] < width else w
    per = UNIT // width
    short = -kt % per
    t = w.reshape(kt, P, width)
    t = np.concatenate([t, np.zeros((short, P, width), w.dtype)]) if short else t
    return t.reshape(-1, per, P, width).transpose(0, 2, 1, 3).reshape(-1, P, UNIT)


def _chunks(w, row0=0, kt=KT, width=512):
    return [_units(w, slice(c, c + width), row0, kt, width) for c in range(0, w.shape[1], width)]


def _stream(a):
    cat = np.concatenate
    r = lambda c0, n: np.arange(c0, c0 + n)
    w_in = a["w_in"][0]
    q0 = 8 * D
    parts = [u for w in (a["ada_w"][0], a["w_ada_2"][0], a["w_ada_2"][1]) for u in _chunks(w)]
    for h in range(HG):
        tile = lambda s: r(s * D + h * P, P)
        parts.append(_units(w_in, cat([tile(0), tile(4), tile(5), tile(6)])))
        parts.append(_units(w_in, cat([tile(7), tile(1), tile(2), tile(3)])))
    parts += _chunks(w_in[:, q0:q0 + D + 512])
    g0 = q0 + D + 512
    for n in range(2):
        for b, w in enumerate((a["w_proj_a"][0], a["w_proj_b"][0], a["w_proj_c"][0])):
            parts.append(_units(w_in, r(g0 + b * D + n * 512, 512)))
            parts.append(_units(w, r(n * 512, 512)))
    parts += _chunks(a["w_out"][0])
    wg, wu, wd = a["w_gate"][0], a["w_up"][0], a["w_down"][0]
    for p in range(NPAIR):
        def pair(w, n):
            e = [_units(w[2 * p + i], r(n * 512, 512)) for i in range(2)]
            return np.stack(e, 1).reshape(-1, P, UNIT)
        for n in range(2):
            parts += [pair(wg, n), pair(wu, n)]
        for n in range(2):
            parts.append(pair(wd, n))
    dkv = a["mla_w_dkv_2"][0]
    kr = dkv[:, KVL:]
    parts += _chunks(cat([a["mla_w_dq_2"][0], dkv[:, :KVL], kr, kr, np.zeros((D, 256), kr.dtype)], 1))
    uq = a["mla_w_uq_2"][0].reshape(QL, MLA_H, NOPE + ROPE_D)
    parts += _chunks(cat([uq[:, :, :NOPE].reshape(QL, -1), uq[:, :, NOPE:].reshape(QL, -1)], 1), kt=QT)
    ukv = a["mla_w_ukv_2"][0].reshape(KVL, MLA_H, 2 * NOPE)
    parts += _chunks(cat([ukv[:, :, :NOPE].reshape(KVL, -1), ukv[:, :, NOPE:].reshape(KVL, -1)], 1),
                     kt=KVT, width=1024)
    parts += _chunks(a["mla_w_o_2"][0])
    for layer in range(2):
        if layer:
            parts += _chunks(a["swa_w_qkv_2"][0]) + _chunks(a["swa_w_o_2"][0])
        parts += _chunks(a["w_ff1_2"][layer])
        for n in range(2):
            parts += [_units(a["w_ff2_2"][layer], r(n * 512, 512), row0=k * D) for k in range(4)]
    s = cat(parts)
    assert s.shape[0] == N_UNITS, s.shape
    return cat([s, np.zeros((N_STREAM - N_UNITS, P, UNIT), s.dtype)])


def _vecs(a):
    f = lambda v: np.asarray(v).reshape(-1, P)
    two = lambda v: np.concatenate([v.reshape(1, 64)] * 2, 1)
    rows = [f(a["c"]), f(a["c_ctx"]), f(a["c_2"]), f(a["ada_b"]), f(a["norm1_g"]), f(a["norm2_g"]),
            f(a["final_norm_g"]), f(a["hg_norm_g"]), f(a["conv_w"]),
            f(a["b_ada_2"]), f(a["g_mix_2"]), f(a["g_mlp_2"]),
            f(a["g_final_2"]), f(a["mla_g_q_2"]), f(a["mla_g_kv_2"]), f(a["swa_b_qkv_2"]),
            f(a["swa_b_o_2"]), two(a["q_norm_g"]), two(a["k_norm_g"])]
    rows = np.concatenate(rows)
    rows = np.concatenate([rows, np.zeros((N_VEC - len(rows), P), rows.dtype)])
    return np.ascontiguousarray(rows.reshape(3, P, P).transpose(1, 0, 2))


def _constants():
    c = np.zeros((P, N_CST), np.float32)
    p = np.arange(P)
    c[:, C_ID:C_ID + P] = np.eye(P)
    c[:, C_ONE:C_ONE + P] = 1
    c[:, C_BLK:C_BLK + P] = p[:, None] // 64 == p[None] // 64
    for m in range(P):
        c[m + 1 if m % 2 == 0 else m - 1, C_ROT1 + m] = -1 if m % 2 == 0 else 1
        c[m + 32 if m % 64 < 32 else m - 32, C_ROT2 + m] = -1 if m % 64 < 32 else 1
    c[:, C_CAUS:C_CAUS + P] = np.where(p[None] <= p[:, None], 0, NEG)
    dist = P + p[:, None] - np.arange(2 * P)[None]
    c[:, C_DIST:C_DIST + 2 * P] = np.where((dist >= 0) & (dist < P), dist, -NEG)
    c[:, C_SLOPE:C_SLOPE + 16] = -8.0 * 2.0 ** (-8.0 * np.arange(1, 17) / 16)
    c[:, C_PART:C_PART + 4] = p[:, None] + P * np.arange(4)
    for j in range(3):
        c[j::32, C_SEL + j] = 1
    c[:, C_INV] = (np.float32(10000.0) ** (-(p % 32).astype(np.float32) / 32)).astype(np.float32)
    h = np.zeros((P, N_HCST), np.float32)
    s, t = p[:, None], p[None]
    for lv, L in enumerate(LEVELS):
        same = s // (2 * L) == t // (2 * L)
        h[:, lv * P:(lv + 1) * P] = same & (s % (2 * L) < L) & (t % (2 * L) >= L)
        h[:, (NL + 1 + lv) * P:(NL + 2 + lv) * P] = same & (s % (2 * L) >= L) & (t % (2 * L) < L)
    for d in range(2):
        h[:, (d * (NL + 1) + NL) * P:(d * (NL + 1) + NL + 1) * P] = np.eye(P)
    h[:, H_SCAN:] = np.arange(TA) % P != 0
    inv = (np.float32(10000.0) ** (-np.arange(0, 32, 2, dtype=np.float32) / 32)).astype(np.float32)
    tok = np.arange(T)
    row, col = (tok // GRID_W).astype(np.float32), (tok % GRID_W).astype(np.float32)
    ang = np.concatenate([row[:, None] * inv, col[:, None] * inv], 1)
    f = (p % 64) // 2
    acst = np.concatenate([np.cos(ang)[:, f].T, np.sin(ang)[:, f].T], 1).astype(np.float32)
    iota = np.broadcast_to(np.arange(T, dtype=np.float32), (P, T))
    return c, h, np.ascontiguousarray(acst), np.ascontiguousarray(iota)


def host_arrays(a):
    c, h, ac, io = _constants()
    return {
        "stream": _stream(a), "vecs": _vecs(a), "cst": c, "hcst": h, "acst": ac, "iota": io,
        "x": np.ascontiguousarray(a["x"][0]), "ctxt": np.ascontiguousarray(a["ctx"][0]),
        "router": np.ascontiguousarray(a["router_w"][0].reshape(KT, P, NE).transpose(1, 0, 2)),
        "pos": np.ascontiguousarray(np.broadcast_to(a["positions_2"].reshape(1, T), (P, T))),
        "sinks": np.ascontiguousarray(np.broadcast_to(a["swa_sinks_2"].reshape(1, 16), (P, 16))),
        "bv": np.ascontiguousarray(np.broadcast_to(a["swa_b_qkv_2"].reshape(-1)[1280:], (P, 256))),
    }


def kernel(**inputs):
    import concourse.bacc as bacc
    from concourse.bass_utils import run_bass_kernel_spmd

    a = {k: np.asarray(v) for k, v in inputs.items()}
    arrays = host_arrays(a)
    nc = bacc.Bacc("TRN2", target_bir_lowering=False, num_devices=1)
    aps = {n: nc.dram_tensor(n, v.shape, mybir.dt.from_np(v.dtype), kind="ExternalInput").ap()
           for n, v in arrays.items()}
    out = nc.dram_tensor("out", (T, D), mybir.dt.float32, kind="ExternalOutput").ap()
    build(nc, out=out, **aps)
    r = run_bass_kernel_spmd(nc, [arrays], core_ids=[0])
    return r.results[0]["out"].reshape(1, T, D)
```

```python
import numpy as np
import concourse.bass as bass
from concourse import mybir
from contextlib import ExitStack

P = 128
D = 1024
KT = D // P
T = 512
TC = 256
TA = T + TC
NT, NC_, NA = T // P, TC // P, TA // P
HG = 8
GRID_W = 64
EPS = 1e-6
NE, CAP, FF = 16, 64, 1024
NPAIR = NE // 2
LEVELS = (64, 32, 16, 8, 4, 2, 1)
NL = len(LEVELS)
SLOTS, WIDE = 4, 8
UNIT = 2048
NEG = -1e30
MLA_H, NOPE, ROPE_D, QL, KVL = 8, 128, 64, 384, 256
QT, KVT = QL // P, KVL // P
DFF = 4 * D
FT = DFF // P

C_ID, C_ONE, C_BLK, C_ROT1, C_ROT2 = 0, 128, 256, 384, 512
C_CAUS = 640
C_DIST = 768
C_SLOPE = C_DIST + 256
C_PART = C_SLOPE + 16
C_SEL = C_PART + 4
C_INV = C_SEL + 4
N_CST = C_INV + 4
H_MASK, H_SCAN = 0, 2 * (NL + 1) * P
N_HCST = H_SCAN + TA
A_COS, A_SIN, N_ACST = 0, T, 2 * T

V_C, V_CC, V_C2, V_ADAB, V_N1, V_N2, V_FN, V_HG, V_CONV = 0, 8, 16, 24, 72, 80, 88, 96, 104
V_ADAB2, V_GMIX, V_GMLP = 128, 224, 240
V_GF, V_GQ, V_GKV, V_BQKV, V_BO, V_QN, V_KN = 256, 264, 267, 269, 281, 289, 290
N_VEC = 384

U_ADA = 0
U_HG = U_ADA + 24
HGU = 12
U_QKV = U_HG + 4 + (HG - 2) * HGU + 4
U_MERGE = U_QKV + 6
U_OUT = U_MERGE + 24
U_EXP = U_OUT + 4
U_MD = U_EXP + 24 * NPAIR
U_MUQ = U_MD + 4
U_MUKV = U_MUQ + 3
U_MWO = U_MUKV + 2
U_FF = (U_MWO + 4, U_MWO + 4 + 32 + 10)
U_SQKV = U_MWO + 4 + 32
U_SWO = U_SQKV + 6
N_UNITS = U_FF[1] + 32
N_STREAM = U_MD + (N_UNITS - U_MD + SLOTS - 1) // SLOTS * SLOTS
assert (U_MD - U_EXP) % WIDE == 0 and (U_MD - U_EXP) % SLOTS == 0

G_X = 0
G_ADA = G_X + 2 * KT
G_HG = G_ADA + 12
HGG = 18
G_QKV = G_HG + 10 + (HG - 2) * HGG + 10
G_MERGE = G_QKV + 14
G_OUT = G_MERGE + 48
G_H2T = G_OUT + KT
G_MD = G_H2T + 8
G_MUQ = G_MD + 6
G_MUKV = G_MUQ + 12
G_MWO = G_MUKV + 16
G_FF0 = G_MWO + KT
G_SQKV = G_FF0 + FT
G_SWO = G_SQKV + 12
G_FF1 = G_SWO + KT
G_FIN = G_FF1 + FT


def build(nc, stream, vecs, cst, hcst, acst, iota, x, ctxt, router, pos, sinks, bv, out):
    fp32, i32, u32 = mybir.dt.float32, mybir.dt.int32, mybir.dt.uint32
    ALU, ACT, AX = mybir.AluOpType, mybir.ActivationFunctionType, mybir.AxisListType
    ctx = ExitStack()
    with ctx:
        def sb(name, shape, dt=fp32):
            return ctx.enter_context(nc.sbuf_tensor(name, shape, dt))

        def sem(name):
            return ctx.enter_context(nc.semaphore(name))

        ring = [sb(f"ring{s}", [P, UNIT]) for s in range(SLOTS)]
        xT = sb("xT", [P, KT, T])
        hT = sb("hT", [P, KT, T])
        C = sb("C", [P, N_CST])
        V = sb("V", [P, N_VEC])
        cs = sb("cs", [P, KT, 32])
        mod = sb("mod", [P, 48])
        modc = sb("modc", [P, 16])
        mod2 = sb("mod2", [P, 96])
        gsc = sb("gsc", [P, 7, KT])
        rstd = sb("rstd", [P, T])
        pt = sb("pt", [P, 2, T])
        st8 = sb("st8", [P, 32])
        arena_n = 33100
        arena = sb("arena", [P, arena_n])
        PS = ctx.enter_context(nc.psum_tensor("PS", [P, 8, 512], fp32))

        def area(at, *shape):
            n = int(np.prod(shape))
            assert at + n <= arena_n, (at + n, arena_n)
            v = arena[:, at:at + n]
            names = "abcd"[:len(shape)]
            if len(shape) == 1:
                return v
            return v.rearrange(f"p ({' '.join(names)}) -> p {' '.join(names)}",
                               **{k: s for k, s in zip(names[1:], shape[1:])})

        def slot(u):
            j = u - U_EXP
            if 0 <= j < U_MD - U_EXP and j % WIDE >= SLOTS:
                return j % WIDE
            return u % SLOTS

        def arrival(u):
            j = u - U_EXP
            if j < 0:
                return u // SLOTS + 1
            before = sum(1 for s in range(slot(u), U_EXP, SLOTS))
            if j < U_MD - U_EXP:
                return j // WIDE + 1 + (before if slot(u) < SLOTS else 0)
            return before + (U_MD - U_EXP) // WIDE + (u - U_MD) // SLOTS + 1

        ring += [area(arena_n - (WIDE - s) * UNIT, UNIT) for s in range(SLOTS, WIDE)]

        ident = C[:, C_ID:C_ID + P]
        ones = C[:, C_ONE:C_ONE + P]

        w_loaded = [sem(f"w_loaded{s}") for s in range(WIDE)]
        w_used = sem("w_used")
        mm_done = sem("mm_done")
        evac_done = sem("evac_done")
        pt_used = sem("pt_used")
        in_const, in_vec, in_x, in_cst2, in_acst, in_iota = (sem(n) for n in
            ("in_const", "in_vec", "in_x", "in_cst2", "in_acst", "in_iota"))
        vec_t, vec_ok, cs_ok, ada_sel = (sem(n) for n in ("vec_t", "vec_ok", "cs_ok", "ada_sel"))
        mods_ok = sem("mods_ok")
        n_sq, n_ss, n_r, n_h, n_mod = (sem(n) for n in ("n_sq", "n_ss", "n_r", "n_h", "n_mod"))
        x_ok = sem("x_ok")

        def unit_wait(pe, su, per=0):
            pe.wait_ge(w_loaded[slot(su)], 16 * arrival(su) + 16 * per)

        def apart(act):
            nc.scalar.activation(st8[0:1, 30:31], st8[0:1, 31:32], ACT.Copy)
            act.drain()

        def first(eng, s):
            eng.drain().then_inc(s, 1)

        pend = [0]

        def mm(out_, lhsT, rhs, start, stop_, done=None, **kw):
            ins = nc.tensor.matmul(out_, lhsT, rhs, start=start, stop=stop_, **kw)
            if done is not None:
                ins.then_inc(done, 1)
            elif pend[0]:
                ins.then_inc(w_used, pend[0])
                pend[0] = 0

        def flush(pe):
            if pend[0]:
                pe.drain().then_inc(w_used, pend[0])
                pend[0] = 0

        def bank_wait(pe, g, first_free=2):
            if isinstance(g, int) and g < 2:
                return
            pe.wait_ge(evac_done, g - 1)

        def gemm(pe, g, gp, su, per, tiles, rhs, kt=KT, ncol=T, units=None, cols=512, waits=True, ready=None):
            kpu = UNIT // cols
            for n, c0 in enumerate(tiles):
                bank = (gp + n) % 2
                bank_wait(pe, g + n)
                for k in range(kt):
                    if n == 0 and k % kpu == 0 and waits:
                        unit_wait(pe, su + k // kpu, per)
                    if n == 0 and ready is not None:
                        pe.wait_ge(n_mod, ready + k + 1)
                    w = ring[slot(su + k // kpu)][:, :].rearrange("p (k n) -> p k n", n=cols)
                    mm(PS[:, bank, 0:ncol], w[:, k % kpu, c0:c0 + P], rhs[:, k, 0:ncol],
                       k == 0, k == kt - 1, mm_done if k == kt - 1 else None)

        def gemm_tok(pe, g, gp, su, tok, toks, c0, ncol, kt=KT, cols=512):
            kpu = UNIT // cols
            bank = gp % 2
            bank_wait(pe, g)
            for m, t0 in enumerate(toks):
                for k in range(kt):
                    w = ring[slot(su + k // kpu)][:, :].rearrange("p (k n) -> p k n", n=cols)
                    last = k == kt - 1 and m == len(toks) - 1
                    mm(PS[:, bank, m * ncol:(m + 1) * ncol], tok[:, k, t0:t0 + P],
                       w[:, k % kpu, c0:c0 + ncol], k == 0, k == kt - 1, mm_done if last else None)

        def evac(act, g, gp, dst, n=T, func=ACT.Copy, w=None, **kw):
            act.wait_ge(mm_done, g + 1)
            src = PS[:, gp % 2, 0:n]
            if w is not None:
                src = src.rearrange("p (a b) -> p a b", b=w)
            nc.scalar.activation(dst, src, func, **kw).then_inc(evac_done, 1)

        def norm_pe(pe, use, sq, kt=KT, n=T):
            for k in range(kt):
                pe.wait_ge(n_sq, NSQ[use] + k + 1)
                mm(PS[:, 7, 0:n], ones, sq[:, k, 0:n], k == 0, k == kt - 1, n_ss if k == kt - 1 else None)

        def norm_act(act, use, src, sq, kt=KT, n=T, ready=None):
            if ready is not None:
                act.wait_ge(*ready)
            for k in range(kt):
                nc.scalar.activation(sq[:, k, 0:n], src[:, k, 0:n], ACT.Square).then_inc(n_sq, 1)
            act.wait_ge(n_ss, use + 1)
            if use > 0:
                act.wait_ge(n_h, NH[use])
            act.drain()
            nc.scalar.activation(rstd[:, 0:n], PS[:, 7, 0:n], ACT.Ln, bias=epsb, scale=1.0 / (kt * P))
            act.drain()
            nc.scalar.activation(rstd[:, 0:n], rstd[:, 0:n], ACT.Exp, scale=-0.5).then_inc(n_r, 1)

        def norm_dve(v, use, src, dst, g=None, kt=KT, n=T):
            v.wait_ge(n_r, use + 1)
            v.drain()
            for k in range(kt):
                if g is None:
                    nc.vector.tensor_tensor(dst[:, k, 0:n], src[:, k, 0:n], rstd[:, 0:n], ALU.mult)\
                        .then_inc(n_h, 1)
                else:
                    nc.vector.scalar_tensor_tensor(dst[:, k, 0:n], src[:, k, 0:n], g(k), rstd[:, 0:n],
                                                   ALU.mult, ALU.mult).then_inc(n_h, 1)

        def norm_shift(act, use, dst, row, sh, n=T):
            for k in range(KT):
                act.wait_ge(n_h, NH[use] + k + 1)
                nc.scalar.activation(dst[:, k, 0:n], dst[:, k, 0:n], ACT.Identity,
                                     scale=gsc[:, row, k:k + 1], bias=sh[:, k:k + 1]).then_inc(n_mod, 1)

        KTS = [KT, KT, KT, KT, KT, QT, KVT, KT, KT, KT, KT]
        NSQ = [sum(KTS[:i]) for i in range(len(KTS) + 1)]
        NH = NSQ
        NM = {use: KT * i for i, use in enumerate((1, 0, 2, 4, 7, 8, 9))}
        epsb = st8[:, 31:32]
        HC = area(0, KT, TC)
        OA = area(2048, KT, T)
        OB = area(6144, KT, T)
        x_tok = area(10240, NT, D)
        c_tok = area(14336, NC_, D)
        cT = area(16384, KT, TC)
        arow = area(18432, 2, 512)
        v_rows = area(19456, 3, P)
        at = 10240
        H_CST = area(at, N_HCST); at += N_HCST
        hq = area(at, 2, T); at += 2 * T
        hg = area(at, 2, T); at += 2 * T
        hv = area(at, 2, NA, P); at += 2 * TA
        hz = area(at, 2, TA); at += 2 * TA
        hp = area(at, 3, T); at += 3 * T
        hW = area(at, NL, T); at += NL * T
        hk = area(at, 2, TA); at += 2 * TA
        hX = area(at, TA); at += TA
        htmp = area(at, TA); at += TA
        hQ = area(at, 2, T); at += 2 * T
        hKo = area(at, 2, TA); at += 2 * TA
        hKT = area(at, TA); at += TA
        hS = area(at, 2, 5, P); at += 10 * P
        hAT = area(at, 2, T); at += 2 * T
        ho = area(at, T); at += T
        hsq = area(at, T); at += T
        hT_ = area(at, 2, NA); at += 2 * NA
        hada = area(at, 2, 16); at += 32
        hr = rstd[:, :]
        hM = pt[:, :, :].rearrange("p a b -> p (a b)")
        hmask = H_CST[:, H_MASK:H_MASK + 2 * (NL + 1) * P].rearrange("p (d n) -> p d n", d=2)
        hscan = H_CST[:, H_SCAN:H_SCAN + TA]

        h_l, h_km, h_x, h_e, h_kout, h_w, h_d, h_wl = (sem(n) for n in
            ("h_l", "h_km", "h_x", "h_e", "h_kout", "h_w", "h_d", "h_wl"))
        h_T, h_kT, h_A, h_afree, h_at, h_st, h_S, h_conv = (sem(n) for n in
            ("h_T", "h_kT", "h_A", "h_afree", "h_at", "h_st", "h_S", "h_conv"))
        h_o, h_sq, h_ss, h_r, h_out = (sem(n) for n in ("h_o", "h_sq", "h_ss", "h_r", "h_out"))
        h_sl, h_sm, h_sg = (sem(n) for n in ("h_sl", "h_sm", "h_sg"))

        WALK = [[NT + i for i in range(NC_)] + list(range(NT - 1)),
                [NA - 1 - i for i in range(NC_)] + list(range(NT - 1, 0, -1))]
        BEFORE = [[NC_ - 1 + i for i in range(NT)], [NC_ - 1 + NT - 1 - i for i in range(NT)]]

        def start_pe(pe):
            pe.wait_ge(in_const, 16)
            pe.wait_ge(in_vec, 16)
            for j in range(3):
                nc.tensor.transpose(PS[:, 6, j * P:(j + 1) * P], v_rows[:, j, :], ident)\
                    .then_inc(vec_t, 1)
            pe.wait_ge(in_x, 32)
            for k in range(KT):
                g = G_X + k
                bank_wait(pe, g)
                for m in range(NT):
                    ins = nc.tensor.transpose(PS[:, g % 2, m * P:(m + 1) * P],
                                              x_tok[:, m, k * P:(k + 1) * P], ident)
                ins.then_inc(mm_done, 1)
            for k in range(KT):
                g = G_X + KT + k
                bank_wait(pe, g)
                for m in range(NC_):
                    ins = nc.tensor.transpose(PS[:, g % 2, m * P:(m + 1) * P],
                                              c_tok[:, m, k * P:(k + 1) * P], ident)
                ins.then_inc(mm_done, 1)
            pe.wait_ge(cs_ok, 2)
            first(pe, ada_sel)
            sel = C[:, C_SEL:C_SEL + 3]

            def select(i, c):
                pe.wait_ge(evac_done, G_ADA + 2 * i + c + 1)
                for j in range(4):
                    ins = nc.tensor.matmul(PS[:, 4, bass.ds(24 * i + 12 * c + 3 * j, 3)],
                                           arow[:, c, j * P:(j + 1) * P], sel, start=True, stop=True)
                ins.then_inc(ada_sel, 1)

            for part in range(3):
                with pe.Fori(2 * part, 2 * part + 2) as i:
                    for c in range(2):
                        g = G_ADA + 2 * i + c
                        pe.wait_ge(evac_done, g - 1)
                        for k in range(KT):
                            q = k % 4
                            if k % 4 == 0:
                                unit_wait(pe, U_ADA + 2 * c + k // 4, i)
                            w = ring[2 * c + k // 4][:, (k % 4) * 512:(k % 4 + 1) * 512]
                            ins = nc.tensor.matmul(PS[32 * q:32 * q + 32, (G_ADA + c) % 2, :], cs[:, k, :], w,
                                                   start=k < 4, stop=k >= 4, tile_position=(0, 32 * q))
                            if k == KT - 1:
                                ins.then_inc(mm_done, 1)
                            elif k % 4 == 3:
                                ins.then_inc(w_used, 1)
                    select(i, 0)
                    select(i, 1)
                    pe.drain().then_inc(w_used, 2)
                if part == 0:
                    norm_pe(pe, 0, HC, n=TC)
                elif part == 1:
                    norm_pe(pe, 1, hT)

        def start_act(act):
            act.wait_ge(vec_t, 3)
            nc.scalar.activation(V[:, :], PS[:, 6, 0:N_VEC], ACT.Copy).then_inc(vec_ok, 1)
            act.wait_ge(cs_ok, 1)
            act.drain()
            for j, v0 in enumerate((V_C, V_CC, V_C2)):
                ins = nc.scalar.activation(cs[:, :, j], V[:, v0:v0 + KT], ACT.Silu)
            ins.then_inc(cs_ok, 1)
            for k in range(KT):
                evac(act, G_X + k, G_X + k, xT[:, k, :])
            for k in range(KT):
                evac(act, G_X + KT + k, G_X + KT + k, cT[:, k, :], n=TC)
            nc.scalar.preload_act_table_set("natural_log_exp_and_others")
            for part in range(3):
                with act.Fori(2 * part, 2 * part + 2) as i:
                    for c in range(2):
                        g = G_ADA + 2 * i + c
                        act.wait_ge(mm_done, g + 1)
                        act.wait_ge(ada_sel, 2 * i + 1)
                        nc.scalar.activation(arow[:, c, :], PS[:, (G_ADA + c) % 2, :], ACT.Copy)\
                            .then_inc(evac_done, 1)
                if part == 0:
                    norm_act(act, 0, cT, HC, n=TC, ready=(evac_done, G_X + 2 * KT))
                elif part == 1:
                    norm_act(act, 1, xT, hT)
            act.wait_ge(mods_ok, 1)
            norm_shift(act, 1, hT, 1, mod[:, 0:KT])
            norm_shift(act, 0, HC, 0, modc[:, 0:KT], n=TC)

        def norm_scales(r0, norms):
            for r, (m, s, n) in enumerate(norms):
                nc.vector.scalar_tensor_tensor(gsc[:, r0 + r, :], m[:, s:s + KT], 1.0, V[:, n:n + KT],
                                               ALU.add, ALU.mult)

        def start_dve(v):
            nc.vector.memset(st8[:, 31:32], EPS)
            nc.vector.memset(cs[:, :, :], 0.0).then_inc(cs_ok, 1)
            norm_dve(v, 0, cT, HC, n=TC)
            norm_dve(v, 1, xT, hT)
            v.wait_ge(ada_sel, 13)
            v.wait_ge(vec_ok, 1)
            m3 = PS[:, 4, 0:144].rearrange("p (c m) -> p c m", m=3)
            nc.vector.tensor_tensor(mod[:, :], m3[:, 0:48, 0], V[:, V_ADAB:V_ADAB + 48], ALU.add)
            nc.vector.tensor_tensor(modc[:, :], m3[:, 0:16, 1], V[:, V_ADAB:V_ADAB + 16], ALU.add)
            v.drain()
            norm_scales(0, ((modc, 8, V_N1), (mod, 8, V_N1), (mod, 32, V_N2)))
            v.drain().then_inc(mods_ok, 1)

        def head_group(h):
            return G_HG if isinstance(h, int) and h == 0 else G_HG + HGG * (h - 1) + 10

        def first_products(pe, h, u, per, ready=None):
            g = head_group(h)
            gemm(pe, g, G_HG, u, per, (0, 128, 256, 384), hT, ready=ready)
            pend[0] += 2
            gemm(pe, g + 4, G_HG + 4, u + 2, per, (0,), hT)

        def second_products(pe, h, u, per):
            g = head_group(h)
            gemm(pe, g + 5, G_HG + 5, u + 2, per, (128, 256), hT, waits=False)
            bank = (G_HG + 7) % 2
            bank_wait(pe, g + 7)
            for d in range(2):
                for k in range(KT):
                    w = ring[slot(u + 2 + k // 4)]
                    c0 = (k % 4) * 512 + 128 + 128 * d
                    mm(PS[:, bank, d * TC:(d + 1) * TC], w[:, c0:c0 + P], HC[:, k, :], k == 0, k == KT - 1,
                       mm_done if d == 1 and k == KT - 1 else None)
            gemm_tok(pe, g + 8, G_HG + 8, u + 2, hT, range(0, T, P), 384, P)
            gemm_tok(pe, g + 9, G_HG + 9, u + 2, HC, range(0, TC, P), 384, P)
            pend[0] += 2
            flush(pe)

        ADA_V, ADA_S = (0, 1, 3, 5), (2, 4, 6, 7)
        arow2 = OA[:, 6:8, :]

        def ada_products(pe, h, u, per, c):
            g = head_group(h + 1) + 10 + ADA_V[c]
            bank_wait(pe, g)
            for k in range(KT):
                q, su = k % 4, u + 2 * c + k // 4
                if k % 4 == 0:
                    unit_wait(pe, su, per)
                mm(PS[32 * q:32 * q + 32, (G_HG + ADA_V[c]) % 2, :], cs[:, k, :],
                   ring[slot(su)][:, (k % 4) * 512:(k % 4 + 1) * 512], k < 4, k >= 4,
                   mm_done if k == KT - 1 else None, tile_position=(0, 32 * q))
            pend[0] += 2

        def ada_sums(pe, h, c):
            g = head_group(h + 1) + 10 + ADA_S[c]
            bank_wait(pe, g)
            for j in range(4):
                mm(PS[:, (G_HG + ADA_S[c]) % 2, j:j + 1], arow2[:, c % 2, j * P:(j + 1) * P],
                   C[:, C_SEL + 2:C_SEL + 3], True, True, mm_done if j == 3 else None)

        def ada_evac(act, h, par, n):
            if n in ADA_V:
                dst, w = arow2[:, ADA_V.index(n) % 2, :], 512
            else:
                c = ADA_S.index(n)
                dst, w = hada[:, par, 4 * c:4 * c + 4], 4
            act.wait_ge(mm_done, head_group(h + 1) + 10 + n + 1)
            nc.scalar.activation(dst, PS[:, (G_HG + n) % 2, 0:w], ACT.Copy).then_inc(evac_done, 1)

        def rec_pe(pe, h, par, d, between=None):
            Ko, W = hKo[:, d, :], hW
            pe.wait_ge(h_kout, 2 * h + d + 2)
            if d == 0:
                pe.wait_ge(h_r, h + 1)
            else:
                pe.wait_ge(h_S, 2 * h + 1)
            for m in range(NA):
                ins = nc.tensor.transpose(PS[:, 6 + m // 4, (m % 4) * P:(m % 4 + 1) * P],
                                          Ko[:, m * P:(m + 1) * P], ident)
            ins.then_inc(h_T, 1)
            pe.wait_ge(h_wl, 2 * h + d + 1)
            for i in range(NT):
                b0 = 2 + 2 * (i % 2)
                n = 8 * h + 4 * d + i
                pe.wait_ge(h_afree, n + 1)
                tile = slice(i * P, (i + 1) * P)
                for lv in range(NL):
                    nc.tensor.matmul(PS[:, b0 + lv // 4, (lv % 4) * P:(lv % 4 + 1) * P],
                                     W[:, lv, tile], W[:, lv, tile], start=True, stop=True)
                nc.tensor.matmul(PS[:, b0 + NL // 4, (NL % 4) * P:(NL % 4 + 1) * P],
                                 hk[:, d, tile], hq[:, par, tile], start=True, stop=True).then_inc(h_A, 1)
            if between is not None:
                between()
            pe.wait_ge(h_kT, 2 * h + d + 1)
            for n, m in enumerate(WALK[d]):
                ins = nc.tensor.matmul(PS[:, 6 + n // 4, (n % 4) * P:(n % 4 + 1) * P],
                                       hKT[:, m * P:(m + 1) * P], hv[:, par, m, :], start=True, stop=True)
            ins.then_inc(h_st, 1)

        def out_pe(pe, h, par, before=None, between=None):
            if before is not None:
                before()
            pe.wait_ge(h_S, 2 * h + 2)
            pe.wait_ge(h_at, 2 * h + 2)
            for i in range(NT):
                tile = slice(i * P, (i + 1) * P)
                o = PS[:, 6, tile]
                nc.tensor.matmul(o, hv[:, par, i, :], hAT[:, 0, tile], start=True, stop=False)
                nc.tensor.matmul(o, hv[:, par, i, :], hAT[:, 1, tile], start=False, stop=False)
                nc.tensor.matmul(o, hS[:, 0, BEFORE[0][i], :], hQ[:, 0, tile], start=False, stop=False)
                ins = nc.tensor.matmul(o, hS[:, 1, BEFORE[1][i], :], hQ[:, 1, tile], start=False, stop=True)
            ins.then_inc(h_o, 1)
            if between is not None:
                between()
            pe.wait_ge(h_sq, h + 1)
            nc.tensor.matmul(PS[:, 7, :], ones, hsq, start=True, stop=True).then_inc(h_ss, 1)

        def head_pe(pe, h, par, nxt=None, ada=None):
            if nxt:
                first_products(pe, h + 1, *nxt)
                flush(pe)
            rec_pe(pe, h, par, 0)
            if nxt:
                second_products(pe, h + 1, *nxt)
            if ada is None:
                rec_pe(pe, h, par, 1)
                out_pe(pe, h, par)
                return

            def chunk(c):
                ada_products(pe, h, *ada, c)
                ada_sums(pe, h, c - 1)

            ada_products(pe, h, *ada, 0)
            rec_pe(pe, h, par, 1, lambda: chunk(1))
            out_pe(pe, h, par, lambda: chunk(2), lambda: chunk(3))
            ada_sums(pe, h, 3)
            flush(pe)

        def hgrn_pe(pe):
            pe.wait_ge(in_cst2, 16)
            first(pe, h_ss)
            first_products(pe, 0, U_HG, 0, ready=NM[1])
            flush(pe)
            pe.wait_ge(n_mod, NM[0] + KT)
            second_products(pe, 0, U_HG, 0)
            turns = 2 * HGU // SLOTS
            with pe.Fori(0, 3) as i:
                for par in range(2):
                    u = U_HG + 4 + HGU * par
                    head_pe(pe, 2 * i + par, par, (u, turns * i), (u + 4, turns * i))
            head_pe(pe, 6, 0, (U_QKV - 4, 0))
            head_pe(pe, 7, 1)

        def evac_first(act, h, par, n):
            g = head_group(h)
            if n == 2 and not (isinstance(h, int) and h == 0):
                act.wait_ge(h_conv, h)
            dst = (hq[:, par, :], hg[:, par, :], hp[:, 0, :], hp[:, 1, :], hp[:, 2, :])[n]
            act.wait_ge(mm_done, g + n + 1)
            nc.scalar.activation(dst, PS[:, (G_HG + n) % 2, :], ACT.Copy).then_inc(evac_done, 1)

        def evac_second(act, h, par, n):
            g = head_group(h) + 5
            act.wait_ge(mm_done, g + n + 1)
            src = PS[:, (G_HG + 5 + n) % 2, :]
            if n < 2:
                dst = hz[:, n, 0:T]
            elif n == 2:
                dst, src = hz[:, :, T:TA], src.rearrange("p (a b) -> p a b", a=2)
            elif n == 3:
                dst, src = hv[:, par, 0:NT, :], src.rearrange("p (a b) -> p a b", b=P)
            else:
                dst, src = hv[:, par, NT:NA, :], src[:, 0:TC].rearrange("p (a b) -> p a b", b=P)
            nc.scalar.activation(dst, src, ACT.Copy).then_inc(evac_done, 1)

        def gate_act(act, h, par):
            if not (isinstance(h, int) and h == 0):
                act.drain()
                act.wait_ge(h_ss, h + 1)
            else:
                act.drain()
            nc.scalar.activation(hsq, hg[:, par, :], ACT.Abs)
            act.drain()
            nc.scalar.activation(hsq, hsq, ACT.Exp, scale=-1.0)
            act.drain()
            nc.scalar.activation(hsq, hsq, ACT.Ln, bias=1.0).then_inc(h_sl, 1)
            act.wait_ge(h_sm, h + 1)
            nc.scalar.activation(hsq, hsq, ACT.Exp).then_inc(h_sg, 1)

        def prep_act(act, h, par, d):
            z = hz[:, d, :]
            n = 2 * h + d
            if not (isinstance(n, int) and n == 0):
                act.drain()
                act.wait_ge(h_kout, n + 1)
            else:
                act.drain()
            nc.scalar.activation(htmp, z, ACT.Abs)
            act.drain()
            nc.scalar.activation(htmp, htmp, ACT.Exp, scale=-1.0)
            act.drain()
            nc.scalar.activation(htmp, htmp, ACT.Ln, bias=1.0).then_inc(h_l, 1)
            act.wait_ge(h_km, n + 1)
            nc.scalar.activation(hk[:, d, :], hk[:, d, :], ACT.Exp)
            act.wait_ge(h_x, n + 1)
            nc.scalar.activation(hT_[:, d, :], hT_[:, d, :], ACT.Exp)
            if d == 0:
                nc.scalar.activation(hKo[:, 0, :], htmp, ACT.Exp)
                nc.scalar.activation(hQ[:, 0, :], hX[:, 0:T], ACT.Exp).then_inc(h_e, 1)
            else:
                nc.scalar.activation(hKo[:, 1, :], hX, ACT.Exp)
                nc.scalar.activation(hQ[:, 1, :], htmp[:, 0:T], ACT.Exp).then_inc(h_e, 1)

        def level_act(act, h, d, lv):
            act.wait_ge(h_d, 2 * NL * h + NL * d + lv + 1)
            nc.scalar.activation(hW[:, lv, :], hW[:, lv, :], ACT.Exp).then_inc(h_w, 1)

        def keys_act(act, h, d):
            act.wait_ge(h_T, 2 * h + d + 1)
            nc.scalar.activation(hKT, PS[:, 6:8, :].rearrange("p a b -> p (a b)")[:, 0:TA], ACT.Copy)\
                .then_inc(h_kT, 1)

        def head_act(act, h, par, more, ada=False):
            gate_act(act, h, par)
            prep_act(act, h, par, 0)
            after = {0: 0, 1: 1, 3: 2, 5: 3}
            for lv in range(NL):
                level_act(act, h, 0, lv)
                if more and lv in after:
                    evac_first(act, h + 1, 1 - par, after[lv])
            prep_act(act, h, par, 1)
            if more:
                evac_first(act, h + 1, 1 - par, 4)
            keys_act(act, h, 0)
            after = {0: 0, 1: 1, 3: 2, 5: 3, 6: 4}
            for lv in range(NL):
                level_act(act, h, 1, lv)
                if more and lv in after:
                    evac_second(act, h + 1, 1 - par, after[lv])
            if ada:
                ada_evac(act, h, par, 0)
            keys_act(act, h, 1)
            if ada:
                for n in range(1, 5):
                    ada_evac(act, h, par, n)
            act.wait_ge(h_o, h + 1)
            if not (isinstance(h, int) and h == 0):
                act.wait_ge(h_out, h + 1)
            nc.scalar.activation(ho, PS[:, 6, :], ACT.Copy)
            act.wait_ge(h_gm, h + 1)
            nc.scalar.activation(hsq, PS[:, 6, :], ACT.Square).then_inc(h_sq, 1)
            if ada:
                ada_evac(act, h, par, 5)
                ada_evac(act, h, par, 6)
            act.wait_ge(h_ss, h + 2)
            nc.scalar.activation(hr, PS[:, 7, :], ACT.Ln, bias=epsb, scale=1.0 / P)
            act.drain()
            nc.scalar.activation(hr, hr, ACT.Exp, scale=-0.5).then_inc(h_r, 1)
            if ada:
                ada_evac(act, h, par, 7)

        h_gm = sem("h_gm")

        def hgrn_act(act):
            first(act, h_r)
            for n in range(5):
                evac_first(act, 0, 0, n)
            for n in range(5):
                evac_second(act, 0, 0, n)
            with act.Fori(0, 3) as i:
                head_act(act, 2 * i, 0, True, True)
                head_act(act, 2 * i + 1, 1, True, True)
            head_act(act, 6, 0, True)
            head_act(act, 7, 1, False)

        def conv_dve(v, h):
            v.wait_ge(evac_done, head_group(h) + 5)
            w = [V[:, bass.ds(V_CONV + 8 * t + h, 1)] for t in range(3)]
            p5, p6, p7 = hp[:, 0, :], hp[:, 1, :], hp[:, 2, :]
            nc.vector.tensor_tensor(p6, p6, p7, ALU.mult)
            v.drain()
            nc.vector.tensor_scalar(p7, p6, w[1], None, ALU.mult)
            v.drain()
            nc.vector.scalar_tensor_tensor(p7[:, 1:T], p6[:, 0:T - 1], w[0], p7[:, 1:T], ALU.mult, ALU.add)
            v.drain()
            nc.vector.scalar_tensor_tensor(p7[:, 0:T - 1], p6[:, 1:T], w[2], p7[:, 0:T - 1],
                                           ALU.mult, ALU.add)
            v.drain()
            dst = OB[:, h, :] if isinstance(h, int) else OB[:, bass.ds(h, 1), :].rearrange("p a b -> p (a b)")
            nc.vector.tensor_tensor(dst, p7, p5, ALU.mult).then_inc(h_conv, 1)

        def prep_dve(v, h, par, d):
            z = hz[:, d, :]
            n = 2 * h + d
            v.wait_ge(h_l, n + 1)
            nc.vector.scalar_tensor_tensor(htmp, z, 0.0, htmp, ALU.min, ALU.subtract)
            v.drain()
            nc.vector.tensor_tensor(hk[:, d, :], htmp, z, ALU.subtract).then_inc(h_km, 1)
            nc.vector.tensor_tensor_scan(hX, hscan, htmp, 0.0, ALU.mult, ALU.add)
            v.drain()
            x3 = hX.rearrange("p (m t) -> p m t", t=P)
            t3 = htmp.rearrange("p (m t) -> p m t", t=P)
            nc.vector.tensor_copy(hT_[:, d, :], x3[:, :, P - 1])
            if d == 1:
                v.drain()
                nc.vector.tensor_tensor(hX, hX, htmp, ALU.subtract)
            v.drain()
            nc.vector.tensor_tensor(t3, hT_[:, d, :].unsqueeze(2).broadcast_to([P, NA, P]), x3,
                                    ALU.subtract).then_inc(h_x, 1)
            v.wait_ge(h_e, n + 1)
            nc.vector.tensor_tensor(hKo[:, d, :], hKo[:, d, :], hk[:, d, :], ALU.mult)
            nc.vector.tensor_tensor(hQ[:, d, :], hQ[:, d, :], hq[:, par, :], ALU.mult).then_inc(h_kout, 1)

        def level_views(lv):
            L = LEVELS[lv]
            X = hX[:, 0:T].rearrange("p (n a l) -> p n a l", a=2, l=L)
            W = hW[:, lv, :].rearrange("p (n a l) -> p n a l", a=2, l=L)
            return L, X, W

        def levels_dve(v, h, par, d):
            def factors(lv):
                L, X, W = level_views(lv)
                mid = X[:, :, 1, 0:1].broadcast_to([P, T // (2 * L), L])
                nc.vector.tensor_tensor(W[:, :, 0, :], mid, X[:, :, 0, :], ALU.subtract)
                nc.vector.tensor_tensor(W[:, :, 1, :], X[:, :, 1, :], mid, ALU.subtract).then_inc(h_d, 1)

            def roles(lv):
                L, X, W = level_views(lv)
                v.wait_ge(h_w, 2 * NL * h + NL * d + lv + 1)
                a, b = (hk[:, d, 0:T], hq[:, par, :]) if d == 0 else (hq[:, par, :], hk[:, d, 0:T])
                a = a.rearrange("p (n a l) -> p n a l", a=2, l=L)
                b = b.rearrange("p (n a l) -> p n a l", a=2, l=L)
                nc.vector.tensor_tensor(W[:, :, 0, :], W[:, :, 0, :], a[:, :, 0, :], ALU.mult)
                ins = nc.vector.tensor_tensor(W[:, :, 1, :], W[:, :, 1, :], b[:, :, 1, :], ALU.mult)
                if lv == NL - 1:
                    ins.then_inc(h_wl, 1)

            factors(0)
            for lv in range(NL):
                if lv + 1 < NL:
                    factors(lv + 1)
                roles(lv)

        def scores_dve(v, h, d):
            for i in range(NT):
                b0 = 2 + 2 * (i % 2)
                v.drain()
                v.wait_ge(h_A, 8 * h + 4 * d + i + 1)
                nc.vector.tensor_tensor(hM, PS[:, b0:b0 + 2, :].rearrange("p a b -> p (a b)"),
                                        hmask[:, d, :], ALU.mult).then_inc(h_afree, 1)
                v.drain()
                ins = nc.vector.tensor_reduce(hAT[:, d, i * P:(i + 1) * P],
                                              hM.rearrange("p (l t) -> p t l", t=P), AX.X, ALU.add)
            ins.then_inc(h_at, 1)

        def states_dve(v, h, d):
            for n, m in enumerate(WALK[d]):
                src = PS[:, 6 + n // 4, (n % 4) * P:(n % 4 + 1) * P]
                v.drain()
                if n == 0:
                    v.wait_ge(h_st, 2 * h + d + 1)
                    nc.vector.tensor_copy(hS[:, d, 0, :], src)
                else:
                    ins = nc.vector.scalar_tensor_tensor(hS[:, d, n, :], hS[:, d, n - 1, :],
                                                         hT_[:, d, m:m + 1], src, ALU.mult, ALU.add)
            ins.then_inc(h_S, 1)

        def head_dve(v, h, par, more, ada=False):
            v.wait_ge(h_sl, h + 1)
            nc.vector.scalar_tensor_tensor(hsq, hg[:, par, :], 0.0, hsq, ALU.min, ALU.subtract).then_inc(h_sm, 1)
            v.wait_ge(h_sg, h + 1)
            nc.vector.tensor_tensor(hg[:, par, :], hg[:, par, :], hsq, ALU.mult).then_inc(h_gm, 1)
            prep_dve(v, h, par, 0)
            levels_dve(v, h, par, 0)
            prep_dve(v, h, par, 1)
            scores_dve(v, h, 0)
            states_dve(v, h, 0)
            levels_dve(v, h, par, 1)
            scores_dve(v, h, 1)
            states_dve(v, h, 1)
            if more:
                conv_dve(v, h + 1)
            if ada:
                v.wait_ge(evac_done, head_group(h + 1) + 10 + 8)
                nc.vector.tensor_tensor(mod2[:, bass.ds(16 * h, 16)], hada[:, par, :],
                                        V[:, bass.ds(V_ADAB2 + 16 * h, 16)], ALU.add)
            v.wait_ge(h_r, h + 2)
            gn = V[:, bass.ds(V_HG + h, 1)]
            nc.vector.scalar_tensor_tensor(ho, ho, gn, hr, ALU.mult, ALU.mult)
            v.drain()
            dst = OA[:, h, :] if isinstance(h, int) else OA[:, bass.ds(h, 1), :].rearrange("p a b -> p (a b)")
            nc.vector.tensor_tensor(dst, ho, hg[:, par, :], ALU.mult).then_inc(h_out, 1)

        def hgrn_dve(v):
            v.wait_ge(in_cst2, 16)
            first(v, h_kout)
            first(v, h_out)
            conv_dve(v, 0)
            v.wait_ge(evac_done, G_HG + 10)
            v.drain().then_inc(h_afree, 2)
            with v.Fori(0, 3) as i:
                head_dve(v, 2 * i, 0, True, True)
                head_dve(v, 2 * i + 1, 1, True, True)
            head_dve(v, 6, 0, True)
            head_dve(v, 7, 1, False)
            norm_scales(3, ((mod2, 8, V_GMIX), (mod2, 56, V_GMIX + 8), (mod2, 32, V_GMLP),
                            (mod2, 80, V_GMLP + 8)))

        A_CST = area(10240, 2, T)
        qT = area(11264, KT, T)
        KP = area(15360, 4, 2, TA)
        VKV = area(21504, NA, 256)
        Pb = area(23040, 2, TA)
        PT = area(24576, 2, 6, T)
        qs = area(30720, 1, T)
        vs = area(31232, NA, 64)
        qk_k = area(23040, 2, T)
        qk_c = area(24064, T)
        qk_sq = area(24576, 2, T)
        qk_r = area(25600, 2, T)
        qk_t = area(26624, T)
        items = [qT[:, j, :] for j in range(8)] + [qk_k[:, 0, :], qk_k[:, 1, :], qk_c]
        NI = len(items)
        q_sq, q_ss, q_r, q_n, q_rot, q_done, kp_ok = (sem(n) for n in
            ("q_sq", "q_ss", "q_r", "q_n", "q_rot", "q_done", "kp_ok"))

        def qkv_pe(pe):
            pe.wait_ge(h_out, HG + 1)
            for j in range(14):
                g, su = G_QKV + j, U_QKV + 2 * min(j // 4, 2)
                if j < 10:
                    gemm(pe, g, g, su, 0, ((j % 4) * P,), hT)
                elif j == 10:
                    bank_wait(pe, g)
                    for t in range(2):
                        for k in range(KT):
                            w = ring[slot(su + k // 4)]
                            c0 = (k % 4) * 512 + P * t
                            mm(PS[:, g % 2, t * TC:(t + 1) * TC], w[:, c0:c0 + P], HC[:, k, :],
                               k == 0, k == KT - 1, mm_done if t == 1 and k == KT - 1 else None)
                else:
                    tok, t0 = (hT, (j - 11) * 2 * P) if j < 13 else (HC, 0)
                    gemm_tok(pe, g, g, su, tok, (t0, t0 + P), 256, 256)
                if j in (3, 7, 13):
                    pend[0] += 2
                n = j - 1
                if 0 <= n < NI:
                    pe.wait_ge(q_sq, n + 1)
                    if n >= 2:
                        pe.wait_ge(q_r, n - 1)
                    mm(PS[:, 4 + n % 2, :], C[:, C_BLK:C_BLK + P], qk_sq[:, n % 2, :], True, True, q_ss)
                n = j - 2
                if 0 <= n < NI - 1:
                    pe.wait_ge(q_n, n + 1)
                    if n >= 2:
                        pe.wait_ge(q_done, n - 1)
                    mm(PS[:, 6 + n % 2, :], C[:, C_ROT1:C_ROT1 + P], items[n], True, True, q_rot)
            flush(pe)

        def qkv_act(act):
            act.wait_ge(h_out, HG + 1)
            for j in range(14):
                g = G_QKV + j
                if j < NI:
                    evac(act, g, g, items[j])
                    act.drain()
                    if j >= 2:
                        act.wait_ge(q_ss, j - 1)
                    nc.scalar.activation(qk_sq[:, j % 2, :], items[j], ACT.Square).then_inc(q_sq, 1)
                else:
                    m = 2 * (j - 11)
                    evac(act, g, g, VKV[:, m:m + 2, :], w=256)
                n = j - 1
                if 0 <= n < NI:
                    act.wait_ge(q_ss, n + 1)
                    if n >= 2:
                        act.wait_ge(q_n, n - 1)
                    r = qk_r[:, n % 2, :]
                    nc.scalar.activation(r, PS[:, 4 + n % 2, :], ACT.Ln, bias=epsb, scale=1.0 / 64)
                    act.drain()
                    nc.scalar.activation(r, r, ACT.Exp, scale=-0.5).then_inc(q_r, 1)

        def rotate_dve(v, x, rot, tmp, cos, sin, done):
            nc.vector.tensor_tensor(tmp, rot, sin, ALU.mult)
            nc.vector.tensor_tensor(x, x, cos, ALU.mult)
            v.drain()
            nc.vector.tensor_tensor(x, x, tmp, ALU.add).then_inc(done, 1)

        def qkv_dve(v):
            v.drain()
            v.wait_ge(in_acst, 16)
            nc.vector.memset(KP[:, :, :, :], 0.0)
            for n in range(NI):
                v.wait_ge(q_r, n + 1)
                gn = V_QN if n < 8 else V_KN
                nc.vector.scalar_tensor_tensor(items[n], items[n], V[:, gn:gn + 1], qk_r[:, n % 2, :],
                                               ALU.mult, ALU.mult).then_inc(q_n, 1)
                v.drain()
                if n < NI - 1:
                    v.wait_ge(q_rot, n + 1)
                    rotate_dve(v, items[n], PS[:, 6 + n % 2, :], qk_t, A_CST[:, 0, :], A_CST[:, 1, :], q_done)
                v.drain()
            for g in range(4):
                r0 = (g % 2) * 64
                for e in range(2):
                    dst = slice(64 * e, 64 * e + 64)
                    nc.vector.tensor_copy(KP[dst, g, e, 0:T], qk_k[r0:r0 + 64, g // 2, :])
                    ins = nc.vector.tensor_copy(KP[dst, g, e, T:TA],
                                                qk_c[r0:r0 + 64, (g // 2) * TC:(g // 2 + 1) * TC])
            ins.then_inc(kp_ok, 1)

        def attention(name, E, keys, loads, score, value, store, scale, Pb, PT, bias=None, sink=None,
                      depth=2):
            a_ld, a_s, a_m, a_e, a_p, a_t, a_te, a_pv, a_oe = (sem(f"{name}_{x}") for x in
                ("ld", "s", "m", "e", "p", "t", "te", "pv", "oe"))
            NB = E * NT
            tdepth = lag = depth // 2
            ahead = max(depth - 1, 2)
            width = 4 // depth
            S2 = [PS[:, width * i:width * (i + 1), :].rearrange("p a b -> p (a b)") for i in range(depth)]
            TB = [PS[:, 4 + i:4 + i + 2 // tdepth, :].rearrange("p a b -> p (a b)") for i in range(tdepth)]
            per_out = E // 2
            col = lambda what, b: st8[:, what * depth + b % depth:what * depth + b % depth + 1]
            MAX, NEGMAX, SUM, RECIP, SINK = range(5)

            def pe_(pe):
                pe.drain().then_inc(a_t, depth)
                pe.drain().then_inc(a_pv, 2)
                with pe.Fori(0, 4) as it:
                    def scores(b):
                        n = NB * it + b
                        pe.wait_ge(a_e, n + 1)
                        score(pe, it, b // NT, b % NT, S2[b % depth]).then_inc(a_s, 1)

                    def values(e):
                        pe.wait_ge(a_te, NB * it + NT * e + NT + tdepth)
                        if e % per_out == 0:
                            pe.wait_ge(a_oe, 2 * it + e // per_out + 1)
                        value(pe, it, e).then_inc(a_pv, 1)

                    pe.wait_ge(a_ld, it + 1)
                    for b in range(depth):
                        scores(b)
                    for b in range(NB):
                        e, qb = b // NT, b % NT
                        if depth == 2 and b + depth < NB:
                            scores(b + depth)
                        pe.wait_ge(a_te, NB * it + b + 1)
                        pe.wait_ge(a_p, NB * it + b + 1)
                        nk = keys(qb)[1]
                        for t in range(nk):
                            ins = nc.tensor.transpose(TB[b % tdepth][:, t * P:(t + 1) * P],
                                                      Pb[:, b % depth, t * P:(t + 1) * P], ident)
                        ins.then_inc(a_t, 1)
                        if depth > 2 and b + depth < NB:
                            scores(b + depth)
                        if qb == lag - 1 and e > 0:
                            values(e - 1)
                    values(E - 1)

            def act_(act):
                act.drain().then_inc(a_e, depth)
                act.drain().then_inc(a_oe, 2)
                act.drain().then_inc(a_te, tdepth)
                with act.Fori(0, 4) as it:
                    def transposed(b):
                        e, qb = b // NT, b % NT
                        if qb == 0:
                            act.wait_ge(a_pv, E * it + e + 1)
                        act.wait_ge(a_t, NB * it + b + 1 + depth)
                        nk = keys(qb)[1]
                        nc.scalar.activation(PT[:, e % 2, 0:nk, qb * P:(qb + 1) * P],
                                             TB[b % tdepth][:, 0:nk * P].rearrange("p (a b) -> p a b", b=P),
                                             ACT.Copy).then_inc(a_te, 1)

                    def output(e):
                        act.wait_ge(a_pv, E * it + e + 3)
                        apart(act)
                        nc.scalar.activation(store(it, e), PS[:, 6 + e // per_out, :], ACT.Copy)\
                            .then_inc(a_oe, 1)

                    act.wait_ge(a_pv, E * it + 2)
                    apart(act)
                    for dst, src in loads(it):
                        ins = nc.scalar.activation(dst, src, ACT.Copy)
                    ins.then_inc(a_ld, 1)
                    if sink is not None:
                        act.drain()
                    for b in range(NB):
                        n = NB * it + b
                        w = keys(b % NT)[1] * P
                        act.wait_ge(a_t, n + 1)
                        act.wait_ge(a_m, n + 1)
                        if sink is not None:
                            nc.scalar.activation(col(SINK, b), sink(b // NT), ACT.Exp, bias=col(NEGMAX, b))
                        nc.scalar.activation(Pb[:, b % depth, 0:w], S2[b % depth][:, 0:w], ACT.Exp,
                                             bias=col(NEGMAX, b), scale=scale,
                                             accum_out=col(SUM, b)).then_inc(a_e, 1)
                        if b >= lag:
                            transposed(b - lag)
                        done = b - lag - 1
                        if done >= 0 and done % NT == NT - 1 and (done // NT + 1) % per_out == 0:
                            output(done // NT)
                    for b in range(NB - lag, NB):
                        transposed(b)
                    output(E - 1)

            def dve_(v):
                with v.Fori(0, 4) as it:
                    def maximum(b):
                        n = NB * it + b
                        w = keys(b % NT)[1] * P
                        S = S2[b % depth]
                        v.drain()
                        v.wait_ge(a_s, n + 1)
                        if bias is not None:
                            bias(it, b // NT, b % NT, S)
                            v.drain()
                        nc.vector.tensor_reduce(col(MAX, b), S[:, 0:w], AX.X, ALU.max)
                        v.drain()
                        if sink is None:
                            nc.vector.tensor_scalar(col(NEGMAX, b), col(MAX, b), -scale, None, ALU.mult)\
                                .then_inc(a_m, 1)
                        else:
                            nc.vector.tensor_scalar(col(NEGMAX, b), col(MAX, b), -scale, nsink(it, b // NT),
                                                    ALU.mult, ALU.min).then_inc(a_m, 1)

                    def normalise(b):
                        w = keys(b % NT)[1] * P
                        v.wait_ge(a_e, NB * it + b + 1 + depth)
                        if sink is not None:
                            nc.vector.tensor_tensor(col(SUM, b), col(SUM, b), col(SINK, b), ALU.add)
                            v.drain()
                        nc.vector.reciprocal(col(RECIP, b), col(SUM, b))
                        v.drain()
                        nc.vector.tensor_scalar(Pb[:, b % depth, 0:w], Pb[:, b % depth, 0:w], col(RECIP, b),
                                                None, ALU.mult).then_inc(a_p, 1)

                    for b in range(ahead):
                        maximum(b)
                    for b in range(NB):
                        normalise(b)
                        if b + ahead < NB:
                            maximum(b + ahead)

            return pe_, act_, dve_, a_oe

        def tile_of(a, i):
            return a[:, bass.ds(i, 1), :].rearrange("p a b -> p (a b)")

        qs4 = [qs[:, 0, :], rstd[:, :]]

        def gqa_score(pe, it, e, qb, S):
            q = qs4[e // 2][:, qb * P:(qb + 1) * P]
            kp = KP[:, bass.ds(it, 1), e % 2, :].rearrange("p a b -> p (a b)")
            nc.tensor.matmul(S[:, 0:512], q, kp[:, 0:512], start=True, stop=True)
            return nc.tensor.matmul(S[:, 512:TA], q, kp[:, 512:TA], start=True, stop=True)

        def gqa_value(pe, it, e):
            o = PS[64 * (e % 2):64 * (e % 2) + 64, 6 + e // 2, :]
            for t in range(NA):
                ins = nc.tensor.matmul(o, vs[:, t, :], PT[:, e % 2, t, :], start=t == 0, stop=t == NA - 1)
            return ins

        gqa_pe, gqa_act, gqa_dve, gqa_oe = attention(
            "gqa", 4, lambda qb: (0, NA),
            lambda it: [(qs4[0], tile_of(qT, 2 * it)), (qs4[1], tile_of(qT, 2 * it + 1)),
                        (vs, VKV[:, :, bass.ds(64 * it, 64)])],
            gqa_score, gqa_value, lambda it, e: tile_of(qT, 2 * it + e // 2), 0.125, Pb, PT)

        gt = area(15360, 4, T)
        y = area(17408, KT, T)
        ytmp = area(21504, T)
        y_ok = sem("y_ok")
        OC = qT

        def merge_pe(pe):
            pe.wait_ge(gqa_oe, 2 + 8)
            with pe.Fori(0, 2) as n:
                for b, o in enumerate((OA, OB, OC)):
                    for w, rhs in enumerate((hT, o)):
                        g, u = 24 * n + 8 * b + 4 * w, 4 * b + 2 * w
                        gemm(pe, G_MERGE + g, G_MERGE, U_MERGE + u, 3 * n, (0, 128, 256, 384), rhs)
                        pend[0] += 2
                flush(pe)

        def merge_act(act):
            with act.Fori(0, 2) as n:
                for b in range(3):
                    for t in range(4):
                        act.wait_ge(pt_used, 12 * n + 4 * b + (t - 1 if b else max(t - 1, 1)))
                        evac(act, G_MERGE + 24 * n + 8 * b + t, t, gt[:, t, :], func=ACT.Sigmoid)
                    for t in range(4):
                        act.wait_ge(pt_used, 12 * n + 4 * b + t + 1)
                        evac(act, G_MERGE + 24 * n + 8 * b + 4 + t, t, pt[:, t % 2, :])

        def merge_dve(v):
            v.drain().then_inc(pt_used, 2)
            with v.Fori(0, 2) as n:
                for b in range(3):
                    for t in range(4):
                        v.drain()
                        v.wait_ge(evac_done, G_MERGE + 24 * n + 8 * b + 4 + t + 1)
                        dst = tile_of(y, 4 * n + t)
                        if b == 0:
                            nc.vector.tensor_tensor(dst, pt[:, t % 2, :], gt[:, t, :], ALU.mult)\
                                .then_inc(pt_used, 1)
                        else:
                            nc.vector.tensor_tensor(ytmp, pt[:, t % 2, :], gt[:, t, :], ALU.mult)\
                                .then_inc(pt_used, 1)
                            v.drain()
                            nc.vector.tensor_tensor(dst, dst, ytmp, ALU.add)
                v.drain().then_inc(y_ok, 1)

        def residual_pe(pe, g, su, rhs):
            for c in range(2):
                gemm(pe, g + 4 * c, g, su + 2 * c, 0, (0, 128, 256, 384), rhs)
                pend[0] += 2
            flush(pe)

        def residual_act(act, g, r, bias=None):
            for j in range(KT):
                act.wait_ge(pt_used, r + j + 1)
                if bias is None:
                    evac(act, g + j, g + j, pt[:, (r + j) % 2, :])
                else:
                    evac(act, g + j, g + j, pt[:, (r + j) % 2, :], func=ACT.Identity,
                         bias=V[:, bias + j:bias + j + 1])

        def residual_dve(v, g, r, gate):
            for j in range(KT):
                v.wait_ge(evac_done, g + j + 1)
                nc.vector.scalar_tensor_tensor(xT[:, j, :], pt[:, (r + j) % 2, :], gate(j), xT[:, j, :],
                                               ALU.mult, ALU.add).then_inc(pt_used, 1)
            v.drain().then_inc(x_ok, 1)

        h2 = area(0, NT, D)
        Pm = area(4096, NT, NE * CAP)
        PTm = area(8192, NPAIR, T)
        acc = area(12288, KT, T)
        xs = area(16384, KT, P)
        hid = area(17408, FF)
        hidT = area(18432, FF // P, P)
        ys = area(19456, D)
        sg = area(20480, 2, 512)
        iota_s = area(21504, T)
        aff = area(22016, NT, NE)
        affT = area(22080, 2, T)
        vals = area(23104, CAP)
        idxf = area(23232, CAP)
        blk = area(23296, NE, CAP)
        idxc = area(24320, NPAIR)
        wsel = area(24328, NPAIR)
        rw = area(24336, KT, NE)
        mx4 = area(24464, NT)
        sm4 = area(24468, NT)
        rs4 = area(24472, NT)
        idxu = sb("idxu", [NE, CAP], u32)
        in_router, r_lg, r_mx, r_ex, r_aff, r_affT, r_top, r_tt, r_blk, r_row, r_ok = (sem(n) for n in
            ("in_router", "r_lg", "r_mx", "r_ex", "r_aff", "r_affT", "r_top", "r_tt", "r_blk", "r_row", "r_ok"))
        e_g, e_xs, e_gu, e_sg, e_hid, e_T, e_hT, e_dn, e_ys, e_cb, e_acc = (sem(n) for n in
            ("e_g", "e_xs", "e_gu", "e_sg", "e_hid", "e_T", "e_hT", "e_dn", "e_ys", "e_cb", "e_acc"))

        def route_pe(pe):
            pe.wait_ge(in_router, 16)
            for m in range(NT):
                for k in range(KT):
                    if m == 0:
                        pe.wait_ge(n_mod, NM[2] + k + 1)
                    ins = nc.tensor.matmul(PS[:, 6, m * NE:(m + 1) * NE], hT[:, k, m * P:(m + 1) * P],
                                           rw[:, k, :], start=k == 0, stop=k == KT - 1)
            ins.then_inc(r_lg, 1)
            for i in range(8):
                g = G_H2T + i
                bank_wait(pe, g)
                for k in range(4):
                    kk = 4 * (i % 2) + k
                    ins = nc.tensor.transpose(PS[:, g % 2, k * P:(k + 1) * P],
                                              hT[:, kk, (i // 2) * P:(i // 2 + 1) * P], ident)
                ins.then_inc(mm_done, 1)
            pe.wait_ge(r_aff, 1)
            for m in range(NT):
                ins = nc.tensor.transpose(PS[0:NE, 7, m * P:(m + 1) * P], aff[:, m, :], ident)
            ins.then_inc(r_affT, 1)
            pe.wait_ge(r_top, 1)
            nc.tensor.transpose(PS[0:CAP, 6, 0:NE], vals[0:NE, :], C[0:NE, C_ID:C_ID + NE])
            nc.tensor.transpose(PS[0:CAP, 6, NE:2 * NE], idxf[0:NE, :], C[0:NE, C_ID:C_ID + NE]).then_inc(r_tt, 1)
            pe.wait_ge(r_blk, 1)
            for c in range(2):
                ins = nc.tensor.matmul(PS[:, 4 + c, :], C[0:NE, C_ONE:C_ONE + P],
                                       blk[0:NE, 8 * c:8 * c + 8, :].rearrange("p a b -> p (a b)"),
                                       start=True, stop=True)
            ins.then_inc(r_row, 1)

        def route_act(act):
            act.wait_ge(r_mx, 1)
            for m in range(NT):
                ins = nc.scalar.activation(aff[:, m, :], PS[:, 6, m * NE:(m + 1) * NE], ACT.Exp,
                                           bias=mx4[:, m:m + 1], accum_out=sm4[:, m:m + 1])
            ins.then_inc(r_ex, 1)
            for i in range(8):
                g = G_H2T + i
                evac(act, g, g, h2[:, i // 2, (i % 2) * 512:(i % 2 + 1) * 512])

        def route_dve(v):
            v.wait_ge(r_lg, 1)
            nc.vector.tensor_reduce(mx4, PS[:, 6, 0:NT * NE].rearrange("p (m e) -> p m e", e=NE),
                                    AX.X, ALU.max, negate=True).then_inc(r_mx, 1)
            nc.vector.memset(acc[:, :, :], 0.0)
            v.wait_ge(r_ex, 1)
            nc.vector.reciprocal(rs4, sm4)
            v.drain()
            for m in range(NT):
                ins = nc.vector.tensor_scalar(aff[:, m, :], aff[:, m, :], rs4[:, m:m + 1], None, ALU.mult)
            ins.then_inc(r_aff, 1)
            v.wait_ge(r_affT, 1)
            nc.vector.tensor_copy(affT[0:NE, 0, :], PS[0:NE, 7, :])
            for r in range(CAP // 8):
                cur, nxt, top = affT[0:NE, r % 2, :], affT[0:NE, 1 - r % 2, :], vals[0:NE, 8 * r:8 * r + 8]
                v.drain()
                nc.vector.max(top, cur)
                v.drain()
                nc.vector.max_index(idxu[:, 8 * r:8 * r + 8], top, cur)
                if r < CAP // 8 - 1:
                    nc.vector.match_replace(nxt, top, cur, -1.0)
            v.drain()
            nc.vector.tensor_copy(idxf[0:NE, :], idxu[:, :])
            v.drain().then_inc(r_top, 1)
            nc.vector.tensor_tensor(blk[0:NE, :, :], idxf[0:NE, :].unsqueeze(1).broadcast_to([NE, NE, CAP]),
                                    C[0:NE, C_ID:C_ID + NE].unsqueeze(2).broadcast_to([NE, NE, CAP]),
                                    ALU.mult).then_inc(r_blk, 1)
            v.wait_ge(r_tt, 1)
            for e in range(2):
                dst = slice(CAP * e, CAP * e + CAP)
                nc.vector.tensor_copy(wsel[dst, :], PS[0:CAP, 6, e:NE:2])
                nc.vector.tensor_copy(idxc[dst, :], PS[0:CAP, 6, NE + e:2 * NE:2])
            v.drain()
            v.wait_ge(in_iota, 16)
            for p in range(NPAIR):
                nc.vector.tensor_scalar(PTm[:, p, :], iota_s, idxc[:, p:p + 1], None, ALU.is_equal)
            v.wait_ge(r_row, 1)
            for m in range(NT):
                nc.vector.tensor_scalar(Pm[:, m, :], PS[:, 4:6, :].rearrange("p a b -> p (a b)"),
                                        C[:, C_PART + m:C_PART + m + 1], None, ALU.is_equal)
            v.drain().then_inc(r_ok, 1)
            v.drain().then_inc(e_acc, 2)

        def pair_product(pe, p, j, x_, bank, done):
            for kg in range(2):
                for e in range(2):
                    unit_wait(pe, U_EXP + 4 * j + 2 * kg + e, 3 * p)
                for kk in range(4):
                    k = 4 * kg + kk
                    for e in range(2):
                        w = ring[slot(U_EXP + 4 * j + 2 * kg + e)][:, kk * 512:(kk + 1) * 512]
                        mm(PS[64 * e:64 * e + 64, bank, :], x_[:, k, 64 * e:64 * e + 64], w,
                           k == 0, k == KT - 1, done if k == KT - 1 and e == 1 else None)
                pend[0] += 2

        def gather_pe(pe, p):
            for k in range(KT):
                for m in range(NT):
                    mm(PS[:, 4 + k // 4, (k % 4) * P:(k % 4 + 1) * P], h2[:, m, k * P:(k + 1) * P],
                       Pm[:, m, bass.ds(P * p, P)], m == 0, m == NT - 1,
                       e_g if k == KT - 1 and m == NT - 1 else None)

        def combine_pe(pe, p, half):
            pe.wait_ge(e_ys, 2 * p + half + 2)
            for k in range(4 * half, 4 * half + 4):
                pe.wait_ge(e_acc, 8 * p + k + 1)
                mm(PS[:, 6 + k % 2, :], ys[:, k * P:(k + 1) * P], tile_of(PTm, p), True, True, e_cb)

        def pair_pe(pe, p, before, after):
            pe.wait_ge(e_xs, p + 1)
            pe.wait_ge(e_ys, 2 * p + 1)
            for c in range(2):
                pair_product(pe, p, 2 * c, xs, 2 * c, e_gu)
                pair_product(pe, p, 2 * c + 1, xs, 2 * c + 1, e_gu)
                if before:
                    combine_pe(pe, p - 1, c)
            for j in range(KT):
                if j % 4 == 0:
                    pe.wait_ge(e_hid, 2 * p + j // 4 + 1)
                ins = nc.tensor.transpose(PS[:, 4 + j // 4, (j % 4) * P:(j % 4 + 1) * P],
                                          hid[:, j * P:(j + 1) * P], ident)
            ins.then_inc(e_T, 1)
            pe.wait_ge(e_hT, p + 2)
            pair_product(pe, p, 4, hidT, 0, e_dn)
            if after:
                gather_pe(pe, p + 1)
            pair_product(pe, p, 5, hidT, 1, e_dn)
            flush(pe)

        def experts_pe(pe):
            pe.wait_ge(r_ok, 1)
            pe.wait_ge(evac_done, G_H2T + 8)
            first(pe, e_cb)
            gather_pe(pe, 0)
            pair_pe(pe, 0, False, True)
            with pe.Fori(1, NPAIR - 1) as p:
                pair_pe(pe, p, True, True)
            pair_pe(pe, NPAIR - 1, True, False)
            combine_pe(pe, NPAIR - 1, 0)
            combine_pe(pe, NPAIR - 1, 1)

        def pair_act(act, p, after):
            two = PS[:, 4:6, :].rearrange("p a b -> p (a b)")
            for c in range(2):
                act.wait_ge(e_gu, 4 * p + 2 * c + 1)
                nc.scalar.activation(sg[:, c, :], PS[:, 2 * c, :], ACT.Silu).then_inc(e_sg, 1)
            act.wait_ge(e_T, p + 1)
            nc.scalar.activation(hidT.rearrange("p a b -> p (a b)"), two, ACT.Copy).then_inc(e_hT, 1)
            for c in range(2):
                act.wait_ge(e_cb, 8 * p + 1)
                act.wait_ge(e_dn, 2 * p + c + 1)
                apart(act)
                nc.scalar.activation(ys[:, c * 512:(c + 1) * 512], PS[:, c, :], ACT.Copy,
                                     scale=wsel[:, bass.ds(p, 1)]).then_inc(e_ys, 1)
                if c == 0 and after:
                    act.wait_ge(e_g, p + 2)
                    nc.scalar.activation(xs.rearrange("p a b -> p (a b)"), two, ACT.Copy).then_inc(e_xs, 1)

        def experts_act(act):
            first(act, e_hT)
            first(act, e_ys)
            act.wait_ge(e_g, 1)
            nc.scalar.activation(xs.rearrange("p a b -> p (a b)"),
                                 PS[:, 4:6, :].rearrange("p a b -> p (a b)"), ACT.Copy).then_inc(e_xs, 1)
            pair_act(act, 0, True)
            with act.Fori(1, NPAIR - 1) as p:
                pair_act(act, p, True)
            pair_act(act, NPAIR - 1, False)

        def combine_dve(v, p, half):
            for k in range(4 * half, 4 * half + 4):
                v.wait_ge(e_cb, 8 * p + k + 2)
                nc.vector.tensor_tensor(acc[:, k, :], acc[:, k, :], PS[:, 6 + k % 2, :], ALU.add)\
                    .then_inc(e_acc, 1)

        def pair_dve(v, p, before):
            v.drain()
            for c in range(2):
                v.wait_ge(e_gu, 4 * p + 2 * c + 2)
                v.wait_ge(e_sg, 2 * p + c + 1)
                nc.vector.tensor_tensor(hid[:, c * 512:(c + 1) * 512], sg[:, c, :], PS[:, 2 * c + 1, :],
                                        ALU.mult).then_inc(e_hid, 1)
                if before:
                    combine_dve(v, p - 1, c)

        def experts_dve(v):
            pair_dve(v, 0, False)
            with v.Fori(1, NPAIR) as p:
                pair_dve(v, p, True)
            v.drain()
            combine_dve(v, NPAIR - 1, 0)
            combine_dve(v, NPAIR - 1, 1)
            v.drain()
            for k in range(KT):
                ins = nc.vector.scalar_tensor_tensor(xT[:, k, :], acc[:, k, :], mod[:, 40 + k:41 + k],
                                                     xT[:, k, :], ALU.mult, ALU.add)
            ins.then_inc(x_ok, 1)

        cq = area(0, QT, T)
        ckv = area(1536, KVT, T)
        kr = area(2560, T)
        down = area(0, 6, T)
        krp = area(3072, 2, T)
        qn = area(4096, KT, T)
        qr = area(8192, 4, T)
        up = area(4096, 12, T)
        kn = area(10240, KT, T)
        vt = area(14336, NT, D)
        sqb = area(18432, QT, T)
        cs2 = area(19968, 2, T)
        ang = area(20992, 2, T)
        Pb2 = area(22016, 4, T)
        PT2 = area(24064, 2, NT, T)
        qs2 = area(29696, 3, T)
        vs2 = area(31232, 2, NT, P)
        rt2 = area(22016, T)
        posi = area(21504, T).bitcast(i32)
        in_pos, t_ang, t_cs, r2_rot, r2_done, krp_ok = (sem(n) for n in
            ("in_pos", "t_ang", "t_cs", "r2_rot", "r2_done", "krp_ok"))

        def angles_dve(v):
            two_pi = 2 * np.pi
            c1 = 6.28125
            c2 = float(np.round((two_pi - c1) * 2.0 ** 21) / 2.0 ** 21)
            c3 = float(np.float32(two_pi - c1 - c2))
            magic = 1.5 * 2.0 ** 23
            a, w = ang[:, 0, :], ang[:, 1, :]
            v.wait_ge(in_pos, 16)
            v.wait_ge(x_ok, 2)
            nc.vector.tensor_copy(a, posi)
            v.drain()
            nc.vector.tensor_scalar(a, a, C[:, C_INV:C_INV + 1], None, ALU.mult)
            for i, (shift, turn) in enumerate(((np.pi / 2, 0.25), (0.0, 0.0))):
                t = cs2[:, i, :]
                v.drain()
                nc.vector.tensor_scalar(w, a, 1.0 / two_pi, turn, ALU.mult, ALU.add)
                v.drain()
                nc.vector.tensor_scalar(w, w, magic, None, ALU.add)
                v.drain()
                nc.vector.tensor_scalar(w, w, magic, None, ALU.subtract)
                v.drain()
                nc.vector.scalar_tensor_tensor(t, w, -c1, a, ALU.mult, ALU.add)
                v.drain()
                nc.vector.scalar_tensor_tensor(t, w, -c2, t, ALU.mult, ALU.add)
                v.drain()
                nc.vector.scalar_tensor_tensor(t, w, -c3, t, ALU.mult, ALU.add)
                v.drain()
                nc.vector.tensor_scalar(t, t, float(shift), 3.1415925, ALU.add, ALU.min)
                v.drain()
                nc.vector.tensor_scalar(t, t, -3.1415925, None, ALU.max)
            v.drain().then_inc(t_ang, 1)

        def angles_act(act):
            act.wait_ge(t_ang, 1)
            nc.scalar.activation(cs2[:, :, :], cs2[:, :, :], ACT.Sin).then_inc(t_cs, 1)

        def mla_pe(pe):
            gemm(pe, G_MD, G_MD, U_MD, 0, (0, 128, 256, 384), hT, ready=NM[4])
            pend[0] += 2
            gemm(pe, G_MD + 4, G_MD + 4, U_MD + 2, 0, (0, 128), hT)
            pend[0] += 2
            flush(pe)
            norm_pe(pe, 5, sqb, kt=QT)
            norm_pe(pe, 6, sqb, kt=KVT)
            pe.wait_ge(n_h, NH[6])
            for c in range(3):
                gemm(pe, G_MUQ + 4 * c, G_MUQ, U_MUQ + c, 0, (0, 128, 256, 384), cq, kt=QT)
                pend[0] += 1
            pe.wait_ge(n_h, NH[7])
            gemm(pe, G_MUKV, G_MUKV, U_MUKV, 0, range(0, D, P), ckv, kt=KVT, cols=1024)
            pend[0] += 1
            unit_wait(pe, U_MUKV + 1)
            for m in range(NT):
                for c in range(2):
                    g = G_MUKV + 8 + 2 * m + c
                    gemm_tok(pe, g, g, U_MUKV + 1, ckv, (m * P,), c * 512, 512, kt=KVT, cols=1024)
            pend[0] += 1
            flush(pe)
            for n in range(5):
                x = qr[:, n, :] if n < 4 else kr
                if n >= 2:
                    pe.wait_ge(r2_done, n - 1)
                nc.tensor.matmul(PS[:, 4 + n % 2, :], C[:, C_ROT2:C_ROT2 + P], x, start=True, stop=True)\
                    .then_inc(r2_rot, 1)

        def mla_act(act):
            for j in range(6):
                evac(act, G_MD + j, G_MD + j, down[:, j, :])
            angles_act(act)
            nc.scalar.preload_act_table_set("natural_log_exp_and_others")
            norm_act(act, 5, cq, sqb, kt=QT)
            act.wait_ge(n_h, NH[6])
            norm_act(act, 6, ckv, sqb, kt=KVT)
            for j in range(12):
                evac(act, G_MUQ + j, G_MUQ + j, up[:, j, :])
            for j in range(8):
                evac(act, G_MUKV + j, G_MUKV + j, kn[:, j, :])
            for j in range(8):
                evac(act, G_MUKV + 8 + j, G_MUKV + 8 + j, vt[:, j // 2, (j % 2) * 512:(j % 2 + 1) * 512])

        def mla_dve(v):
            norm_dve(v, 5, cq, cq, lambda k: V[:, V_GQ + k:V_GQ + k + 1], kt=QT)
            norm_dve(v, 6, ckv, ckv, lambda k: V[:, V_GKV + k:V_GKV + k + 1], kt=KVT)
            nc.vector.memset(krp[:, :, :], 0.0)
            v.wait_ge(t_cs, 1)
            for n in range(5):
                x = qr[:, n, :] if n < 4 else kr
                v.drain()
                v.wait_ge(r2_rot, n + 1)
                rotate_dve(v, x, PS[:, 4 + n % 2, :], rt2, cs2[:, 0, :], cs2[:, 1, :], r2_done)
            v.drain()
            for e in range(2):
                half = slice(64 * e, 64 * e + 64)
                nc.vector.tensor_copy(krp[half, e, :], kr[half, :])
            v.drain().then_inc(krp_ok, 1)

        def mla_score(pe, it, e, qb, S):
            w = (qb + 1) * P
            q = slice(qb * P, (qb + 1) * P)
            nc.tensor.matmul(S[:, 0:w], qs2[:, e, q], tile_of(kn, 2 * it + e)[:, 0:w], start=True, stop=False)
            return nc.tensor.matmul(S[:, 0:w], qs2[:, 2, q], krp[:, e, 0:w], start=False, stop=True)

        def mla_bias(it, e, qb, S):
            d = S[:, qb * P:(qb + 1) * P]
            nc.vector.tensor_tensor(d, d, C[:, C_CAUS:C_CAUS + P], ALU.add)

        def mla_value(pe, it, e):
            for t in range(NT):
                ins = nc.tensor.matmul(PS[:, 6 + e, t * P:T], vs2[:, e, t, :], PT2[:, e, t, t * P:T],
                                       start=t == 0, stop=t == NT - 1)
            return ins

        mla_att_pe, mla_att_act, mla_att_dve, mla_oe = attention(
            "mla", 2, lambda qb: (0, qb + 1),
            lambda it: [(qs2[:, 0, :], tile_of(qn, 2 * it)), (qs2[:, 1, :], tile_of(qn, 2 * it + 1)),
                        (qs2[:, 2, :], tile_of(qr, it)),
                        (vs2[:, 0, :, :], vt[:, :, bass.ds(256 * it, P)]),
                        (vs2[:, 1, :, :], vt[:, :, bass.ds(256 * it + P, P)])],
            mla_score, mla_value, lambda it, e: tile_of(qn, 2 * it + e), float((NOPE + ROPE_D) ** -0.5),
            Pb2, PT2, bias=mla_bias, depth=4)

        fh = area(0, FT, T)
        f_h, f_mm, f_x = (sem(n) for n in ("f_h", "f_mm", "f_x"))

        def ff_pe(pe, L, use):
            g0 = (G_FF0, G_FF1)[L]
            with pe.Fori(0, 4) as i:
                for c in range(2):
                    gemm(pe, g0 + 8 * i + 4 * c, g0, U_FF[L] + 2 * c, i, (0, 128, 256, 384), hT,
                         ready=NM[use] if c == 0 else None)
                    pend[0] += 2
                flush(pe)
            pe.wait_ge(f_h, FT * (L + 1))
            with pe.Fori(0, 2) as n:
                pe.wait_ge(f_x, 8 * L + 4 * n + 1)
                for kc in range(4):
                    for j in range(4):
                        for k in range(KT):
                            su = U_FF[L] + 16 + 2 * kc + k // 4
                            if j == 0 and k % 4 == 0:
                                unit_wait(pe, su, 2 * n)
                            c0 = (k % 4) * 512 + j * P
                            last = kc == 3 and k == KT - 1
                            mm(PS[:, 4 + j, :], ring[slot(su)][:, c0:c0 + P], fh[:, 8 * kc + k, :],
                               kc == 0 and k == 0, last, f_mm if last else None, skip_group_check=True)
                    pend[0] += 2
                flush(pe)

        def ff_act(act, L):
            g0 = (G_FF0, G_FF1)[L]
            with act.Fori(0, 4) as i:
                for j in range(8):
                    act.wait_ge(mm_done, g0 + 8 * i + j + 1)
                    apart(act)
                    nc.scalar.activation(tile_of(fh, 8 * i + j), PS[:, (g0 + j) % 2, :], ACT.Relu)\
                        .then_inc(evac_done, 1)

        def ff_dve(v, L):
            if L == 0:
                first(v, f_x)
            g0 = (G_FF0, G_FF1)[L]
            with v.Fori(0, 4) as i:
                for j in range(8):
                    t = tile_of(fh, 8 * i + j)
                    v.wait_ge(evac_done, g0 + 8 * i + j + 1)
                    nc.vector.tensor_tensor(t, t, t, ALU.mult).then_inc(f_h, 1)
            with v.Fori(0, 2) as n:
                for j in range(4):
                    v.wait_ge(f_mm, 8 * L + 4 * n + j + 1)
                    gate = mod2[:, bass.ds(48 * L + 40 + j + 4 * n, 1)]
                    t = tile_of(xT, 4 * n + j)
                    nc.vector.scalar_tensor_tensor(t, PS[:, 4 + j, :], gate, t, ALU.mult, ALU.add)\
                        .then_inc(f_x, 1)
            v.drain().then_inc(x_ok, 1)

        KP2 = area(10240, 4, 2, T)
        VK2 = area(14336, NT, 256)
        bvs = area(15360, 256)
        snk = area(15616, 2, 16)
        kl2 = area(22016, 2, T)
        in_swa, v_ok = sem("in_swa"), sem("v_ok")

        def swa_qkv_pe(pe):
            for j in range(12):
                g, su = G_SQKV + j, U_SQKV + 2 * min(j // 4, 2)
                if j < 10:
                    gemm(pe, g, g, su, 0, ((j % 4) * P,), hT, ready=NM[8] if j == 0 else None)
                else:
                    t0 = (j - 10) * 2 * P
                    gemm_tok(pe, g, g, su, hT, (t0, t0 + P), 256, 256)
                if j in (3, 7, 11):
                    pend[0] += 2
            flush(pe)

        def swa_qkv_act(act):
            for j in range(12):
                g = G_SQKV + j
                if j < 10:
                    dst = qn[:, j, :] if j < 8 else kl2[:, j - 8, :]
                    evac(act, g, g, dst, func=ACT.Identity, bias=V[:, V_BQKV + j:V_BQKV + j + 1])
                else:
                    evac(act, g, g, VK2[:, 2 * (j - 10):2 * (j - 10) + 2, :], w=256)

        def swa_qkv_dve(v):
            nc.vector.memset(KP2[:, :, :, :], 0.0)
            v.drain()
            v.wait_ge(evac_done, G_SQKV + 10)
            for g in range(4):
                r0 = (g % 2) * 64
                for e in range(2):
                    nc.vector.tensor_copy(KP2[64 * e:64 * e + 64, g, e, :], kl2[r0:r0 + 64, g // 2, :])
            v.wait_ge(in_swa, 32)
            nc.vector.tensor_scalar(snk[:, 1, :], snk[:, 0, :], -1.0, None, ALU.mult)
            v.wait_ge(evac_done, G_SQKV + 12)
            nc.vector.tensor_tensor(VK2[:, :, :], VK2[:, :, :], bvs.unsqueeze(1).broadcast_to([P, NT, 256]),
                                    ALU.add)
            v.drain().then_inc(v_ok, 1)

        def swa_keys(qb):
            return (max(qb - 1, 0), min(qb + 1, 2))

        qs3, vs3 = area(29696, 2, T), area(31232, NT, 64)
        sink4 = area(31488, 4)

        def swa_score(pe, it, e, qb, S):
            k0, nk = swa_keys(qb)
            kp = KP2[:, bass.ds(it, 1), e % 2, :].rearrange("p a b -> p (a b)")
            return nc.tensor.matmul(S[:, 0:nk * P], qs3[:, e // 2, qb * P:(qb + 1) * P],
                                    kp[:, k0 * P:(k0 + nk) * P], start=True, stop=True)

        def swa_bias(it, e, qb, S):
            nk = swa_keys(qb)[1]
            s = S[:, 0:nk * P]
            nc.vector.scalar_tensor_tensor(s, C[:, C_DIST + (2 - nk) * P:C_DIST + 2 * P],
                                           C[:, bass.ds(C_SLOPE + 4 * it + e, 1)], s, ALU.mult, ALU.add)

        def swa_value(pe, it, e):
            for qb in range(NT):
                k0, nk = swa_keys(qb)
                o = PS[64 * (e % 2):64 * (e % 2) + 64, 6 + e // 2, qb * P:(qb + 1) * P]
                for t in range(nk):
                    ins = nc.tensor.matmul(o, vs3[:, k0 + t, :], PT2[:, e % 2, t, qb * P:(qb + 1) * P],
                                           start=t == 0, stop=t == nk - 1)
            return ins

        def nsink(it, e):
            return snk[:, 1, bass.ds(4 * it + e, 1)]

        swa_att_pe, swa_att_act, swa_att_dve, swa_oe = attention(
            "swa", 4, swa_keys,
            lambda it: [(qs3[:, 0, :], tile_of(qn, 2 * it)), (qs3[:, 1, :], tile_of(qn, 2 * it + 1)),
                        (vs3, VK2[:, :, bass.ds(64 * it, 64)]), (sink4, snk[:, 0, bass.ds(4 * it, 4)])],
            swa_score, swa_value, lambda it, e: tile_of(qn, 2 * it + e // 2), 0.125, Pb2, PT2,
            bias=swa_bias, sink=lambda e: sink4[:, e:e + 1], depth=4)

        xf = area(0, KT, T)
        otok = area(4096, NT, D)
        out_done = sem("out_done")

        def end_pe(pe):
            norm_pe(pe, 10, hT)
            pe.wait_ge(n_h, NH[11])
            for i in range(8):
                g = G_FIN + i
                bank_wait(pe, g)
                for k in range(4):
                    kk = 4 * (i % 2) + k
                    ins = nc.tensor.transpose(PS[:, g % 2, k * P:(k + 1) * P],
                                              xf[:, kk, (i // 2) * P:(i // 2 + 1) * P], ident)
                ins.then_inc(mm_done, 1)

        def end_act(act):
            norm_act(act, 10, xT, hT, ready=(x_ok, 6))
            for i in range(8):
                g = G_FIN + i
                evac(act, g, g, otok[:, i // 2, (i % 2) * 512:(i % 2 + 1) * 512])

        def end_dve(v):
            norm_dve(v, 10, xT, xf, lambda k: V[:, V_GF + k:V_GF + k + 1])
        block = ctx.enter_context(nc.Block())
        @block.sync
        def _(sp):
            def load(u, used, base=0):
                if used is not None:
                    sp.wait_ge(w_used, base + used)
                src = stream[bass.ds(base + u, 1), :, :].rearrange("a p n -> (a p) n")
                sp.dma_start(ring[slot(u)][:, :], src).then_inc(w_loaded[slot(u)], 16)

            def turns(first_, last, width):
                n = (last - first_) // width
                with sp.Fori(0, n) as turn:
                    for s in range(width):
                        load(first_ + s, first_ + s - width + 1, width * turn)
                for u in range(first_ + n * width, last):
                    load(u, u - width + 1)

            for u in range(SLOTS):
                load(u, None)
            turns(SLOTS, U_EXP, SLOTS)
            for j in range(WIDE):
                load(U_EXP + j, U_EXP + min(j, SLOTS - 1) - SLOTS + 1)
            turns(U_EXP + WIDE, U_MD, WIDE)
            for u in range(U_MD, U_MD + SLOTS):
                load(u, u - WIDE + 1)
            turns(U_MD + SLOTS, N_STREAM, SLOTS)
            for m in range(NT):
                sp.wait_ge(evac_done, G_FIN + 2 * m + 2)
                sp.dma_start(out[m * P:(m + 1) * P, :], otok[:, m, :]).then_inc(out_done, 16)
            sp.wait_ge(out_done, 16 * NT)

        @block.gpsimd
        def _(pool):
            pool.dma_start(C[:, :], cst).then_inc(in_const, 16)
            pool.dma_start(v_rows, vecs).then_inc(in_vec, 16)
            pool.wait_ge(evac_done, G_X + 2 * KT)
            pool.dma_start(H_CST, hcst).then_inc(in_cst2, 16)
            pool.wait_ge(h_out, HG + 1)
            pool.dma_start(A_CST, acst.rearrange("p (a b) -> p a b", a=2)).then_inc(in_acst, 16)
            pool.wait_ge(y_ok, 2)
            pool.dma_start(iota_s, iota).then_inc(in_iota, 16)
            pool.dma_start(rw, router).then_inc(in_router, 16)
            pool.wait_ge(x_ok, 2)
            pool.dma_start(posi, pos).then_inc(in_pos, 16)
            pool.wait_ge(x_ok, 4)
            pool.dma_start(bvs, bv).then_inc(in_swa, 16)
            pool.dma_start(snk[:, 0, :], sinks).then_inc(in_swa, 16)

        @block.tensor
        def _(pe):
            start_pe(pe)
            hgrn_pe(pe)
            qkv_pe(pe)
            pe.wait_ge(kp_ok, 1)
            gqa_pe(pe)
            merge_pe(pe)
            pe.wait_ge(y_ok, 2)
            residual_pe(pe, G_OUT, U_OUT, y)
            norm_pe(pe, 2, hT)
            route_pe(pe)
            experts_pe(pe)
            norm_pe(pe, 3, hT)
            norm_pe(pe, 4, hT)
            mla_pe(pe)
            pe.wait_ge(krp_ok, 1)
            mla_att_pe(pe)
            pe.wait_ge(mla_oe, 2 + 8)
            residual_pe(pe, G_MWO, U_MWO, qn)
            norm_pe(pe, 7, hT)
            ff_pe(pe, 0, 7)
            norm_pe(pe, 8, hT)
            swa_qkv_pe(pe)
            pe.wait_ge(v_ok, 1)
            swa_att_pe(pe)
            pe.wait_ge(swa_oe, 2 + 8)
            residual_pe(pe, G_SWO, U_SWO, qn)
            norm_pe(pe, 9, hT)
            ff_pe(pe, 1, 9)
            end_pe(pe)

        @block.scalar
        def _(act):
            tables = lambda: nc.scalar.preload_act_table_set("natural_log_exp_and_others")
            act.dma_start(x_tok, x.rearrange("(m p) d -> p m d", p=P)).then_inc(in_x, 16)
            act.dma_start(c_tok, ctxt.rearrange("(m p) d -> p m d", p=P)).then_inc(in_x, 16)
            start_act(act)
            hgrn_act(act)
            qkv_act(act)
            gqa_act(act)
            merge_act(act)
            residual_act(act, G_OUT, 24)
            tables()
            norm_act(act, 2, xT, hT, ready=(x_ok, 1))
            norm_shift(act, 2, hT, 2, mod[:, 24:32])
            route_act(act)
            experts_act(act)
            tables()
            norm_act(act, 3, xT, hT, ready=(x_ok, 2))
            norm_act(act, 4, xT, hT, ready=(n_h, NH[4]))
            norm_shift(act, 4, hT, 3, mod2[:, 0:8])
            mla_act(act)
            mla_att_act(act)
            residual_act(act, G_MWO, 32)
            norm_act(act, 7, xT, hT, ready=(x_ok, 3))
            norm_shift(act, 7, hT, 5, mod2[:, 24:32])
            ff_act(act, 0)
            norm_act(act, 8, xT, hT, ready=(x_ok, 4))
            norm_shift(act, 8, hT, 4, mod2[:, 48:56])
            swa_qkv_act(act)
            act.wait_ge(v_ok, 1)
            swa_att_act(act)
            residual_act(act, G_SWO, 40, bias=V_BO)
            norm_act(act, 9, xT, hT, ready=(x_ok, 5))
            norm_shift(act, 9, hT, 6, mod2[:, 72:80])
            ff_act(act, 1)
            end_act(act)

        @block.vector
        def _(v):
            start_dve(v)
            hgrn_dve(v)
            qkv_dve(v)
            gqa_dve(v)
            merge_dve(v)
            residual_dve(v, G_OUT, 24, lambda j: mod[:, 16 + j:17 + j])
            norm_dve(v, 2, xT, hT)
            route_dve(v)
            experts_dve(v)
            norm_dve(v, 3, xT, xT, lambda k: V[:, V_FN + k:V_FN + k + 1])
            norm_dve(v, 4, xT, hT)
            angles_dve(v)
            mla_dve(v)
            mla_att_dve(v)
            residual_dve(v, G_MWO, 32, lambda j: mod2[:, 16 + j:17 + j])
            norm_dve(v, 7, xT, hT)
            ff_dve(v, 0)
            norm_dve(v, 8, xT, hT)
            swa_qkv_dve(v)
            swa_att_dve(v)
            residual_dve(v, G_SWO, 40, lambda j: mod2[:, 64 + j:65 + j])
            norm_dve(v, 9, xT, hT)
            ff_dve(v, 1)
            end_dve(v)


def _units(w, cols, row0=0, kt=KT, width=512):
    w = w[row0:row0 + kt * P][:, cols]
    w = np.concatenate([w, np.zeros((w.shape[0], width - w.shape[1]), w.dtype)], 1) if w.shape[1] < width else w
    per = UNIT // width
    short = -kt % per
    t = w.reshape(kt, P, width)
    t = np.concatenate([t, np.zeros((short, P, width), w.dtype)]) if short else t
    return t.reshape(-1, per, P, width).transpose(0, 2, 1, 3).reshape(-1, P, UNIT)


def _chunks(w, row0=0, kt=KT, width=512):
    return [_units(w, slice(c, c + width), row0, kt, width) for c in range(0, w.shape[1], width)]


def _stream(a):
    cat = np.concatenate
    r = lambda c0, n: np.arange(c0, c0 + n)
    w_in = a["w_in"][0]
    q0 = 8 * D
    parts = _chunks(a["ada_w"][0])
    ada2 = _chunks(a["w_ada_2"][0]) + _chunks(a["w_ada_2"][1])
    for h in range(HG):
        tile = lambda s: r(s * D + h * P, P)
        parts.append(_units(w_in, cat([tile(0), tile(4), tile(5), tile(6)])))
        parts.append(_units(w_in, cat([tile(7), tile(1), tile(2), tile(3)])))
        if 0 < h < HG - 1:
            parts += ada2[4 * (h - 1):4 * h]
    parts += _chunks(w_in[:, q0:q0 + D + 512])
    g0 = q0 + D + 512
    for n in range(2):
        for b, w in enumerate((a["w_proj_a"][0], a["w_proj_b"][0], a["w_proj_c"][0])):
            parts.append(_units(w_in, r(g0 + b * D + n * 512, 512)))
            parts.append(_units(w, r(n * 512, 512)))
    parts += _chunks(a["w_out"][0])
    wg, wu, wd = a["w_gate"][0], a["w_up"][0], a["w_down"][0]
    for p in range(NPAIR):
        def pair(w, n):
            e = [_units(w[2 * p + i], r(n * 512, 512)) for i in range(2)]
            return np.stack(e, 1).reshape(-1, P, UNIT)
        for n in range(2):
            parts += [pair(wg, n), pair(wu, n)]
        for n in range(2):
            parts.append(pair(wd, n))
    dkv = a["mla_w_dkv_2"][0]
    kr = dkv[:, KVL:]
    parts += _chunks(cat([a["mla_w_dq_2"][0], dkv[:, :KVL], kr, kr, np.zeros((D, 256), kr.dtype)], 1))
    uq = a["mla_w_uq_2"][0].reshape(QL, MLA_H, NOPE + ROPE_D)
    parts += _chunks(cat([uq[:, :, :NOPE].reshape(QL, -1), uq[:, :, NOPE:].reshape(QL, -1)], 1), kt=QT)
    ukv = a["mla_w_ukv_2"][0].reshape(KVL, MLA_H, 2 * NOPE)
    parts += _chunks(cat([ukv[:, :, :NOPE].reshape(KVL, -1), ukv[:, :, NOPE:].reshape(KVL, -1)], 1),
                     kt=KVT, width=1024)
    parts += _chunks(a["mla_w_o_2"][0])
    for layer in range(2):
        if layer:
            parts += _chunks(a["swa_w_qkv_2"][0]) + _chunks(a["swa_w_o_2"][0])
        parts += _chunks(a["w_ff1_2"][layer])
        for n in range(2):
            parts += [_units(a["w_ff2_2"][layer], r(n * 512, 512), row0=k * D) for k in range(4)]
    s = cat(parts)
    assert s.shape[0] == N_UNITS, s.shape
    return cat([s, np.zeros((N_STREAM - N_UNITS, P, UNIT), s.dtype)])


def _vecs(a):
    f = lambda v: np.asarray(v).reshape(-1, P)
    two = lambda v: np.concatenate([v.reshape(1, 64)] * 2, 1)
    rows = [f(a["c"]), f(a["c_ctx"]), f(a["c_2"]), f(a["ada_b"]), f(a["norm1_g"]), f(a["norm2_g"]),
            f(a["final_norm_g"]), f(a["hg_norm_g"]), f(a["conv_w"]),
            f(a["b_ada_2"]), f(a["g_mix_2"]), f(a["g_mlp_2"]),
            f(a["g_final_2"]), f(a["mla_g_q_2"]), f(a["mla_g_kv_2"]), f(a["swa_b_qkv_2"]),
            f(a["swa_b_o_2"]), two(a["q_norm_g"]), two(a["k_norm_g"])]
    rows = np.concatenate(rows)
    rows = np.concatenate([rows, np.zeros((N_VEC - len(rows), P), rows.dtype)])
    return np.ascontiguousarray(rows.reshape(3, P, P).transpose(1, 0, 2))


def _constants():
    c = np.zeros((P, N_CST), np.float32)
    p = np.arange(P)
    c[:, C_ID:C_ID + P] = np.eye(P)
    c[:, C_ONE:C_ONE + P] = 1
    c[:, C_BLK:C_BLK + P] = p[:, None] // 64 == p[None] // 64
    for m in range(P):
        c[m + 1 if m % 2 == 0 else m - 1, C_ROT1 + m] = -1 if m % 2 == 0 else 1
        c[m + 32 if m % 64 < 32 else m - 32, C_ROT2 + m] = -1 if m % 64 < 32 else 1
    c[:, C_CAUS:C_CAUS + P] = np.where(p[None] <= p[:, None], 0, NEG)
    dist = P + p[:, None] - np.arange(2 * P)[None]
    c[:, C_DIST:C_DIST + 2 * P] = np.where((dist >= 0) & (dist < P), dist, -NEG)
    c[:, C_SLOPE:C_SLOPE + 16] = -8.0 * 2.0 ** (-8.0 * np.arange(1, 17) / 16)
    c[:, C_PART:C_PART + 4] = p[:, None] + P * np.arange(4)
    for j in range(3):
        c[j::32, C_SEL + j] = 1
    c[:, C_INV] = (np.float32(10000.0) ** (-(p % 32).astype(np.float32) / 32)).astype(np.float32)
    h = np.zeros((P, N_HCST), np.float32)
    s, t = p[:, None], p[None]
    for lv, L in enumerate(LEVELS):
        same = s // (2 * L) == t // (2 * L)
        h[:, lv * P:(lv + 1) * P] = same & (s % (2 * L) < L) & (t % (2 * L) >= L)
        h[:, (NL + 1 + lv) * P:(NL + 2 + lv) * P] = same & (s % (2 * L) >= L) & (t % (2 * L) < L)
    for d in range(2):
        h[:, (d * (NL + 1) + NL) * P:(d * (NL + 1) + NL + 1) * P] = np.eye(P)
    h[:, H_SCAN:] = np.arange(TA) % P != 0
    inv = (np.float32(10000.0) ** (-np.arange(0, 32, 2, dtype=np.float32) / 32)).astype(np.float32)
    tok = np.arange(T)
    row, col = (tok // GRID_W).astype(np.float32), (tok % GRID_W).astype(np.float32)
    ang = np.concatenate([row[:, None] * inv, col[:, None] * inv], 1)
    f = (p % 64) // 2
    acst = np.concatenate([np.cos(ang)[:, f].T, np.sin(ang)[:, f].T], 1).astype(np.float32)
    iota = np.broadcast_to(np.arange(T, dtype=np.float32), (P, T))
    return c, h, np.ascontiguousarray(acst), np.ascontiguousarray(iota)


def host_arrays(a):
    c, h, ac, io = _constants()
    return {
        "stream": _stream(a), "vecs": _vecs(a), "cst": c, "hcst": h, "acst": ac, "iota": io,
        "x": np.ascontiguousarray(a["x"][0]), "ctxt": np.ascontiguousarray(a["ctx"][0]),
        "router": np.ascontiguousarray(a["router_w"][0].reshape(KT, P, NE).transpose(1, 0, 2)),
        "pos": np.ascontiguousarray(np.broadcast_to(a["positions_2"].reshape(1, T), (P, T))),
        "sinks": np.ascontiguousarray(np.broadcast_to(a["swa_sinks_2"].reshape(1, 16), (P, 16))),
        "bv": np.ascontiguousarray(np.broadcast_to(a["swa_b_qkv_2"].reshape(-1)[1280:], (P, 256))),
    }


def kernel(**inputs):
    import concourse.bacc as bacc
    from concourse.bass_utils import run_bass_kernel_spmd

    a = {k: np.asarray(v) for k, v in inputs.items()}
    arrays = host_arrays(a)
    nc = bacc.Bacc("TRN2", target_bir_lowering=False, num_devices=1)
    aps = {n: nc.dram_tensor(n, v.shape, mybir.dt.from_np(v.dtype), kind="ExternalInput").ap()
           for n, v in arrays.items()}
    out = nc.dram_tensor("out", (T, D), mybir.dt.float32, kind="ExternalOutput").ap()
    build(nc, out=out, **aps)
    r = run_bass_kernel_spmd(nc, [arrays], core_ids=[0])
    return r.results[0]["out"].reshape(1, T, D)
```
